# Optimizing a Trainium2 kernel written in Bass

```python
import jax
import jax.numpy as jnp
from jax import lax
import numpy as np

D_MODEL = 1024
BATCH = 1
SEQ = 512
DEPTH = 1

CHUNK = 64
Q_BLOCK = 128
EPS = 1e-6
H_M = 4
W_M = D_MODEL // 2
DH_M = W_M // H_M
CONV_K = 4
H_F = 8
W_F = D_MODEL // 2
DH_F = W_F // H_F
D_FF = (8 * D_MODEL + 3 * 256 - 1) // (3 * 256) * 256
IN_SIZES = (W_M, W_M, W_M, W_M, H_M, H_M, W_F, W_F, W_F, H_F, D_MODEL, D_MODEL)
N_IN = sum(IN_SIZES)
MF_OFF = 4 * W_M + H_M
FF_OFF = 4 * W_M + 2 * H_M + 3 * W_F

kernel_name = "hybrid_mlstm_fox_block"

def rmsnorm(x, g):
    xf = x.astype(jnp.float32)
    y = xf * lax.rsqrt(jnp.mean(xf * xf, axis=-1, keepdims=True) + EPS)
    return (y * g.astype(jnp.float32)).astype(x.dtype)

def split_heads(t, n_heads):
    b, s, _ = t.shape
    return t.reshape(b, s, n_heads, -1).transpose(0, 2, 1, 3)

def merge_heads(t):
    b, h, s, d = t.shape
    return t.transpose(0, 2, 1, 3).reshape(b, s, h * d)

def causal_depthwise_conv(u, w, b):
    y = lax.conv_general_dilated(
        u, w[:, None, :].astype(u.dtype), window_strides=(1,),
        padding=[(CONV_K - 1, 0)], dimension_numbers=("NWC", "WIO", "NWC"),
        feature_group_count=u.shape[-1])
    return y + b.astype(u.dtype)

def mlstm_chunkwise(q, k, v, log_i, log_f):
    bsz, nh, s, d = q.shape
    nc = s // CHUNK

    def to_chunks(t):
        t = t.reshape(bsz, nh, nc, CHUNK, *t.shape[3:])
        return jnp.moveaxis(t, 2, 0)

    causal = jnp.tril(jnp.ones((CHUNK, CHUNK), dtype=bool))

    def step(carry, inp):
        c_mat, n_vec, m_prev = carry
        qc, kc, vc, ic, fc = inp
        b = jnp.cumsum(fc, axis=-1)
        log_d = jnp.where(causal, b[..., :, None] - b[..., None, :] + ic[..., None, :], -jnp.inf)
        m_inter = b + m_prev[..., None]
        m_t = jnp.maximum(m_inter, jnp.max(log_d, axis=-1))
        a = jnp.exp(m_inter - m_t)
        s_qk = jnp.einsum("bhtd,bhsd->bhts", qc, kc) * jnp.exp(log_d - m_t[..., None])
        num = a[..., None] * jnp.einsum("bhtk,bhkv->bhtv", qc, c_mat) + jnp.einsum("bhts,bhsv->bhtv", s_qk, vc)
        den = a * jnp.einsum("bhtk,bhk->bht", qc, n_vec) + jnp.sum(s_qk, axis=-1)
        h = num / jnp.maximum(jnp.abs(den), jnp.exp(-m_t))[..., None]
        b_last = b[..., -1]
        log_w = b_last[..., None] - b + ic
        m_new = jnp.maximum(b_last + m_prev, jnp.max(log_w, axis=-1))
        decay = jnp.exp(b_last + m_prev - m_new)
        w = jnp.exp(log_w - m_new[..., None])
        c_new = decay[..., None, None] * c_mat + jnp.einsum("bhs,bhsk,bhsv->bhkv", w, kc, vc)
        n_new = decay[..., None] * n_vec + jnp.einsum("bhs,bhsk->bhk", w, kc)
        return (c_new, n_new, m_new), h

    init = (jnp.zeros((bsz, nh, d, d), jnp.float32),
            jnp.zeros((bsz, nh, d), jnp.float32),
            jnp.zeros((bsz, nh), jnp.float32))
    _, hs = lax.scan(step, init, (to_chunks(q), to_chunks(k), to_chunks(v),
                                  to_chunks(log_i), to_chunks(log_f)))
    return jnp.moveaxis(hs, 0, 2).reshape(bsz, nh, s, d)

def forgetting_attention(q, k, v, log_f):
    s = q.shape[2]
    scale = q.shape[-1] ** -0.5
    cum = jnp.cumsum(log_f, axis=-1)
    outs = []
    for blk in range(s // Q_BLOCK):
        lo = blk * Q_BLOCK
        hi = lo + Q_BLOCK
        logits = (jnp.einsum("bhtd,bhsd->bhts", q[:, :, lo:hi], k[:, :, :hi]) * scale
                  + (cum[:, :, lo:hi, None] - cum[:, :, None, :hi]))
        mask = (lo + jnp.arange(Q_BLOCK))[:, None] >= jnp.arange(hi)[None, :]
        p = jax.nn.softmax(jnp.where(mask, logits, -jnp.inf), axis=-1)
        outs.append(jnp.einsum("bhts,bhsd->bhtd", p, v[:, :, :hi]))
    return jnp.concatenate(outs, axis=2)

def swiglu(h, w_gate, w_up, w_down):
    return (jax.nn.silu(h @ w_gate) * (h @ w_up)) @ w_down

def setup_inputs(seed: int = 0) -> dict:
    key = jax.random.key(seed)
    ks = jax.random.split(key, 16)

    def dense(k, shape, fan_in):
        return jax.random.normal(k, shape, jnp.float32) * fan_in ** -0.5

    def gain(k, shape):
        return 1.0 + 0.02 * jax.random.normal(k, shape, jnp.float32)

    x = jax.random.normal(ks[0], (BATCH, SEQ, D_MODEL), jnp.float32)
    norm1_g = gain(ks[1], (DEPTH, D_MODEL))
    w_in = dense(ks[2], (DEPTH, D_MODEL, N_IN), D_MODEL)
    b_in = 0.02 * jax.random.normal(ks[3], (DEPTH, N_IN), jnp.float32)
    b_in = b_in.at[:, MF_OFF:MF_OFF + H_M].add(jnp.linspace(3.0, 6.0, H_M))
    b_in = b_in.at[:, FF_OFF:FF_OFF + H_F].add(jnp.linspace(2.0, 6.0, H_F))
    conv_w = dense(ks[4], (DEPTH, CONV_K, 2 * W_M), CONV_K)
    conv_b = 0.02 * jax.random.normal(ks[5], (DEPTH, 2 * W_M), jnp.float32)
    mlstm_norm_g = gain(ks[6], (DEPTH, W_M))
    w_br_mlstm = dense(ks[7], (DEPTH, W_M, D_MODEL), W_M)
    w_br_fox = dense(ks[8], (DEPTH, W_F, D_MODEL), W_F)
    w_out = dense(ks[9], (DEPTH, D_MODEL, D_MODEL), D_MODEL)
    norm2_g = gain(ks[10], (DEPTH, D_MODEL))
    w_gate = dense(ks[11], (DEPTH, D_MODEL, D_FF), D_MODEL)
    w_up = dense(ks[12], (DEPTH, D_MODEL, D_FF), D_MODEL)
    w_down = dense(ks[13], (DEPTH, D_FF, D_MODEL), D_FF)
    norm_f_g = gain(ks[14], (D_MODEL,))
    return {"x": x, "norm1_g": norm1_g, "w_in": w_in, "b_in": b_in,
            "conv_w": conv_w, "conv_b": conv_b, "mlstm_norm_g": mlstm_norm_g,
            "w_br_mlstm": w_br_mlstm, "w_br_fox": w_br_fox, "w_out": w_out,
            "norm2_g": norm2_g, "w_gate": w_gate, "w_up": w_up, "w_down": w_down,
            "norm_f_g": norm_f_g}

def reference(x, norm1_g, w_in, b_in, conv_w, conv_b, mlstm_norm_g, w_br_mlstm,
              w_br_fox, w_out, norm2_g, w_gate, w_up, w_down, norm_f_g):
    f32 = jnp.float32
    split_points = np.cumsum(IN_SIZES)[:-1].tolist()
    for l in range(DEPTH):
        h = rmsnorm(x, norm1_g[l])
        z = h @ w_in[l] + b_in[l]
        mq, mk, mv, mo, mi, mf, fq, fk, fv, ff, gm, gf = jnp.split(z, split_points, axis=-1)

        qk = jax.nn.silu(causal_depthwise_conv(jnp.concatenate([mq, mk], axis=-1), conv_w[l], conv_b[l]))
        mq, mk = qk[..., :W_M], qk[..., W_M:]
        hm = mlstm_chunkwise(
            split_heads(mq, H_M).astype(f32),
            split_heads(mk, H_M).astype(f32) * DH_M ** -0.5,
            split_heads(mv, H_M).astype(f32),
            mi.astype(f32).transpose(0, 2, 1),
            jax.nn.log_sigmoid(mf.astype(f32)).transpose(0, 2, 1))
        hm = hm * lax.rsqrt(jnp.mean(hm * hm, axis=-1, keepdims=True) + EPS)
        y_m = (merge_heads(hm) * mlstm_norm_g[l].astype(f32)
               * jax.nn.sigmoid(mo.astype(f32))).astype(x.dtype)

        hf = forgetting_attention(
            split_heads(fq, H_F).astype(f32),
            split_heads(fk, H_F).astype(f32),
            split_heads(fv, H_F).astype(f32),
            jax.nn.log_sigmoid(ff.astype(f32)).transpose(0, 2, 1))
        y_f = merge_heads(hf).astype(x.dtype)

        mix = jax.nn.sigmoid(gm) * (y_m @ w_br_mlstm[l]) + jax.nn.sigmoid(gf) * (y_f @ w_br_fox[l])
        x = x + mix @ w_out[l]

        x = x + swiglu(rmsnorm(x, norm2_g[l]), w_gate[l], w_up[l], w_down[l])
    return rmsnorm(x, norm_f_g)


_drawn_inputs = setup_inputs


def setup_inputs(seed=0):
    import zlib

    import numpy as np

    out = dict(_drawn_inputs(seed))
    spreads = {}
    factors = {'norm1_g': 4.34,
     'conv_b': 52.859,
     'mlstm_norm_g': 8.0,
     'norm2_g': 4.102,
     'norm_f_g': 8.235}
    for name, (base, spread) in spreads.items():
        noise = np.random.default_rng([zlib.crc32(name.encode()), seed]).standard_normal(out[name].shape)
        drawn = base * np.exp(spread * noise) if base else spread * noise
        out[name] = jnp.asarray(drawn.astype(out[name].dtype))
    for name, factor in factors.items():
        out[name] = (out[name] * factor).astype(out[name].dtype)
    return out
```

```python
import numpy as np
import concourse.bass as bass
from concourse import mybir
from contextlib import ExitStack

F32 = mybir.dt.float32
F32R = mybir.dt.float32r
BF16 = mybir.dt.bfloat16
ACT = mybir.ActivationFunctionType
ALU = mybir.AluOpType
AX = mybir.AxisListType

P = 128
D = 1024
SEQ = 512
ROWS = SEQ // P
KD = D // P
HALF = D // 2
H_M, H_F = 4, 8
W_M = W_F = D // 2
DH_M, DH_F = W_M // H_M, W_F // H_F
KB = W_M // P
CONV_K = 4
D_FF = 2816
F_BLOCKS = D_FF // P
EPS = 1e-6
LANES = H_M + H_F
NEG = -1.0e30

C_QK = 0
C_MV = 2 * W_M
C_MO = 3 * W_M
C_MI = 4 * W_M
C_FQK = C_MI + 2 * H_M
C_FV = C_FQK + 2 * W_F
C_FF = C_FV + W_F
C_GM = C_FF + H_F
C_GF = C_GM + D

V_QK, V_MO, V_FQK, V_GM, V_GF = 0, 8, 12, 20, 28
V_CONVW, V_CONVB, V_NORM, N_VEC = 36, 68, 76, 80

RING = 4
STAGES = 2
AHEAD = 2
GRAN = 1024


def block_kernel(nc, x, norm1_g, w_in, b_in, conv_w, conv_b, mlstm_norm_g, w_br_mlstm,
                 w_br_fox, w_out, norm2_g, w_gate, w_up, w_down, norm_f_g, out):
    w_in, b_in = w_in[0], b_in[0]
    conv_w, conv_b, mlstm_norm_g = conv_w[0], conv_b[0], mlstm_norm_g[0]
    w_bm, w_bf, w_o = w_br_mlstm[0], w_br_fox[0], w_out[0]
    w_g, w_u, w_d = w_gate[0], w_up[0], w_down[0]
    norm1_g, norm2_g = norm1_g[0], norm2_g[0]
    x_rows = x[0].rearrange("(r p) d -> r p d", p=P)
    out_rows = out[0].rearrange("(r p) d -> r p d", p=P)

    slots, granules = [], []

    def slot(views, loads):
        for view in views:
            granules.append((len(slots), view))
        slots.append((len(granules), loads))

    def whole(n):
        return lambda st: st.rearrange("p (k c) -> p k c", k=n)

    def column_slot(w, col):
        src = w[:, col:col + 2 * P].rearrange("(k p) c -> p k c", p=P)
        slot([lambda st, j=j: whole(KD)(st)[:, :, j * P:(j + 1) * P] for j in range(2)],
             [(whole(KD), src)])

    def row_slot(w, block, col):
        src = w[block * P:(block + 4) * P, col:col + HALF].rearrange("(k p) c -> p k c", p=P)
        slot([lambda st, j=j: whole(4)(st)[:, 2 * j:2 * j + 2, :] for j in range(2)],
             [(whole(4), src)])

    gate_view = lambda st: st[:, 0:GRAN].rearrange("p (k c) -> p k c", k=KD)
    slot([gate_view],
         [(lambda st: gate_view(st)[:, :, 0:2 * H_M],
           w_in[:, C_MI:C_MI + 2 * H_M].rearrange("(k p) c -> p k c", p=P)),
          (lambda st: gate_view(st)[:, :, 2 * H_M:P],
           w_in[:, C_FF:C_FF + P - 2 * H_M].rearrange("(k p) c -> p k c", p=P))])
    G_QK = len(granules)
    for i in range(4):
        column_slot(w_in, C_QK + 2 * P * i)
    G_MV = len(granules)
    for i in range(2):
        row_slot(w_in, 4 * i, C_MV)
    G_FV = len(granules)
    for i in range(2):
        row_slot(w_in, 4 * i, C_FV)
    G_FQK = len(granules)
    for i in range(4):
        column_slot(w_in, C_FQK + 2 * P * i)
    G_MO = len(granules)
    for i in range(2):
        column_slot(w_in, C_MO + 2 * P * i)
    G_BR = len(granules)
    for i in range(4):
        column_slot(w_in, C_GM + 2 * P * i)
        column_slot(w_in, C_GF + 2 * P * i)
        slot([lambda st, j=j: whole(KD)(st)[:, :, j * P:(j + 1) * P] for j in range(2)],
             [(lambda st, n=n: whole(KD)(st)[:, n * KB:(n + 1) * KB, :],
               w[:, 2 * P * i:2 * P * (i + 1)].rearrange("(k p) c -> p k c", p=P))
              for n, w in enumerate((w_bm, w_bf))])
    G_OUT = len(granules)
    S_OUT = len(slots)
    for half in range(2):
        for i in range(2):
            row_slot(w_o, 4 * i, half * HALF)
    G_FFN = len(granules)
    for i in range(F_BLOCKS // 2):
        column_slot(w_g, 2 * P * i)
        column_slot(w_u, 2 * P * i)
    G_DOWN = len(granules)
    D_GRAN = F_BLOCKS // 2
    down = [(half, 2 * d) for half in range(2) for d in range(D_GRAN)]
    for i in range(0, 2 * D_GRAN, 2):
        slot([lambda st, j=j: whole(4)(st)[:, 2 * j:2 * j + 2, :] for j in range(2)],
             [(lambda st, j=j: whole(4)(st)[:, 2 * j:2 * j + 2, :],
               w_d[f * P:(f + 2) * P, half * HALF:(half + 1) * HALF]
               .rearrange("(k p) c -> p k c", p=P))
              for j, (half, f) in enumerate(down[i:i + 2])])
    N_GRAN = len(granules)

    ctx = ExitStack()
    with ctx:
        base = (nc.sbuf_base + 31) // 32 * 32

        def at(name, shape, dtype, offset):
            return nc.alloc_sbuf_tensor_at(name, shape, dtype, offset=base + offset)

        K = 1024
        A = 0
        x_nat = at("x_nat", [P, ROWS, D], F32, A)
        v_m = at("v_m", [P, ROWS, H_M, DH_M + 1], F32, A)
        v_f = at("v_f", [P, ROWS, W_F], F32, A + 8256)
        x1 = at("x1", [P, ROWS, D], F32, A)
        B = A + 16896
        hT_hi = at("hT_hi", [P, KD, SEQ], F32R, B)
        hT_lo = at("hT_lo", [P, KD, SEQ], F32R, B + 16 * K)
        C = B + 32 * K
        stage = [at(f"stage{i}", [P, 2 * GRAN], F32, C + 8 * K * i) for i in range(STAGES)]
        C += 8 * K * STAGES
        w_hi = [at(f"w_hi{i}", [P, GRAN], F32R, C + 8 * K * i) for i in range(RING)]
        w_lo = [at(f"w_lo{i}", [P, GRAN], F32R, C + 8 * K * i + 4 * K) for i in range(RING)]
        G = C + 8 * K * RING
        gain_a = at("gain_a", [P, D], F32, G)
        gain_b = at("gain_b", [P, D], F32, G + 4 * K)
        v_bias = at("v_bias", [P, 2, W_M], F32, G + 4 * K)
        W = G + 8 * K
        work = [at(f"work{i}", [P, SEQ], F32, W + 2 * K * i) for i in range(6)]
        square_out = at("square_out", [P, SEQ], F32, W + 8 * K)
        R = W + 12 * K
        q_m = at("q_m", [P, H_M, SEQ], F32, R)
        k_m = at("k_m", [P, H_M, SEQ], F32, R + 8 * K)
        q_f = at("q_f", [P, KB, SEQ], F32, R + 16 * K)
        k_f = at("k_f", [P, KB, SEQ], F32, R + 24 * K)
        o_gate = at("o_gate", [P, KB, SEQ], F32, R + 32 * K)
        ymT_hi = at("ymT_hi", [P, KB, SEQ], F32R, R + 40 * K)
        ymT_lo = at("ymT_lo", [P, KB, SEQ], F32R, R + 48 * K)
        yfT_hi = at("yfT_hi", [P, KB, SEQ], F32R, R + 56 * K)
        yfT_lo = at("yfT_lo", [P, KB, SEQ], F32R, R + 64 * K)
        xn = [at(f"xn{i}", [P, D], F32, R + 56 * K + 4 * K * i) for i in range(2)]
        z_pad = at("z_pad", [P, CONV_K - 1 + SEQ], F32, R + 64 * K)
        N_E = sum(SEQ - P * j for j in range(ROWS))
        decay = [at(f"decay{i}", [P, N_E], F32, R + 56 * K + 5 * K * i) for i in range(2)]
        rows_hi = at("rows_hi", [LANES, 10 * P], F32R, R + 72 * K)
        rows_lo = at("rows_lo", [LANES, 10 * P], F32R, R + 77 * K)
        y_nat = [at(f"y_nat{i}", [P, ROWS, P], F32, R + 82 * K + 2 * K * i) for i in range(2)]
        stab_masked = [at(f"stab_masked{i}", [P, SEQ], F32, R + 82 * K + 2 * K * i) for i in range(2)]
        vec_raw = at("vec_raw", [N_VEC, P], F32, R + 82 * K)
        upper = at("upper", [P, P], F32, R + 86 * K)
        ones = at("ones", [P, P], F32, R + 86 * K + 512)
        mixT_hi = at("mixT_hi", [P, KD, SEQ], F32R, R)
        mixT_lo = at("mixT_lo", [P, KD, SEQ], F32R, R + 16 * K)
        mix_sum = [at(f"mix_sum{i}", [P, SEQ], F32, R + 72 * K + 2 * K * i) for i in range(2)]
        xn2 = [at(f"xn2{i}", [P, D], F32, R + 40 * K + 4 * K * i) for i in range(2)]
        aT_hi = at("aT_hi", [P, F_BLOCKS, SEQ], F32R, R)
        aT_lo = at("aT_lo", [P, F_BLOCKS, SEQ], F32R, R + 44 * K)
        S = R + 88 * K
        small_at = [S]

        def small(name, shape, dtype=F32):
            n = int(np.prod(shape[1:])) * (2 if dtype == BF16 else 4)
            t = at(name, shape, dtype, small_at[0])
            small_at[0] += (n + 31) // 32 * 32
            assert base + small_at[0] <= nc.sbuf_usable_end, small_at[0]
            return t

        ident = small("ident", [P, P])
        ident_b = small("ident_b", [P, P], BF16)
        mask_b = small("mask_b", [P, P], BF16)
        mask_T = small("mask_T", [P, P], BF16)
        ident_r = small("ident_r", [LANES, LANES], F32R)
        vec = small("vec", [P, N_VEC])
        vec_half = small("vec_half", [P, N_VEC])
        gate_bias = small("gate_bias", [LANES + H_M, 1])
        square_sum = small("square_sum", [P, ROWS, 2])
        mean_sq = small("mean_sq", [P, ROWS])
        rstd = small("rstd", [P, ROWS])
        minus_half = small("minus_half", [P, ROWS])
        frame = small("frame", [P, ROWS * ROWS, LANES])
        before = small("before", [P, ROWS, H_M])
        m_stab = small("m_stab", [P, ROWS, H_M])
        m_floor = small("m_floor", [P, ROWS, H_M])
        den = small("den", [P, ROWS])
        head_ms = small("head_ms", [P, ROWS])
        head_rs = small("head_rs", [P, ROWS])
        neg_max = small("neg_max", [P, 4])
        row_sum = small("row_sum", [P, 4])
        row_inv = small("row_inv", [P, 4])
        gate_rows = work[5]
        abs_neg = work[4][:, 0:ROWS * LANES].rearrange("p (j l) -> p j l", l=LANES)
        gates = work[4][:, 128:192].rearrange("p (j l) -> p j l", l=LANES + H_M)
        log_f = work[4][:, 192:192 + ROWS * LANES].rearrange("p (j l) -> p j l", l=LANES)
        cum = work[4][:, 256:256 + ROWS * LANES].rearrange("p (j l) -> p j l", l=LANES)
        softp = work[4][:, 64:64 + ROWS * LANES].rearrange("p (j l) -> p j l", l=LANES)
        psum = [ctx.enter_context(nc.psum_tensor(f"bank{i}", [P, 512], F32)) for i in range(8)]

        def sem(name):
            return ctx.enter_context(nc.semaphore(name))

        x_in = [sem(f"x_in{r}") for r in range(ROWS)]
        gain1_in, vec_in, gbias_in, vbias_in = (sem(n) for n in ("gain1_in", "vec_in", "gbias_in", "vbias_in"))
        gain2_in, gain3_in, xagain_in = sem("gain2_in"), sem("gain3_in"), sem("xagain_in")
        stage_in = [sem(f"stage_in{i}") for i in range(STAGES)]
        hi_split, lo_split, used = sem("hi_split"), sem("lo_split"), sem("granule_used")
        consts = sem("consts")
        vec_T, vec_ready = sem("vec_T"), sem("vec_ready")
        norm = [{n: sem(f"{n}_{i}") for n in ("squared", "summed", "rstd_ready", "xn_ready", "xn_T",
                                              "hT_hi_ready", "hT_lo_ready")} for i in range(3)]
        z_padded, conv_tap, conv_tanh, qk_ready = (sem(n) for n in ("z_padded", "conv_tap", "conv_tanh", "qk_ready"))
        v_ready, v_ones = sem("v_ready"), sem("v_ones")
        fq_ready, fk_ready, mo_tanh, o_ready = (sem(n) for n in ("fq_ready", "fk_ready", "mo_tanh", "o_ready"))
        gate_rows_ready, gates_T, gates_ready = sem("gate_rows_ready"), sem("gates_T"), sem("gates_ready")
        gate_abs, gate_exp, gate_ln, log_f_ready = (sem(n) for n in ("gate_abs", "gate_exp", "gate_ln", "log_f_ready"))
        cum_done, frame_step, frame_T = sem("cum_done"), sem("frame_step"), sem("frame_T")
        rows_hi_ready, rows_lo_ready = sem("rows_hi_ready"), sem("rows_lo_ready")
        g_spread, g_max, m_step, floor_ready = (sem(n) for n in ("g_spread", "g_max", "m_step", "floor_ready"))
        m_spread, s_m, decay_exp, m_masked, weighted = (sem(n) for n in ("m_spread", "s_m", "decay_exp", "m_masked", "weighted"))
        num_m, den_step, h_m, h_squared, h_mean, h_rstd, y_m = (sem(n) for n in ("num_m", "den_step", "h_m", "h_squared", "h_mean", "h_rstd", "y_m"))
        y_mT, y_m32, ymT_hi_ready, ymT_lo_ready = (sem(n) for n in ("y_mT", "y_m32", "ymT_hi_ready", "ymT_lo_ready"))
        logits, fox_max, fox_exp, fox_T, fox_PT, fox_pv = (sem(n) for n in ("logits", "fox_max", "fox_exp", "fox_T", "fox_PT", "fox_pv"))
        fox_inv, fox_y, y_fT, yfT_hi_ready, yfT_lo_ready = (sem(n) for n in ("fox_inv", "fox_y", "y_fT", "yfT_hi_ready", "yfT_lo_ready"))
        gate_tanh, mix_step, mix_hi_ready, mix_lo_ready = (sem(n) for n in ("gate_tanh", "mix_step", "mix_hi_ready", "mix_lo_ready"))
        row_out, x1_ready = sem("row_out"), sem("x1_ready")
        ffn_tanh, ffn_step, aT_hi_ready, aT_lo_ready = (sem(n) for n in ("ffn_tanh", "ffn_step", "aT_hi_ready", "aT_lo_ready"))
        row_down, x2_ready, stored = sem("row_down"), sem("x2_ready"), sem("stored")
        block = ctx.enter_context(nc.Block())

        def pair(i, j):
            return i * (i + 1) // 2 + j

        def decay_at(j):
            return sum(SEQ - P * n for n in range(j))

        def wait_stage(eng, g):
            s = granules[g][0]
            n = sum(len(slots[i][1]) for i in range(s % STAGES, s + 1, STAGES))
            eng.wait_ge(stage_in[s % STAGES], 16 * n)

        def staged(g):
            s, view = granules[g]
            return view(stage[s % STAGES][:, :])

        def ring(tiles, g):
            n = granules_shape(g)
            return tiles[g % RING][:, :].rearrange("p (k c) -> p k c", k=n)

        def granules_shape(g):
            rows = (G_MV <= g < G_FQK) or (G_OUT <= g < G_FFN) or g >= G_DOWN
            return 2 if rows else KD

        @block.sync
        def _(sp):
            for r in range(ROWS):
                sp.dma_start(x_nat[:, r, :], x_rows[r]).then_inc(x_in[r], 16)
            before_slot = 0
            for s, (n_gran, loads) in enumerate(slots):
                if s == 12:
                    sp.wait_ge(v_ready, 2 * ROWS)
                    sp.dma_start(gain_b[:, :], norm2_g.rearrange("(a n) -> a n", a=1).to_broadcast([P, D])).then_inc(gain2_in, 16)
                    sp.wait_ge(norm[0]["xn_ready"], ROWS)
                    sp.dma_start(gain_a[:, :], norm_f_g.rearrange("(a n) -> a n", a=1).to_broadcast([P, D])).then_inc(gain3_in, 16)
                if s == S_OUT - 4:
                    sp.wait_ge(fox_pv, 32)
                    sp.wait_ge(num_m, 2 * H_M)
                    sp.dma_start(x1[:, :, :], x[0].rearrange("(r p) d -> p r d", p=P)).then_inc(xagain_in, 16)
                if s >= STAGES:
                    sp.wait_ge(lo_split, slots[s - STAGES][0])
                for view, src in loads:
                    sp.dma_start(view(stage[s % STAGES][:, :]), src).then_inc(stage_in[s % STAGES], 16)
            for r in range(ROWS):
                sp.wait_ge(norm[2]["xn_ready"], r + 1)
                sp.dma_start(out_rows[r], x1[:, r, :]).then_inc(stored, 16)
            sp.wait_ge(stored, 16 * ROWS)

        @block.gpsimd
        def _(pool):
            steps = [0]

            def const(ins):
                ins.then_inc(consts, 1)
                steps[0] += 1

            const(pool.memset(ident[:, :], 0.0))
            const(pool.memset(ident_b[:, :], 0.0))
            const(pool.memset(mask_b[:, :], 0.0))
            const(pool.memset(mask_T[:, :], 0.0))
            const(pool.memset(ident_r[:, :].bitcast(F32), 0.0))
            const(pool.memset(upper[:, :], 1.0))
            const(pool.memset(ones[:, :], 1.0))
            const(pool.memset(minus_half[:, :], -0.5))
            const(pool.memset(z_pad[:, 0:CONV_K - 1], 0.0))
            pool.wait_ge(consts, steps[0])
            for t, n in ((ident, P), (ident_b, P), (ident_r, LANES)):
                const(pool.affine_select(out=t[:, :], in_=t[:, :].bitcast(F32) if t is ident_r else t[:, :],
                                         compare_op=ALU.not_equal, fill=1.0, base=0,
                                         pattern=[[-1, n]], channel_multiplier=1))
            const(pool.affine_select(out=mask_b[:, :], in_=mask_b[:, :], compare_op=ALU.is_ge, fill=NEG,
                                     base=0, pattern=[[-1, P]], channel_multiplier=1))
            const(pool.affine_select(out=mask_T[:, :], in_=mask_T[:, :], compare_op=ALU.is_ge, fill=-NEG,
                                     base=0, pattern=[[1, P]], channel_multiplier=-1))
            const(pool.affine_select(out=upper[:, :], in_=upper[:, :], compare_op=ALU.is_ge, fill=0.0,
                                     base=0, pattern=[[1, P]], channel_multiplier=-1))
            assert steps[0] == N_CONSTS

            def rows_rstd(i):
                for r in range(ROWS):
                    pool.wait_ge(norm[i]["summed"], (1 if False else 2) * (r + 1))
                    pool.tensor_tensor(rstd[:, r:r + 1], mean_sq[:, r:r + 1], minus_half[:, 0:1],
                                       ALU.pow).then_inc(norm[i]["rstd_ready"], 1)

            rows_rstd(0)
            pool.wait_ge(norm[0]["xn_ready"], ROWS)
            pool.memset(v_m[:, :, :, DH_M:DH_M + 1], 1.0).then_inc(v_ones, 1)
            for i in range(H_M + 2):
                if 1 <= i <= H_M:
                    h = i - 1
                    pool.wait_ge(h_m, 2 * h + 2)
                    if h >= 1:
                        pool.wait_ge(h_mean, 2 * h)
                    pool.tensor_tensor(work[2][:, :], work[h % 2][:, :], work[h % 2][:, :],
                                       ALU.mult).then_inc(h_squared, 1)
                if i >= 2:
                    h = i - 2
                    pool.wait_ge(h_mean, 2 * h + 2)
                    if h >= 1:
                        pool.wait_ge(y_m, h)
                    pool.tensor_tensor(head_rs[:, :], head_ms[:, :], minus_half[:, :],
                                       ALU.pow).then_inc(h_rstd, 1)
            rows_rstd(1)
            rows_rstd(2)

        @block.scalar
        def _(act):
            act.dma_start(gain_a[:, :], norm1_g.rearrange("(a n) -> a n", a=1).to_broadcast([P, D])).then_inc(gain1_in, 16)
            vec_loads = ((V_QK, b_in[C_QK:C_QK + 2 * W_M]), (V_MO, b_in[C_MO:C_MO + W_M]),
                         (V_FQK, b_in[C_FQK:C_FQK + 2 * W_F]), (V_GM, b_in[C_GM:C_GM + 2 * D]),
                         (V_CONVW, conv_w.rearrange("j c -> (j c)")), (V_CONVB, conv_b), (V_NORM, mlstm_norm_g))
            for row, src in vec_loads:
                n = src.shape[0] // P
                act.dma_start(vec_raw[row:row + n, :], src.rearrange("(a n) -> a n", n=P)).then_inc(vec_in, 16)
            act.dma_start(gate_bias[0:2 * H_M, :], b_in[C_MI:C_MI + 2 * H_M].rearrange("(n a) -> n a", a=1)).then_inc(gbias_in, 16)
            act.dma_start(gate_bias[2 * H_M:2 * H_M + H_F, :], b_in[C_FF:C_FF + H_F].rearrange("(n a) -> n a", a=1)).then_inc(gbias_in, 16)
            for n, c in enumerate((C_MV, C_FV)):
                act.dma_start(v_bias[:, n, :], b_in[c:c + W_M].rearrange("(a n) -> a n", a=1).to_broadcast([P, W_M])).then_inc(vbias_in, 16)

            def square(i, src, r, halves):
                for half in halves:
                    n = count_squares[i]
                    if n:
                        act.wait_ge(norm[i]["squared"], n)
                    act.activation(square_out[:, :], src[:, r, half * HALF:(half + 1) * HALF], ACT.Square,
                                   accum_out=square_sum[:, r, half:half + 1]).then_inc(norm[i]["squared"], 1)
                    count_squares[i] += 1

            count_squares = [0, 0, 0]

            def take_hT_hi(i, r):
                for half in range(2):
                    act.wait_ge(norm[i]["xn_T"], 2 * r + half + 1)
                    bank = norm_bank(i, r, half)
                    act.activation(hT_hi[:, 4 * half:4 * half + 4, r * P:(r + 1) * P],
                                   psum[bank][:, :].rearrange("p (k c) -> p k c", k=4),
                                   ACT.Copy).then_inc(norm[i]["hT_hi_ready"], 1)

            def split_hi(g):
                if g >= N_GRAN:
                    return
                wait_stage(act, g)
                if g >= RING:
                    act.wait_ge(used, g - RING + 1)
                act.activation(ring(w_hi, g), staged(g), ACT.Copy).then_inc(hi_split, 1)

            act.wait_ge(x_in[0], 16)
            square(0, x_nat, 0, (0, 1))
            for r in range(1, ROWS):
                act.wait_ge(x_in[r], 16)
                square(0, x_nat, r, (0, 1))
                take_hT_hi(0, r - 1)
            for g in range(AHEAD):
                split_hi(g)
            take_hT_hi(0, ROWS - 1)

            def conv_tanh_of(b):
                act.wait_ge(conv_tap, CONV_K * (b + 1))
                if b >= 2:
                    act.wait_ge(qk_ready, b - 1)
                act.activation(work[2 + b % 2][:, :], work[b % 2][:, :], ACT.Tanh, scale=0.5).then_inc(conv_tanh, 1)

            for g in range(G_BR):
                split_hi(g + AHEAD)
                if G_QK <= g < G_MV:
                    b = g - G_QK
                    if b >= 1:
                        conv_tanh_of(b - 1)
                    act.wait_ge(used, g + 1)
                    if b == 0:
                        act.wait_ge(vec_ready, 1)
                        act.wait_ge(consts, N_CONSTS)
                        act.wait_ge(norm[0]["xn_T"], 2 * ROWS)
                    else:
                        act.wait_ge(conv_tap, CONV_K * b)
                    act.activation(z_pad[:, CONV_K - 1:], psum[qk_bank(b)][:, :], ACT.Identity,
                                   bias=vec[:, V_QK + b:V_QK + b + 1]).then_inc(z_padded, 1)
                if g == G_MV:
                    conv_tanh_of(7)
                if g == G_QK + 1:
                    act.wait_ge(gate_abs, 1)
                    act.activation(softp, abs_neg, ACT.Exp).then_inc(gate_exp, 1)
                    act.wait_ge(gate_exp, 1)
                    act.activation(softp, softp, ACT.Ln, bias=1.0).then_inc(gate_ln, 1)
                if g == G_QK + 5:
                    for n, (a, b) in enumerate(ROW_CHUNKS):
                        act.wait_ge(frame_T, n + 1)
                        act.activation(rows_hi[:, a * P:b * P], psum[5 + n][0:LANES, 0:(b - a) * P],
                                       ACT.Copy).then_inc(rows_hi_ready, 1)
                if G_FQK + KB <= g < G_MO:
                    b = g - G_FQK - KB
                    act.wait_ge(used, g + 1)
                    act.activation(k_f[:, b, :], psum[fqk_bank(KB + b)][:, :], ACT.Identity,
                                   bias=vec[:, V_FQK + KB + b:V_FQK + KB + b + 1]).then_inc(fk_ready, 1)
                if g >= G_MO:
                    b = g - G_MO
                    act.wait_ge(used, g + 1)
                    act.wait_ge(qk_ready, 8)
                    if b >= 2:
                        act.wait_ge(o_ready, b - 1)
                    act.activation(work[2 + b % 2][:, :], psum[mo_bank(b)][:, :], ACT.Tanh, scale=0.5,
                                   bias=vec_half[:, V_MO + b:V_MO + b + 1]).then_inc(mo_tanh, 1)
                if g == G_MO + 2:
                    act.wait_ge(m_step, 2)
                    act.activation(m_floor[:, :, :], m_floor[:, :, :], ACT.Exp, scale=-1.0).then_inc(floor_ready, 1)

            def take_ymT_hi(h):
                act.wait_ge(y_m32, h + 1)
                act.activation(ymT_hi[:, h, :], work[4 + h % 2][:, :], ACT.Copy).then_inc(ymT_hi_ready, 1)

            for i in range(H_M + 3):
                if i < H_M:
                    h = i
                    act.wait_ge(m_spread, h + 1)
                    if h == 0:
                        act.wait_ge(conv_tap, 8 * CONV_K)
                    if h >= 2:
                        act.wait_ge(num_m, 2 * (h - 1))
                    act.wait_ge(m_masked, h + 1)
                    for j in range(ROWS):
                        for q in range(j, ROWS):
                            o = decay_at(j) + (q - j) * P
                            m = stab_masked[h % 2] if q == j else psum[2 + h % 2]
                            act.activation(decay[h % 2][:, o:o + P], m[:, q * P:(q + 1) * P],
                                           ACT.Exp, scale=-1.0,
                                           bias=frame[:, ROWS * q + j, h:h + 1]).then_inc(decay_exp, 1)
                if i >= 3:
                    take_ymT_hi(i - 3)

            def take_yfT_hi(hp):
                act.wait_ge(y_fT, hp + 1)
                act.activation(yfT_hi[:, hp, :], psum[7][:, :], ACT.Copy).then_inc(yfT_hi_ready, 1)

            act.wait_ge(num_m, 2 * H_M)
            act.wait_ge(y_m, H_M)
            act.wait_ge(ymT_hi_ready, H_M)
            act.wait_ge(ymT_lo_ready, H_M)
            for u in range(32):
                _, q, _ = fox_unit(u)
                n = (q + 1) * P
                act.wait_ge(fox_max, u + 1)
                if u >= 3:
                    act.wait_ge(fox_T, u - 2)
                if u >= 4:
                    act.wait_ge(fox_inv, u - 3)
                act.activation(work[u % 3][:, 0:n], psum[4 + u % 3][:, 0:n], ACT.Exp,
                               bias=neg_max[:, u % 4:u % 4 + 1],
                               accum_out=row_sum[:, u % 4:u % 4 + 1]).then_inc(fox_exp, 1)
                if u >= 8 and u % 8 == 5:
                    take_yfT_hi(u // 8 - 1)
            take_yfT_hi(KB - 1)

            for c in range(4):
                for n in range(6):
                    g = G_BR + 6 * c + n
                    split_hi(g + AHEAD)
                    act.wait_ge(used, g + 1)
                    if n < 4:
                        if c >= 1:
                            act.wait_ge(mix_step, 3 * 2 * c - (1 if n % 2 else 4))
                        else:
                            act.wait_ge(fox_PT, 32)
                            act.wait_ge(fox_pv, 32)
                        col = (V_GM, V_GF)[n // 2] + 2 * c + n % 2
                        act.activation(work[n][:, :], psum[GATE_BANKS[n]][:, :], ACT.Tanh, scale=0.5,
                                       bias=vec_half[:, col:col + 1]).then_inc(gate_tanh, 1)
                    else:
                        b = 2 * c + n - 4
                        act.wait_ge(mix_step, 3 * b + 3)
                        act.activation(mixT_hi[:, b, :], mix_sum[b % 2][:, :], ACT.Copy, scale=0.5).then_inc(mix_hi_ready, 1)

            for n in range(4):
                split_hi(G_OUT + n + AHEAD)
            split_hi(G_OUT + 6)
            split_hi(G_OUT + 7)
            for r in range(ROWS):
                act.wait_ge(x1_ready, ROWS + r + 1)
                square(1, x1, r, (0, 1))
                if r >= 1:
                    take_hT_hi(1, r - 1)
                if r == ROWS - 2:
                    for n in range(AHEAD):
                        split_hi(G_FFN + n)
            take_hT_hi(1, ROWS - 1)

            for p in range(F_BLOCKS // 2):
                for n in range(4):
                    g = G_FFN + 4 * p + n
                    split_hi(g + AHEAD)
                    act.wait_ge(used, g + 1)
                    if n < 2:
                        f = 2 * p + n
                        if p >= 1:
                            act.wait_ge(ffn_step, 2 * (f - 2) + 1)
                        else:
                            act.wait_ge(mix_lo_ready, 8)
                        act.activation(work[n][:, :], psum[4 * (p % 2) + n][:, :], ACT.Tanh, scale=0.5).then_inc(ffn_tanh, 1)
                    else:
                        f = 2 * p + n - 2
                        act.wait_ge(ffn_step, 2 * f + 2)
                        act.activation(aT_hi[:, f, :], work[2 + n - 2][:, :], ACT.Copy).then_inc(aT_hi_ready, 1)

            for n in range(2 * D_GRAN - RING):
                split_hi(G_DOWN + n + AHEAD)
                if n == D_GRAN + 1:
                    for r in range(ROWS):
                        act.wait_ge(x2_ready, r + 1)
                        square(2, x1, r, (0,))
            for n in range(AHEAD):
                split_hi(N_GRAN - AHEAD + n)
            for r in range(ROWS):
                act.wait_ge(x2_ready, ROWS + r + 1)
                square(2, x1, r, (1,))

        @block.vector
        def _(dve):
            def mean_of_squares(i, r, n_squares):
                dve.wait_ge(norm[i]["squared"], n_squares)
                dve.tensor_tensor(mean_sq[:, r:r + 1], square_sum[:, r, 0:1], square_sum[:, r, 1:2],
                                  ALU.add).then_inc(norm[i]["summed"], 1)
                dve.wait_ge(norm[i]["summed"], 2 * r + 1)
                dve.tensor_scalar(mean_sq[:, r:r + 1], mean_sq[:, r:r + 1], 1.0 / D, EPS, ALU.mult,
                                  ALU.add).then_inc(norm[i]["summed"], 1)

            def normalise(i, src, r, gain, dst):
                dve.wait_ge(norm[i]["rstd_ready"], r + 1)
                dve.scalar_tensor_tensor(out=dst, in0=src[:, r, :], scalar=rstd[:, r:r + 1], in1=gain[:, :],
                                         op0=ALU.mult, op1=ALU.mult).then_inc(norm[i]["xn_ready"], 1)

            def take_hT_lo(i, r):
                for half in range(2):
                    dve.wait_ge(norm[i]["hT_hi_ready"], 2 * r + half + 1)
                    bank = norm_bank(i, r, half)
                    hT = (slice(None), slice(4 * half, 4 * half + 4), slice(r * P, (r + 1) * P))
                    dve.tensor_tensor(hT_lo[hT], psum[bank][:, :].rearrange("p (k c) -> p k c", k=4),
                                      hT_hi[hT].bitcast(F32), ALU.subtract).then_inc(norm[i]["hT_lo_ready"], 1)

            def split_lo(g):
                if g >= N_GRAN:
                    return
                dve.wait_ge(hi_split, g + 1)
                dve.tensor_tensor(ring(w_lo, g), staged(g), ring(w_hi, g).bitcast(F32),
                                  ALU.subtract).then_inc(lo_split, 1)

            dve.wait_ge(gain1_in, 16)
            for r in range(ROWS):
                mean_of_squares(0, r, 2 * r + 2)
                if r >= 2:
                    dve.wait_ge(norm[0]["xn_T"], 2 * (r - 1))
                normalise(0, x_nat, r, gain_a, xn[r % 2][:, :])
                if r >= 1:
                    take_hT_lo(0, r - 1)
            for g in range(AHEAD):
                split_lo(g)
            take_hT_lo(0, ROWS - 1)
            dve.wait_ge(vec_T, 1)
            dve.tensor_copy(vec[:, :], psum[0][:, 0:N_VEC]).then_inc(vec_ready, 1)
            dve.tensor_scalar(vec_half[:, :], psum[0][:, 0:N_VEC], 0.5, None, ALU.mult).then_inc(vec_ready, 1)
            dve.wait_ge(vec_ready, 2)

            def qk_of(b):
                dve.wait_ge(conv_tanh, b + 1)
                dst = (q_m if b < KB else k_m)[:, b % KB, :]
                dve.scalar_tensor_tensor(out=dst, in0=work[2 + b % 2][:, :], scalar=1.0, in1=work[b % 2][:, :],
                                         op0=ALU.add, op1=ALU.mult).then_inc(qk_ready, 1)

            for g in range(G_BR):
                split_lo(g + AHEAD)
                if g == 0:
                    dve.wait_ge(used, 1)
                    dve.wait_ge(gbias_in, 32)
                    dve.tensor_scalar(gate_rows[0:LANES + H_M, :], psum[1][0:LANES + H_M, :], gate_bias[:, 0:1], None,
                                      ALU.add).then_inc(gate_rows_ready, 1)
                if G_QK <= g < G_MV:
                    b = g - G_QK
                    if b >= 1:
                        qk_of(b - 1)
                    dve.wait_ge(z_padded, b + 1)
                    if b >= 2:
                        dve.wait_ge(qk_ready, b - 1)
                    u = work[b % 2]
                    dve.tensor_scalar(u[:, :], z_pad[:, 0:SEQ], vec[:, V_CONVW + b:V_CONVW + b + 1],
                                      vec[:, V_CONVB + b:V_CONVB + b + 1], ALU.mult, ALU.add).then_inc(conv_tap, 1)
                    for j in range(1, CONV_K):
                        dve.wait_ge(conv_tap, CONV_K * b + j)
                        c = V_CONVW + 8 * j + b
                        dve.scalar_tensor_tensor(out=u[:, :], in0=z_pad[:, j:j + SEQ], scalar=vec[:, c:c + 1],
                                                 in1=u[:, :], op0=ALU.mult, op1=ALU.add).then_inc(conv_tap, 1)
                if g == G_MV:
                    qk_of(7)
                if g == G_QK:
                    dve.wait_ge(gates_T, 1)
                    dve.tensor_copy(gates[:, :, :], psum[4][:, 0:64].rearrange("p (j l) -> p j l", l=16)).then_inc(gates_ready, 1)
                    dve.wait_ge(gates_ready, 1)
                    lanes = gates[:, :, H_M:]
                    dve.tensor_scalar(abs_neg, lanes, -1.0, None, ALU.mult).then_inc(gates_ready, 1)
                    dve.wait_ge(gates_ready, 2)
                    dve.tensor_tensor(abs_neg, abs_neg, lanes, ALU.min).then_inc(gate_abs, 1)
                if g == G_QK + 1:
                    dve.wait_ge(gate_ln, 1)
                    dve.scalar_tensor_tensor(out=log_f[:, :, :], in0=gates[:, :, H_M:], scalar=0.0, in1=softp,
                                             op0=ALU.min, op1=ALU.subtract).then_inc(log_f_ready, 1)
                if g == G_QK + 3:
                    dve.wait_ge(cum_done, 1)
                    cums = psum[4][:, 64:64 + ROWS * LANES].rearrange("p (j l) -> p j l", l=LANES)
                    tots = psum[4][:, 128:128 + ROWS * LANES].rearrange("p (j l) -> p j l", l=LANES)
                    n = 0

                    def step(ins):
                        nonlocal n
                        ins.then_inc(frame_step, 1)
                        n += 1
                        dve.wait_ge(frame_step, n)

                    step(dve.tensor_copy(cum[:, :, :], cums))
                    step(dve.tensor_scalar(frame[:, 0::ROWS + 1, :], cum[:, :, :], -1.0, None, ALU.mult))
                    step(dve.tensor_tensor(frame[:, 0::ROWS + 1, 0:H_M], gates[:, :, 0:H_M],
                                           frame[:, 0::ROWS + 1, 0:H_M], ALU.add))
                    step(dve.memset(before[:, 0, :], 0.0))
                    for q in range(1, ROWS):
                        tot = tots[:, q - 1, :]
                        step(dve.tensor_tensor(frame[:, ROWS * q:ROWS * q + q, :],
                                               frame[:, ROWS * (q - 1):ROWS * (q - 1) + q, :],
                                               tots[:, q - 1:q, :].to_broadcast([P, q, LANES]), ALU.add))
                        step(dve.tensor_tensor(before[:, q, :], before[:, q - 1, :], tot[:, 0:H_M], ALU.add))
                    assert n == FRAME_STEPS
                if g == G_QK + 5:
                    for n, (a, b) in enumerate(ROW_CHUNKS):
                        dve.wait_ge(rows_hi_ready, n + 1)
                        dve.tensor_tensor(rows_lo[:, a * P:b * P], psum[5 + n][0:LANES, 0:(b - a) * P],
                                          rows_hi[:, a * P:b * P].bitcast(F32), ALU.subtract).then_inc(rows_lo_ready, 1)
                if g in (G_FV - 1, G_FQK - 1):
                    n = (G_FV - 1, G_FQK - 1).index(g)
                    dve.wait_ge(used, g + 1)
                    dve.wait_ge(vbias_in, 32)
                    dve.wait_ge(norm[0]["xn_ready"], ROWS)
                    for r in range(ROWS):
                        if n == 0:
                            dve.tensor_tensor(v_m[:, r, :, 0:DH_M], psum[4 + r][:, :].rearrange("p (h d) -> p h d", h=H_M),
                                              v_bias[:, 0, :].rearrange("p (h d) -> p h d", h=H_M), ALU.add).then_inc(v_ready, 1)
                        else:
                            dve.tensor_tensor(v_f[:, r, :], psum[r][:, :], v_bias[:, 1, :], ALU.add).then_inc(v_ready, 1)
                if G_FQK <= g < G_FQK + KB:
                    b = g - G_FQK
                    dve.wait_ge(used, g + 1)
                    dve.tensor_scalar(q_f[:, b, :], psum[fqk_bank(b)][:, :], vec[:, V_FQK + b:V_FQK + b + 1],
                                      DH_F ** -0.5, ALU.add, ALU.mult).then_inc(fq_ready, 1)
                if G_FQK <= g < G_MO:
                    for u in (2 * (g - G_FQK), 2 * (g - G_FQK) + 1):
                        q, h = u // H_M, u % H_M
                        dve.wait_ge(g_spread, u + 1)
                        dve.reduce_max(m_stab[:, q, h:h + 1], psum[u % 2][:, 0:(q + 1) * P], AX.X).then_inc(g_max, 1)
                if g == G_MO:
                    dve.wait_ge(g_max, 16)
                    dve.tensor_tensor(m_stab[:, :, :], m_stab[:, :, :], before[:, :, :], ALU.max).then_inc(m_step, 1)
                    dve.wait_ge(m_step, 1)
                    dve.tensor_tensor(m_floor[:, :, :], m_stab[:, :, :], cum[:, :, 0:H_M], ALU.add).then_inc(m_step, 1)
                if g >= G_MO:
                    b = g - G_MO
                    dve.wait_ge(mo_tanh, b + 1)
                    dve.tensor_scalar(o_gate[:, b, :], work[2 + b % 2][:, :], 1.0,
                                      vec_half[:, V_NORM + b:V_NORM + b + 1], ALU.add, ALU.mult).then_inc(o_ready, 1)

            def take_ymT(h):
                dve.wait_ge(y_mT, h + 1)
                if h >= 2:
                    dve.wait_ge(ymT_lo_ready, h - 1)
                dve.tensor_tensor(work[4 + h % 2][:, :], psum[7][:, :], o_gate[:, h, :], ALU.mult).then_inc(y_m32, 1)
                dve.wait_ge(ymT_hi_ready, h + 1)
                dve.tensor_tensor(ymT_lo[:, h, :], work[4 + h % 2][:, :], ymT_hi[:, h, :].bitcast(F32),
                                  ALU.subtract).then_inc(ymT_lo_ready, 1)

            QK_SCALE = 0.25 * DH_M ** -0.5
            for i in range(H_M + 3):
                if i < H_M:
                    dve.wait_ge(m_spread, i + 1)
                    if i >= 2:
                        dve.wait_ge(decay_exp, 10 * (i - 1))
                    dve.tensor_tensor(stab_masked[i % 2][:, :].rearrange("p (q t) -> p q t", q=ROWS),
                                      psum[2 + i % 2][:, :].rearrange("p (q t) -> p q t", q=ROWS),
                                      mask_T[:, :].rearrange("p (a t) -> p a t", a=1).to_broadcast([P, ROWS, P]),
                                      ALU.add).then_inc(m_masked, 1)
                if 2 <= i <= H_M + 1:
                    h = i - 2
                    dve.wait_ge(h_squared, h + 1)
                    if h >= 1:
                        dve.wait_ge(h_rstd, h)
                    dve.reduce_sum(head_ms[:, :], work[2][:, :].rearrange("p (q d) -> p q d", q=ROWS), AX.X).then_inc(h_mean, 1)
                    dve.wait_ge(h_mean, 2 * h + 1)
                    dve.tensor_scalar(head_ms[:, :], head_ms[:, :], 1.0 / DH_M, EPS, ALU.mult, ALU.add).then_inc(h_mean, 1)
                if i < H_M:
                    h = i
                    for j in range(ROWS):
                        o, n = decay_at(j), SEQ - j * P
                        src = psum[4 + min(j, 2)][:, (0, 0, 0, 256)[j]:(0, 0, 0, 256)[j] + n]
                        dve.wait_ge(s_m, 4 * h + min(j + 1 + j // 2, ROWS))
                        dve.wait_ge(decay_exp, 10 * h + sum(ROWS - m for m in range(j + 1)))
                        dve.scalar_tensor_tensor(out=decay[h % 2][:, o:o + n], in0=src, scalar=QK_SCALE,
                                                 in1=decay[h % 2][:, o:o + n], op0=ALU.mult,
                                                 op1=ALU.mult).then_inc(weighted, 1)
                if 1 <= i <= H_M:
                    h = i - 1
                    if h == 0:
                        dve.wait_ge(floor_ready, 1)
                    if h >= 1:
                        dve.wait_ge(h_m, 2 * h)
                    for n in range(2):
                        dve.wait_ge(num_m, 2 * h + n + 1)
                        tile = psum[n][:, 0:2 * (DH_M + 1)].rearrange("p (q d) -> p q d", q=2)
                        dve.scalar_tensor_tensor(out=den[:, 2 * n:2 * n + 2], in0=tile[:, :, DH_M], scalar=-1.0,
                                                 in1=m_floor[:, 2 * n:2 * n + 2, h], op0=ALU.mult,
                                                 op1=ALU.max).then_inc(den_step, 1)
                    for n in range(2):
                        tile = psum[n][:, 0:2 * (DH_M + 1)].rearrange("p (q d) -> p q d", q=2)
                        dve.wait_ge(den_step, 5 * h + n + 1)
                        dve.tensor_tensor(den[:, 2 * n:2 * n + 2], tile[:, :, DH_M], den[:, 2 * n:2 * n + 2],
                                          ALU.max).then_inc(den_step, 1)
                    dve.wait_ge(den_step, 5 * h + 4)
                    dve.reciprocal(den[:, :], den[:, :]).then_inc(den_step, 1)
                    dve.wait_ge(den_step, 5 * h + 5)
                    if h >= 2:
                        dve.wait_ge(y_m, h - 1)
                    for n in range(2):
                        tile = psum[n][:, 0:2 * (DH_M + 1)].rearrange("p (q d) -> p q d", q=2)
                        dve.tensor_tensor(work[h % 2][:, 256 * n:256 * n + 256].rearrange("p (q d) -> p q d", q=2),
                                          tile[:, :, 0:DH_M],
                                          den[:, 2 * n:2 * n + 2].rearrange("p (q a) -> p q a", a=1).to_broadcast([P, 2, DH_M]),
                                          ALU.mult).then_inc(h_m, 1)
                if 2 <= i <= H_M + 1:
                    h = i - 2
                    dve.wait_ge(h_rstd, h + 1)
                    if h >= 1:
                        dve.wait_ge(y_mT, h)
                    dve.tensor_tensor(work[3][:, :].rearrange("p (q d) -> p q d", q=ROWS),
                                      work[h % 2][:, :].rearrange("p (q d) -> p q d", q=ROWS),
                                      head_rs[:, :].rearrange("p (q a) -> p q a", a=1).to_broadcast([P, ROWS, DH_M]),
                                      ALU.mult).then_inc(y_m, 1)
                if i >= 3:
                    take_ymT(i - 3)

            def take_yfT_lo(hp):
                dve.wait_ge(yfT_hi_ready, hp + 1)
                dve.tensor_tensor(yfT_lo[:, hp, :], psum[7][:, :], yfT_hi[:, hp, :].bitcast(F32),
                                  ALU.subtract).then_inc(yfT_lo_ready, 1)

            for u in range(32 + 3):
                if u < 32:
                    _, q, _ = fox_unit(u)
                    dve.wait_ge(logits, u + 1)
                    if u >= 4:
                        dve.wait_ge(fox_exp, u - 3)
                    dve.tensor_reduce(neg_max[:, u % 4:u % 4 + 1], psum[4 + u % 3][:, 0:(q + 1) * P], AX.X, ALU.max,
                                      negate=True).then_inc(fox_max, 1)
                if 2 <= u < 34:
                    w = u - 2
                    _, q, _ = fox_unit(w)
                    n = (q + 1) * P
                    dve.wait_ge(fox_T, w + 1)
                    if w >= 2:
                        dve.wait_ge(fox_pv, w - 1)
                    dve.tensor_copy(work[3 + w % 2][:, 0:n], psum[2 + w % 2][:, 0:n]).then_inc(fox_PT, 1)
                if u >= 3:
                    w = u - 3
                    hp, q, h2 = fox_unit(w)
                    dve.wait_ge(fox_exp, w + 1)
                    if w >= 4:
                        dve.wait_ge(fox_y, w - 3)
                    dve.reciprocal(row_inv[:, w % 4:w % 4 + 1], row_sum[:, w % 4:w % 4 + 1]).then_inc(fox_inv, 1)
                    dve.wait_ge(fox_inv, w + 1)
                    dve.wait_ge(fox_pv, w + 1)
                    if hp >= 2:
                        dve.wait_ge(y_fT, hp - 1)
                    dve.tensor_scalar(y_nat[hp % 2][:, q, h2 * DH_F:(h2 + 1) * DH_F], psum[w % 2][:, 0:DH_F],
                                      row_inv[:, w % 4:w % 4 + 1], None, ALU.mult).then_inc(fox_y, 1)
                if u >= 8 and u % 8 == 5 and u < 32:
                    take_yfT_lo(u // 8 - 1)
            take_yfT_lo(KB - 1)

            for c in range(4):
                for n in range(6):
                    split_lo(G_BR + 6 * c + n + AHEAD)
                    if n >= 4:
                        j, b = n - 4, 2 * c + n - 4
                        dve.wait_ge(used, G_BR + 6 * c + n + 1)
                        dve.wait_ge(gate_tanh, 4 * c + 4)
                        if b >= 2:
                            dve.wait_ge(mix_lo_ready, b - 1)
                        if b >= 1:
                            dve.wait_ge(mix_step, 3 * b)
                        if b == 0:
                            dve.wait_ge(fox_PT, 32)
                        s = mix_sum[b % 2]
                        dve.scalar_tensor_tensor(out=s[:, :], in0=work[j][:, :], scalar=1.0, in1=psum[2 * j][:, :],
                                                 op0=ALU.add, op1=ALU.mult).then_inc(mix_step, 1)
                        dve.scalar_tensor_tensor(out=work[4][:, :], in0=work[2 + j][:, :], scalar=1.0, in1=psum[2 * j + 1][:, :],
                                                 op0=ALU.add, op1=ALU.mult).then_inc(mix_step, 1)
                        dve.wait_ge(mix_step, 3 * b + 2)
                        dve.tensor_tensor(s[:, :], s[:, :], work[4][:, :], ALU.add).then_inc(mix_step, 1)
                        dve.wait_ge(mix_hi_ready, b + 1)
                        dve.scalar_tensor_tensor(out=mixT_lo[:, b, :], in0=s[:, :], scalar=0.5,
                                                 in1=mixT_hi[:, b, :].bitcast(F32), op0=ALU.mult,
                                                 op1=ALU.subtract).then_inc(mix_lo_ready, 1)

            for n in range(4):
                split_lo(G_OUT + n + AHEAD)
            dve.wait_ge(used, G_OUT + 4)
            dve.wait_ge(xagain_in, 16)
            for r in range(ROWS):
                dve.tensor_tensor(x1[:, r, 0:HALF], x1[:, r, 0:HALF], psum[r][:, :], ALU.add).then_inc(x1_ready, 1)
            split_lo(G_OUT + 6)
            split_lo(G_OUT + 7)
            dve.wait_ge(gain2_in, 16)
            for r in range(ROWS):
                if r < ROWS - 1:
                    dve.wait_ge(row_out, r + 1)
                else:
                    dve.wait_ge(used, G_OUT + 8)
                dve.tensor_tensor(x1[:, r, HALF:D], x1[:, r, HALF:D], psum[4 + r][:, :], ALU.add).then_inc(x1_ready, 1)
                mean_of_squares(1, r, 2 * r + 2)
                if r >= 2:
                    dve.wait_ge(norm[1]["xn_T"], 2 * (r - 1))
                normalise(1, x1, r, gain_b, xn2[r % 2][:, :])
                if r >= 1:
                    take_hT_lo(1, r - 1)
                if r == ROWS - 2:
                    for n in range(AHEAD):
                        split_lo(G_FFN + n)
            take_hT_lo(1, ROWS - 1)

            for p in range(F_BLOCKS // 2):
                for n in range(4):
                    g = G_FFN + 4 * p + n
                    split_lo(g + AHEAD)
                    if n >= 2:
                        j, f = n - 2, 2 * p + n - 2
                        y = work[2 + j]
                        dve.wait_ge(used, g + 1)
                        dve.wait_ge(ffn_tanh, f + 1)
                        if f >= 2:
                            dve.wait_ge(aT_lo_ready, f - 1)
                        dve.scalar_tensor_tensor(out=y[:, :], in0=work[j][:, :], scalar=1.0,
                                                 in1=psum[4 * (p % 2) + j][:, :], op0=ALU.add,
                                                 op1=ALU.mult).then_inc(ffn_step, 1)
                        dve.wait_ge(ffn_step, 2 * f + 1)
                        dve.scalar_tensor_tensor(out=y[:, :], in0=y[:, :], scalar=0.5,
                                                 in1=psum[4 * (p % 2) + n][:, :], op0=ALU.mult,
                                                 op1=ALU.mult).then_inc(ffn_step, 1)
                        dve.wait_ge(aT_hi_ready, f + 1)
                        dve.tensor_tensor(aT_lo[:, f, :], y[:, :], aT_hi[:, f, :].bitcast(F32),
                                          ALU.subtract).then_inc(aT_lo_ready, 1)

            for n in range(2 * D_GRAN - RING):
                split_lo(G_DOWN + n + AHEAD)
                if n == D_GRAN - 1:
                    dve.wait_ge(used, G_DOWN + D_GRAN)
                    dve.wait_ge(norm[1]["xn_ready"], ROWS)
                    for r in range(ROWS):
                        dve.tensor_tensor(x1[:, r, 0:HALF], x1[:, r, 0:HALF], psum[4 + r][:, :], ALU.add).then_inc(x2_ready, 1)
            for n in range(AHEAD):
                split_lo(N_GRAN - AHEAD + n)
            dve.wait_ge(gain3_in, 16)
            for r in range(ROWS):
                if r < ROWS - 1:
                    dve.wait_ge(row_down, r + 1)
                else:
                    dve.wait_ge(used, N_GRAN)
                dve.tensor_tensor(x1[:, r, HALF:D], x1[:, r, HALF:D], psum[r][:, :], ALU.add).then_inc(x2_ready, 1)
                mean_of_squares(2, r, ROWS + r + 1)
                normalise(2, x1, r, gain_a, x1[:, r, :])

        @block.tensor
        def _(pe):
            freed = {}

            def take(bank, by):
                if bank in freed:
                    pe.wait_ge(*freed[bank])
                freed[bank] = by

            def three(o, a_hi, a_lo, b_hi, b_lo, first, last):
                pe.matmul(o, a_hi, b_hi, start=first, stop=False)
                pe.matmul(o, a_hi, b_lo, start=False, stop=False)
                return pe.matmul(o, a_lo, b_hi, start=False, stop=last)

            def transpose_rows(i, tiles):
                def one(r):
                    pe.wait_ge(norm[i]["xn_ready"], r + 1)
                    for half in range(2):
                        bank = norm_bank(i, r, half)
                        take(bank, (norm[i]["hT_lo_ready"], 2 * r + half + 1))
                        for k in range(4):
                            c = (4 * half + k) * P
                            last = pe.transpose(psum[bank][:, k * P:(k + 1) * P], tiles[r % 2][:, c:c + P], ident[:, :])
                        last.then_inc(norm[i]["xn_T"], 1)
                return one

            def columns(g, bank, by, src_hi, src_lo, k0=0, n=KD, last_of_granule=True):
                take(bank, by)
                wh, wl = ring(w_hi, g), ring(w_lo, g)
                for k in range(n):
                    last = three(psum[bank][:, :], wh[:, k0 + k, :], wl[:, k0 + k, :], src_hi[:, k, :], src_lo[:, k, :],
                                 k == 0, k == n - 1)
                if last_of_granule:
                    last.then_inc(used, 1)

            def z_columns(g, bank, by):
                pe.wait_ge(lo_split, g + 1)
                columns(g, bank, by, hT_hi, hT_lo)

            def row_product(g, bank, r, src_hi, src_lo, k0, first, last):
                wh, wl = ring(w_hi, g), ring(w_lo, g)
                rows = slice(r * P, (r + 1) * P)
                for k in range(2):
                    ins = three(psum[bank][:, :], src_hi[:, k0 + k, rows], src_lo[:, k0 + k, rows], wh[:, k, :], wl[:, k, :],
                                first and k == 0, last and k == 1)
                return ins

            pe.wait_ge(consts, N_CONSTS)
            one = transpose_rows(0, xn)
            for r in range(ROWS):
                one(r)
            pe.wait_ge(vec_in, 16 * 7)
            take(0, (vec_ready, 2))
            pe.transpose(psum[0][:, 0:N_VEC], vec_raw[:, :], ident[0:N_VEC, 0:N_VEC]).then_inc(vec_T, 1)
            pe.wait_ge(norm[0]["hT_lo_ready"], 2 * ROWS)
            z_columns(0, 1, (gate_rows_ready, 1))

            for b in range(8):
                z_columns(G_QK + b, qk_bank(b), (z_padded, b + 1))
                if b == 0:
                    pe.wait_ge(gate_rows_ready, 1)
                    take(4, (frame_step, FRAME_STEPS))
                    for j in range(ROWS):
                        last = pe.transpose(psum[4][:, 16 * j:16 * j + 16], gate_rows[0:16, j * P:(j + 1) * P], ident[0:16, 0:16])
                    last.then_inc(gates_T, 1)
                if b == 2:
                    pe.wait_ge(log_f_ready, 1)
                    lf = log_f[:, :, :].rearrange("p j l -> p (j l)")
                    pe.matmul(psum[4][:, 64:64 + ROWS * LANES], upper[:, :], lf, start=True, stop=True)
                    pe.matmul(psum[4][:, 128:128 + ROWS * LANES], ones[:, :], lf, start=True, stop=True).then_inc(cum_done, 1)
                if b == 4:
                    pe.wait_ge(frame_step, FRAME_STEPS)
                    for n, (a, z) in enumerate(ROW_CHUNKS):
                        take(5 + n, (rows_lo_ready, n + 1))
                        for m in range(a, z):
                            q = next(i for i in range(ROWS) if pair(i, i) >= m)
                            last = pe.transpose(psum[5 + n][0:LANES, (m - a) * P:(m - a + 1) * P],
                                                frame[:, ROWS * q + m - pair(q, 0), :], ident[:, :])
                        last.then_inc(frame_T, 1)

            for n, (g0, bank0) in enumerate(((G_MV, 4), (G_FV, 0))):
                for r in range(ROWS):
                    take(bank0 + r, (v_ready, ROWS * n + r + 1))
                for d in range(4):
                    pe.wait_ge(lo_split, g0 + d + 1)
                    for r in range(ROWS):
                        last = row_product(g0 + d, bank0 + r, r, hT_hi, hT_lo, 2 * d, d == 0, d == 3)
                    last.then_inc(used, 1)

            def spread_row(bank, lane, q, first, last):
                n = (q + 1) * P
                cols = slice(pair(q, 0) * P, pair(q, 0) * P + n)
                one_hot = ident_r[:, lane:lane + 1].to_broadcast([LANES, P])
                pe.matmul(psum[bank][:, 0:n], one_hot, rows_hi[:, cols], start=first, stop=False)
                pe.matmul(psum[bank][:, 0:n], one_hot, rows_lo[:, cols], start=False, stop=False)
                return pe.matmul(psum[bank][:, q * P:n], ident_b[:, :], mask_b[:, :], start=False, stop=last)

            for b in range(8):
                z_columns(G_FQK + b, fqk_bank(b), (fq_ready, b + 1) if b < KB else (fk_ready, b - KB + 1))
                if b == 0:
                    pe.wait_ge(rows_lo_ready, 3)
                for u in (2 * b, 2 * b + 1):
                    q, h = u // H_M, u % H_M
                    take(u % 2, (g_max, u + 1))
                    spread_row(u % 2, h, q, True, True).then_inc(g_spread, 1)
            for b in range(4):
                z_columns(G_MO + b, mo_bank(b), (mo_tanh, b + 1))

            def mlstm_scores(h):
                if h == 0:
                    pe.wait_ge(m_step, 2)
                    pe.wait_ge(qk_ready, 8)
                take(2 + h % 2, (decay_exp, 10 * (h + 1)))
                for q in range(ROWS):
                    last = pe.matmul(psum[2 + h % 2][:, q * P:(q + 1) * P],
                                     m_stab[:, q, h:h + 1].to_broadcast([P, P]), ident[:, :], start=True, stop=True)
                last.then_inc(m_spread, 1)
                for j in range(ROWS):
                    o = (0, 0, 0, 256)[j]
                    if j < 3:
                        take(4 + j, (weighted, 4 * h + (j + 1 if j < 2 else 4)))
                    pe.matmul(psum[4 + min(j, 2)][:, o:o + SEQ - j * P], k_m[:, h, j * P:(j + 1) * P],
                              q_m[:, h, j * P:SEQ], start=True, stop=True).then_inc(s_m, 1)

            def mlstm_values(h):
                if h == 0:
                    pe.wait_ge(v_ready, ROWS)
                    pe.wait_ge(v_ones, 1)
                for q in range(ROWS):
                    if q % 2 == 0:
                        take(q // 2, (h_m, 2 * h + q // 2 + 1))
                    pe.wait_ge(weighted, 4 * h + q + 1)
                    for j in range(q + 1):
                        o = decay_at(j) + (q - j) * P
                        last = pe.matmul(psum[q // 2][:, (q % 2) * (DH_M + 1):(q % 2 + 1) * (DH_M + 1)],
                                         decay[h % 2][:, o:o + P], v_m[:, j, h, :], start=(j == 0), stop=(j == q))
                    if q % 2:
                        last.then_inc(num_m, 1)

            def mlstm_transpose(h):
                pe.wait_ge(y_m, h + 1)
                take(7, (y_m32, h + 1))
                for q in range(ROWS):
                    last = pe.transpose(psum[7][:, q * P:(q + 1) * P], work[3][:, q * P:(q + 1) * P], ident[:, :])
                last.then_inc(y_mT, 1)

            def fox_logits(u):
                hp, q, h2 = fox_unit(u)
                if u == 0:
                    pe.wait_ge(fq_ready, KB)
                    pe.wait_ge(fk_ready, KB)
                bank, n = 4 + u % 3, (q + 1) * P
                head = slice(h2 * DH_F, (h2 + 1) * DH_F)
                take(bank, (fox_exp, u + 1))
                pe.matmul(psum[bank][:, 0:n], q_f[head, hp, q * P:(q + 1) * P], k_f[head, hp, 0:n], start=True, stop=False)
                spread_row(bank, H_M + 2 * hp + h2, q, False, True).then_inc(logits, 1)

            def fox_transpose(u):
                _, q, _ = fox_unit(u)
                pe.wait_ge(fox_exp, u + 1)
                take(2 + u % 2, (fox_PT, u + 1))
                for j in range(q + 1):
                    last = pe.transpose(psum[2 + u % 2][:, j * P:(j + 1) * P], work[u % 3][:, j * P:(j + 1) * P], ident[:, :])
                last.then_inc(fox_T, 1)

            def fox_values(u):
                hp, q, h2 = fox_unit(u)
                if u == 0:
                    pe.wait_ge(v_ready, 2 * ROWS)
                pe.wait_ge(fox_PT, u + 1)
                take(u % 2, (fox_y, u + 1))
                c = (2 * hp + h2) * DH_F
                for j in range(q + 1):
                    last = pe.matmul(psum[u % 2][:, 0:DH_F], work[3 + u % 2][:, j * P:(j + 1) * P], v_f[:, j, c:c + DH_F],
                                     start=(j == 0), stop=(j == q))
                last.then_inc(fox_pv, 1)

            def fox_pair_transpose(hp):
                pe.wait_ge(fox_y, 8 * (hp + 1))
                take(7, (yfT_lo_ready, hp + 1))
                for q in range(ROWS):
                    last = pe.transpose(psum[7][:, q * P:(q + 1) * P], y_nat[hp % 2][:, q, :], ident[:, :])
                last.then_inc(y_fT, 1)

            mlstm_scores(0)
            mlstm_scores(1)
            mlstm_values(0)
            mlstm_scores(2)
            mlstm_values(1)
            mlstm_transpose(0)
            mlstm_scores(3)
            mlstm_values(2)
            mlstm_transpose(1)
            fox_logits(0)
            mlstm_values(3)
            mlstm_transpose(2)
            fox_logits(1)
            mlstm_transpose(3)
            for u in range(2, 35):
                if u < 32:
                    fox_logits(u)
                if u < 34:
                    fox_transpose(u - 2)
                if u == 32:
                    z_columns(G_BR, GATE_BANKS[0], (gate_tanh, 1))
                if u == 33:
                    z_columns(G_BR + 1, GATE_BANKS[1], (gate_tanh, 2))
                if u >= 3:
                    fox_values(u - 3)
                if u >= 12 and u % 8 == 4:
                    fox_pair_transpose(u // 8 - 1)
            fox_pair_transpose(KB - 1)

            for c in range(4):
                for n in range(4):
                    if c or n >= 2:
                        z_columns(G_BR + 6 * c + n, GATE_BANKS[n], (gate_tanh, 4 * c + n + 1))
                if c == 0:
                    pe.wait_ge(ymT_lo_ready, H_M)
                    pe.wait_ge(yfT_lo_ready, KB)
                for j in range(2):
                    g, b = G_BR + 6 * c + 4 + j, 2 * c + j
                    pe.wait_ge(lo_split, g + 1)
                    columns(g, 2 * j, (mix_step, 3 * b + 1), ymT_hi, ymT_lo, 0, KB, False)
                    columns(g, 2 * j + 1, (mix_step, 3 * b + 2), yfT_hi, yfT_lo, KB, KB)

            for r in range(ROWS):
                take(r, (x1_ready, r + 1))
            for d in range(4):
                pe.wait_ge(lo_split, G_OUT + d + 1)
                pe.wait_ge(mix_lo_ready, 2 * d + 2)
                for r in range(ROWS):
                    last = row_product(G_OUT + d, r, r, mixT_hi, mixT_lo, 2 * d, d == 0, d == 3)
                last.then_inc(used, 1)
            one = transpose_rows(1, xn2)
            for r in range(ROWS):
                take(4 + r, (x1_ready, ROWS + r + 1))
                for d in range(4):
                    if r == 0:
                        pe.wait_ge(lo_split, G_OUT + 4 + d + 1)
                    last = row_product(G_OUT + 4 + d, 4 + r, r, mixT_hi, mixT_lo, 2 * d, d == 0, d == 3)
                    if r == ROWS - 1:
                        last.then_inc(used, 1)
                if r < ROWS - 1:
                    last.then_inc(row_out, 1)
                if r >= 1:
                    one(r - 1)
            one(ROWS - 1)

            pe.wait_ge(norm[1]["hT_lo_ready"], 2 * ROWS)
            for p in range(F_BLOCKS // 2):
                for n in range(4):
                    f = 2 * p + n % 2
                    z_columns(G_FFN + 4 * p + n, 4 * (p % 2) + n, (ffn_step, 2 * f + 1 + n // 2))

            for half in range(2):
                bank0 = 4 - 4 * half
                for r in range(ROWS):
                    take(bank0 + r, (x2_ready, ROWS * half + r + 1))
                n_shared = D_GRAN - half * RING
                for d in range(n_shared):
                    g = G_DOWN + half * D_GRAN + d
                    pe.wait_ge(lo_split, g + 1)
                    pe.wait_ge(aT_lo_ready, 2 * d + 2)
                    for r in range(ROWS):
                        last = row_product(g, bank0 + r, r, aT_hi, aT_lo, 2 * d, d == 0, d == D_GRAN - 1)
                    last.then_inc(used, 1)
            for r in range(ROWS):
                for d in range(D_GRAN - RING, D_GRAN):
                    g = G_DOWN + D_GRAN + d
                    if r == 0:
                        pe.wait_ge(lo_split, g + 1)
                    last = row_product(g, r, r, aT_hi, aT_lo, 2 * d, False, d == D_GRAN - 1)
                    if r == ROWS - 1:
                        last.then_inc(used, 1)
                if r < ROWS - 1:
                    last.then_inc(row_down, 1)


N_CONSTS = 15
FRAME_STEPS = 10
ROW_CHUNKS = ((0, 4), (4, 8), (8, 10))
GATE_BANKS = (6, 4, 5, 7)


def norm_bank(i, r, half):
    return 2 * r + half if i == 0 else (2 * r + half) % 4


def qk_bank(b):
    return (2 + b) % 4


def fqk_bank(b):
    return 4 + b % 4


def mo_bank(b):
    return 4 + b % 4


def fox_unit(u):
    return u // 8, u % 8 // 2, u % 2


_INS = ["x", "norm1_g", "w_in", "b_in", "conv_w", "conv_b", "mlstm_norm_g", "w_br_mlstm", "w_br_fox",
        "w_out", "norm2_g", "w_gate", "w_up", "w_down", "norm_f_g"]


def kernel(**inputs):
    import concourse.bacc as bacc
    from concourse.bass_utils import run_bass_kernel_spmd

    nc = bacc.Bacc("TRN2", target_bir_lowering=False, num_devices=1)
    arrays, args = {}, []
    for name in _INS:
        a = np.ascontiguousarray(inputs[name])
        arrays[f"in_{name}"] = a
        args.append(nc.dram_tensor(f"in_{name}", a.shape, mybir.dt.from_np(a.dtype), kind="ExternalInput").ap())
    out = nc.dram_tensor("out_block", (1, SEQ, D), F32, kind="ExternalOutput").ap()
    block_kernel(nc, *args, out)
    r = run_bass_kernel_spmd(nc, [arrays], core_ids=[0])
    return r.results[0]["out_block"]
```

```python
import numpy as np
import concourse.bass as bass
from concourse import mybir
from contextlib import ExitStack

F32 = mybir.dt.float32
F32R = mybir.dt.float32r
BF16 = mybir.dt.bfloat16
ACT = mybir.ActivationFunctionType
ALU = mybir.AluOpType
AX = mybir.AxisListType

P = 128
D = 1024
SEQ = 512
ROWS = SEQ // P
KD = D // P
HALF = D // 2
H_M, H_F = 4, 8
W_M = W_F = D // 2
DH_M, DH_F = W_M // H_M, W_F // H_F
KB = W_M // P
CONV_K = 4
D_FF = 2816
F_BLOCKS = D_FF // P
EPS = 1e-6
LANES = H_M + H_F
NEG = -1.0e30

C_QK = 0
C_MV = 2 * W_M
C_MO = 3 * W_M
C_MI = 4 * W_M
C_FQK = C_MI + 2 * H_M
C_FV = C_FQK + 2 * W_F
C_FF = C_FV + W_F
C_GM = C_FF + H_F
C_GF = C_GM + D

V_QK, V_MO, V_FQK, V_GM, V_GF = 0, 8, 12, 20, 28
V_CONVW, V_CONVB, V_NORM, N_VEC = 36, 68, 76, 80

RING = 4
STAGES = 2
AHEAD = 2
GRAN = 1024


def block_kernel(nc, x, norm1_g, w_in, b_in, conv_w, conv_b, mlstm_norm_g, w_br_mlstm,
                 w_br_fox, w_out, norm2_g, w_gate, w_up, w_down, norm_f_g, out):
    w_in, b_in = w_in[0], b_in[0]
    conv_w, conv_b, mlstm_norm_g = conv_w[0], conv_b[0], mlstm_norm_g[0]
    w_bm, w_bf, w_o = w_br_mlstm[0], w_br_fox[0], w_out[0]
    w_g, w_u, w_d = w_gate[0], w_up[0], w_down[0]
    norm1_g, norm2_g = norm1_g[0], norm2_g[0]
    x_rows = x[0].rearrange("(r p) d -> r p d", p=P)
    out_rows = out[0].rearrange("(r p) d -> r p d", p=P)

    slots, granules = [], []

    def slot(views, loads):
        for view in views:
            granules.append((len(slots), view))
        slots.append((len(granules), loads))

    def whole(n):
        return lambda st: st.rearrange("p (k c) -> p k c", k=n)

    def column_slot(w, col):
        src = w[:, col:col + 2 * P].rearrange("(k p) c -> p k c", p=P)
        slot([lambda st, j=j: whole(KD)(st)[:, :, j * P:(j + 1) * P] for j in range(2)],
             [(whole(KD), src)])

    def row_slot(w, block, col):
        src = w[block * P:(block + 4) * P, col:col + HALF].rearrange("(k p) c -> p k c", p=P)
        slot([lambda st, j=j: whole(4)(st)[:, 2 * j:2 * j + 2, :] for j in range(2)],
             [(whole(4), src)])

    gate_view = lambda st: st[:, 0:GRAN].rearrange("p (k c) -> p k c", k=KD)
    gate_loads = [
        (lambda st: gate_view(st)[:, :, 0:2 * H_M],
         w_in[:, C_MI:C_MI + 2 * H_M].rearrange("(k p) c -> p k c", p=P)),
        (lambda st: gate_view(st)[:, :, 2 * H_M:P],
         w_in[:, C_FF:C_FF + P - 2 * H_M].rearrange("(k p) c -> p k c", p=P))]
    column_slot(w_in, C_QK)
    G_GATE = len(granules)
    slot([gate_view], gate_loads)
    for i in range(1, 4):
        column_slot(w_in, C_QK + 2 * P * i)
    qk_block = {(b if b < G_GATE else b + 1): b for b in range(2 * KB)}
    G_MV = len(granules)
    for i in range(2):
        row_slot(w_in, 4 * i, C_MV)
    G_FV = len(granules)
    for i in range(2):
        row_slot(w_in, 4 * i, C_FV)
    G_FQK = len(granules)
    for i in range(4):
        column_slot(w_in, C_FQK + 2 * P * i)
    G_MO = len(granules)
    for i in range(2):
        column_slot(w_in, C_MO + 2 * P * i)
    G_BR = len(granules)
    for i in range(4):
        column_slot(w_in, C_GM + 2 * P * i)
        column_slot(w_in, C_GF + 2 * P * i)
        slot([lambda st, j=j: whole(KD)(st)[:, :, j * P:(j + 1) * P] for j in range(2)],
             [(lambda st, n=n: whole(KD)(st)[:, n * KB:(n + 1) * KB, :],
               w[:, 2 * P * i:2 * P * (i + 1)].rearrange("(k p) c -> p k c", p=P))
              for n, w in enumerate((w_bm, w_bf))])
    G_OUT = len(granules)
    S_OUT = len(slots)
    for half in range(2):
        for i in range(2):
            row_slot(w_o, 4 * i, half * HALF)
    G_FFN = len(granules)
    for i in range(F_BLOCKS // 2):
        column_slot(w_g, 2 * P * i)
        column_slot(w_u, 2 * P * i)
    G_DOWN = len(granules)
    D_GRAN = F_BLOCKS // 2
    down = [(half, 2 * d) for half in range(2) for d in range(D_GRAN)]
    for i in range(0, 2 * D_GRAN, 2):
        slot([lambda st, j=j: whole(4)(st)[:, 2 * j:2 * j + 2, :] for j in range(2)],
             [(lambda st, j=j: whole(4)(st)[:, 2 * j:2 * j + 2, :],
               w_d[f * P:(f + 2) * P, half * HALF:(half + 1) * HALF]
               .rearrange("(k p) c -> p k c", p=P))
              for j, (half, f) in enumerate(down[i:i + 2])])
    N_GRAN = len(granules)

    ctx = ExitStack()
    with ctx:
        base = (nc.sbuf_base + 31) // 32 * 32

        def at(name, shape, dtype, offset):
            return nc.alloc_sbuf_tensor_at(name, shape, dtype, offset=base + offset)

        K = 1024
        A = 0
        x_nat = at("x_nat", [P, ROWS, D], F32, A)
        v_m = at("v_m", [P, ROWS, H_M, DH_M + 1], F32, A)
        v_f = at("v_f", [P, ROWS, W_F], F32, A + 8256)
        x1 = at("x1", [P, ROWS, D], F32, A)
        B = A + 16896
        hT_hi = at("hT_hi", [P, KD, SEQ], F32R, B)
        hT_lo = at("hT_lo", [P, KD, SEQ], F32R, B + 16 * K)
        C = B + 32 * K
        stage = [at(f"stage{i}", [P, 2 * GRAN], F32, C + 8 * K * i) for i in range(STAGES)]
        C += 8 * K * STAGES
        w_hi = [at(f"w_hi{i}", [P, GRAN], F32R, C + 8 * K * i) for i in range(RING)]
        w_lo = [at(f"w_lo{i}", [P, GRAN], F32R, C + 8 * K * i + 4 * K) for i in range(RING)]
        G = C + 8 * K * RING
        gain_a = at("gain_a", [P, D], F32, G)
        gain_b = at("gain_b", [P, D], F32, G + 4 * K)
        v_bias = at("v_bias", [P, 2, W_M], F32, G + 4 * K)
        W = G + 8 * K
        work = [at(f"work{i}", [P, SEQ], F32, W + 2 * K * i) for i in range(6)]
        square_out = at("square_out", [P, SEQ], F32, W + 8 * K)
        R = W + 12 * K
        q_m = at("q_m", [P, H_M, SEQ], F32, R)
        k_m = at("k_m", [P, H_M, SEQ], F32, R + 8 * K)
        q_f = at("q_f", [P, KB, SEQ], F32, R + 16 * K)
        k_f = at("k_f", [P, KB, SEQ], F32, R + 24 * K)
        o_gate = at("o_gate", [P, KB, SEQ], F32, R + 32 * K)
        ymT_hi = at("ymT_hi", [P, KB, SEQ], F32R, R + 40 * K)
        ymT_lo = at("ymT_lo", [P, KB, SEQ], F32R, R + 48 * K)
        yfT_hi = at("yfT_hi", [P, KB, SEQ], F32R, R + 56 * K)
        yfT_lo = at("yfT_lo", [P, KB, SEQ], F32R, R + 64 * K)
        xn = [at(f"xn{i}", [P, D], F32, R + 56 * K + 4 * K * i) for i in range(2)]
        z_pad = at("z_pad", [P, CONV_K - 1 + SEQ], F32, R + 64 * K)
        N_E = sum(SEQ - P * j for j in range(ROWS))
        decay = [at(f"decay{i}", [P, N_E], F32, R + 56 * K + 5 * K * i) for i in range(2)]
        rows_both = at("rows_both", [P, 10 * P], F32R, R + 72 * K)
        probs = [at(f"probs{i}", [P, SEQ], F32, R + 82 * K + 2 * K * i) for i in range(3)]
        mo_half_tanh = at("mo_half_tanh", [P, SEQ], F32, R + 86 * K)
        stab_masked = [at(f"stab_masked{i}", [P, SEQ], F32, R + 82 * K + 2 * K * i) for i in range(2)]
        vec_raw = at("vec_raw", [N_VEC, P], F32, R + 82 * K)
        upper = at("upper", [P, P], F32, R + 86 * K)
        ones = at("ones", [P, P], F32, R + 86 * K + 512)
        mixT_hi = at("mixT_hi", [P, KD, SEQ], F32R, R)
        mixT_lo = at("mixT_lo", [P, KD, SEQ], F32R, R + 16 * K)
        mix_sum = [at(f"mix_sum{i}", [P, SEQ], F32, R + 72 * K + 2 * K * i) for i in range(2)]
        xn2 = [at(f"xn2{i}", [P, D], F32, R + 40 * K + 4 * K * i) for i in range(2)]
        aT_hi = at("aT_hi", [P, F_BLOCKS, SEQ], F32R, R)
        aT_lo = at("aT_lo", [P, F_BLOCKS, SEQ], F32R, R + 44 * K)
        S = R + 88 * K
        small_at = [S]

        def small(name, shape, dtype=F32):
            n = int(np.prod(shape[1:])) * (2 if dtype == BF16 else 4)
            t = at(name, shape, dtype, small_at[0])
            small_at[0] += (n + 31) // 32 * 32
            assert base + small_at[0] <= nc.sbuf_usable_end, small_at[0]
            return t

        ident = small("ident", [P, P])
        ident_b = small("ident_b", [P, P], BF16)
        mask_b = small("mask_b", [P, P], BF16)
        mask_T = small("mask_T", [P, P], BF16)
        pick = small("pick", [P, LANES], F32R)
        vec = small("vec", [P, N_VEC])
        vec_half = small("vec_half", [P, N_VEC])
        gate_bias = small("gate_bias", [LANES + H_M, 1])
        square_sum = small("square_sum", [P, ROWS, 2])
        mean_sq = small("mean_sq", [P, ROWS])
        rstd = small("rstd", [P, ROWS])
        minus_half = small("minus_half", [P, ROWS])
        frame = small("frame", [P, ROWS * ROWS, LANES])
        before = small("before", [P, ROWS, H_M])
        m_stab = small("m_stab", [P, ROWS, H_M])
        m_floor = small("m_floor", [P, ROWS, H_M])
        den = small("den", [P, ROWS])
        head_ms = small("head_ms", [P, ROWS])
        head_rs = small("head_rs", [P, ROWS])
        neg_max = small("neg_max", [P, 4])
        row_sum = small("row_sum", [P, 4])
        row_inv = small("row_inv", [P, 4])
        gate_rows = work[5]
        abs_neg = work[4][:, 0:ROWS * LANES].rearrange("p (j l) -> p j l", l=LANES)
        gates = work[4][:, 128:192].rearrange("p (j l) -> p j l", l=LANES + H_M)
        log_f = work[4][:, 192:192 + ROWS * LANES].rearrange("p (j l) -> p j l", l=LANES)
        cum = work[4][:, 256:256 + ROWS * LANES].rearrange("p (j l) -> p j l", l=LANES)
        softp = work[4][:, 64:64 + ROWS * LANES].rearrange("p (j l) -> p j l", l=LANES)
        psum = [ctx.enter_context(nc.psum_tensor(f"bank{i}", [P, 512], F32)) for i in range(8)]

        def sem(name):
            return ctx.enter_context(nc.semaphore(name))

        x_in = [sem(f"x_in{r}") for r in range(ROWS)]
        gain1_in, vec_in, gbias_in, vbias_in = (sem(n) for n in ("gain1_in", "vec_in", "gbias_in", "vbias_in"))
        gain2_in, gain3_in, xagain_in = sem("gain2_in"), sem("gain3_in"), sem("xagain_in")
        stage_in = [sem(f"stage_in{i}") for i in range(STAGES)]
        hi_split, lo_split, used = sem("hi_split"), sem("lo_split"), sem("granule_used")
        consts = sem("consts")
        vec_T, vec_ready = sem("vec_T"), sem("vec_ready")
        norm = [{n: sem(f"{n}_{i}") for n in ("squared", "summed", "rstd_ready", "xn_ready", "xn_T",
                                              "hT_hi_ready", "hT_lo_ready")} for i in range(3)]
        z_padded, conv_tap, conv_tanh, qk_ready = (sem(n) for n in ("z_padded", "conv_tap", "conv_tanh", "qk_ready"))
        v_ready, v_ones = sem("v_ready"), sem("v_ones")
        fq_ready, fk_ready, mo_tanh, o_ready = (sem(n) for n in ("fq_ready", "fk_ready", "mo_tanh", "o_ready"))
        gate_rows_ready, gates_T, gates_ready = sem("gate_rows_ready"), sem("gates_T"), sem("gates_ready")
        gate_abs, gate_exp, gate_ln, log_f_ready = (sem(n) for n in ("gate_abs", "gate_exp", "gate_ln", "log_f_ready"))
        cum_done, frame_step, frame_T = sem("cum_done"), sem("frame_step"), sem("frame_T")
        rows_hi_ready, rows_lo_ready = sem("rows_hi_ready"), sem("rows_lo_ready")
        g_spread, g_max, m_step, floor_ready = (sem(n) for n in ("g_spread", "g_max", "m_step", "floor_ready"))
        m_spread, s_m, decay_exp, m_masked, weighted = (sem(n) for n in ("m_spread", "s_m", "decay_exp", "m_masked", "weighted"))
        num_m, den_step, h_m, h_squared, h_mean, h_rstd, y_m = (sem(n) for n in ("num_m", "den_step", "h_m", "h_squared", "h_mean", "h_rstd", "y_m"))
        y_mT, y_m32, ymT_hi_ready, ymT_lo_ready = (sem(n) for n in ("y_mT", "y_m32", "ymT_hi_ready", "ymT_lo_ready"))
        logits, fox_max, fox_exp, fox_norm, fox_T, fox_pv = (sem(n) for n in ("logits", "fox_max", "fox_exp", "fox_norm", "fox_T", "fox_pv"))
        fox_PT = [sem("fox_PT_even"), sem("fox_PT_odd")]
        yfT_hi_ready, yfT_lo_ready = sem("yfT_hi_ready"), sem("yfT_lo_ready")
        gate_tanh, mix_step, mix_hi_ready, mix_lo_ready = (sem(n) for n in ("gate_tanh", "mix_step", "mix_hi_ready", "mix_lo_ready"))
        row_out, x1_ready = sem("row_out"), sem("x1_ready")
        ffn_tanh, ffn_step, aT_hi_ready, aT_lo_ready = (sem(n) for n in ("ffn_tanh", "ffn_step", "aT_hi_ready", "aT_lo_ready"))
        row_down, x2_ready, stored = sem("row_down"), sem("x2_ready"), sem("stored")
        block = ctx.enter_context(nc.Block())

        def pair(i, j):
            return i * (i + 1) // 2 + j

        def decay_at(j):
            return sum(SEQ - P * n for n in range(j))

        def wait_stage(eng, g):
            s = granules[g][0]
            n = sum(len(slots[i][1]) for i in range(s % STAGES, s + 1, STAGES))
            eng.wait_ge(stage_in[s % STAGES], 16 * n)

        def staged(g):
            s, view = granules[g]
            return view(stage[s % STAGES][:, :])

        def ring(tiles, g):
            n = granules_shape(g)
            return tiles[g % RING][:, :].rearrange("p (k c) -> p k c", k=n)

        def granules_shape(g):
            rows = (G_MV <= g < G_FQK) or (G_OUT <= g < G_FFN) or g >= G_DOWN
            return 2 if rows else KD

        @block.sync
        def _(sp):
            for r in range(ROWS):
                sp.dma_start(x_nat[:, r, :], x_rows[r]).then_inc(x_in[r], 16)
                if r == 1:
                    sp.dma_start(gain_a[:, :], norm1_g.rearrange("(a n) -> a n", a=1).to_broadcast([P, D])).then_inc(gain1_in, 16)
            for s, (n_gran, loads) in enumerate(slots):
                if s == 12:
                    sp.wait_ge(v_ready, 2 * ROWS)
                    sp.dma_start(gain_b[:, :], norm2_g.rearrange("(a n) -> a n", a=1).to_broadcast([P, D])).then_inc(gain2_in, 16)
                    sp.wait_ge(norm[0]["xn_ready"], ROWS)
                    sp.dma_start(gain_a[:, :], norm_f_g.rearrange("(a n) -> a n", a=1).to_broadcast([P, D])).then_inc(gain3_in, 16)
                if s == S_OUT - 4:
                    sp.wait_ge(fox_pv, 32)
                    sp.wait_ge(num_m, 2 * H_M)
                    sp.dma_start(x1[:, :, :], x[0].rearrange("(r p) d -> p r d", p=P)).then_inc(xagain_in, 16)
                if s >= STAGES:
                    sp.wait_ge(lo_split, slots[s - STAGES][0])
                for view, src in loads:
                    sp.dma_start(view(stage[s % STAGES][:, :]), src).then_inc(stage_in[s % STAGES], 16)
            for r in range(ROWS):
                sp.wait_ge(norm[2]["xn_ready"], r + 1)
                sp.dma_start(out_rows[r], x1[:, r, :]).then_inc(stored, 16)
            sp.wait_ge(stored, 16 * ROWS)

        @block.gpsimd
        def _(pool):
            vec_loads = ((V_QK, b_in[C_QK:C_QK + 2 * W_M]), (V_MO, b_in[C_MO:C_MO + W_M]),
                         (V_FQK, b_in[C_FQK:C_FQK + 2 * W_F]), (V_GM, b_in[C_GM:C_GM + 2 * D]),
                         (V_CONVW, conv_w.rearrange("j c -> (j c)")), (V_CONVB, conv_b), (V_NORM, mlstm_norm_g))
            for row, src in vec_loads:
                n = src.shape[0] // P
                pool.dma_start(vec_raw[row:row + n, :], src.rearrange("(a n) -> a n", n=P)).then_inc(vec_in, 16)
            pool.dma_start(gate_bias[0:2 * H_M, :], b_in[C_MI:C_MI + 2 * H_M].rearrange("(n a) -> n a", a=1)).then_inc(gbias_in, 16)
            pool.dma_start(gate_bias[2 * H_M:2 * H_M + H_F, :], b_in[C_FF:C_FF + H_F].rearrange("(n a) -> n a", a=1)).then_inc(gbias_in, 16)
            for n, c in enumerate((C_MV, C_FV)):
                pool.dma_start(v_bias[:, n, :], b_in[c:c + W_M].rearrange("(a n) -> a n", a=1).to_broadcast([P, W_M])).then_inc(vbias_in, 16)
            steps = [0]

            def const(ins):
                ins.then_inc(consts, 1)
                steps[0] += 1

            const(pool.memset(ident[:, :], 0.0))
            const(pool.memset(ident_b[:, :], 0.0))
            const(pool.memset(mask_b[:, :], 0.0))
            const(pool.memset(mask_T[:, :], 0.0))
            const(pool.memset(pick[:, :].bitcast(F32), 0.0))
            const(pool.memset(rows_both[:, :].bitcast(F32), 0.0))
            const(pool.memset(upper[:, :], 1.0))
            const(pool.memset(ones[:, :], 1.0))
            const(pool.memset(minus_half[:, :], -0.5))
            const(pool.memset(z_pad[:, 0:CONV_K - 1], 0.0))
            pool.wait_ge(consts, steps[0])
            for t in (ident, ident_b):
                const(pool.affine_select(out=t[:, :], in_=t[:, :], compare_op=ALU.not_equal, fill=1.0, base=0,
                                         pattern=[[-1, P]], channel_multiplier=1))
            for at_row in (0, LO):
                const(pool.affine_select(out=pick[:, :], in_=pick[:, :].bitcast(F32), compare_op=ALU.not_equal,
                                         fill=1.0, base=-at_row, pattern=[[-1, LANES]], channel_multiplier=1))
                pool.wait_ge(consts, steps[0])
            const(pool.affine_select(out=mask_b[:, :], in_=mask_b[:, :], compare_op=ALU.is_ge, fill=NEG,
                                     base=0, pattern=[[-1, P]], channel_multiplier=1))
            const(pool.affine_select(out=mask_T[:, :], in_=mask_T[:, :], compare_op=ALU.is_ge, fill=-NEG,
                                     base=0, pattern=[[1, P]], channel_multiplier=-1))
            const(pool.affine_select(out=upper[:, :], in_=upper[:, :], compare_op=ALU.is_ge, fill=0.0,
                                     base=0, pattern=[[1, P]], channel_multiplier=-1))
            assert steps[0] == N_CONSTS

            def rows_rstd(i):
                for r in range(ROWS):
                    pool.wait_ge(norm[i]["summed"], 2 * (r + 1))
                    pool.tensor_tensor(rstd[:, r:r + 1], mean_sq[:, r:r + 1], minus_half[:, 0:1],
                                       ALU.pow).then_inc(norm[i]["rstd_ready"], 1)

            rows_rstd(0)
            pool.wait_ge(norm[0]["xn_ready"], ROWS)
            pool.memset(v_m[:, :, :, DH_M:DH_M + 1], 1.0).then_inc(v_ones, 1)
            for i in range(H_M + 1):
                if i >= 1:
                    h = i - 1
                    pool.wait_ge(h_mean, 2 * h + 2)
                    if h >= 1:
                        pool.wait_ge(y_m, h)
                    pool.tensor_tensor(head_rs[:, :], head_ms[:, :], minus_half[:, :],
                                       ALU.pow).then_inc(h_rstd, 1)
                if i < H_M:
                    h = i
                    pool.wait_ge(h_m, 2 * h + 2)
                    if h >= 1:
                        pool.wait_ge(h_mean, 2 * h)
                    pool.tensor_tensor(work[2][:, :], work[h % 2][:, :], work[h % 2][:, :],
                                       ALU.mult).then_inc(h_squared, 1)
            rows_rstd(1)
            rows_rstd(2)

        @block.scalar
        def _(act):
            def square(i, src, r, halves):
                for half in halves:
                    n = count_squares[i]
                    if n:
                        act.wait_ge(norm[i]["squared"], n)
                    act.activation(square_out[:, :], src[:, r, half * HALF:(half + 1) * HALF], ACT.Square,
                                   accum_out=square_sum[:, r, half:half + 1]).then_inc(norm[i]["squared"], 1)
                    count_squares[i] += 1

            count_squares = [0, 0, 0]

            def take_hT_hi(i, r):
                for half in range(2):
                    act.wait_ge(norm[i]["xn_T"], 2 * r + half + 1)
                    bank = norm_bank(i, r, half)
                    act.activation(hT_hi[:, 4 * half:4 * half + 4, r * P:(r + 1) * P],
                                   psum[bank][:, :].rearrange("p (k c) -> p k c", k=4),
                                   ACT.Copy).then_inc(norm[i]["hT_hi_ready"], 1)

            def split_hi(g):
                if g >= N_GRAN:
                    return
                wait_stage(act, g)
                if g >= RING:
                    act.wait_ge(used, g - RING + 1)
                act.activation(ring(w_hi, g), staged(g), ACT.Copy).then_inc(hi_split, 1)

            for r in range(2):
                act.wait_ge(x_in[r], 16)
                square(0, x_nat, r, (0, 1))
            take_hT_hi(0, 0)
            take_hT_hi(0, 1)
            split_hi(0)
            for r in range(2, ROWS):
                act.wait_ge(x_in[r], 16)
                square(0, x_nat, r, (0, 1))
                split_hi(r - 1)
            take_hT_hi(0, 2)
            take_hT_hi(0, 3)

            def conv_tanh_of(b):
                act.wait_ge(conv_tap, CONV_K * (b + 1))
                if b >= 2:
                    act.wait_ge(qk_ready, b - 1)
                act.activation(work[2 + b % 2][:, :], work[b % 2][:, :], ACT.Tanh, scale=0.5).then_inc(conv_tanh, 1)

            for g in range(G_MO):
                if g + AHEAD >= N_FIRST:
                    split_hi(g + AHEAD)
                if g in qk_block:
                    b = qk_block[g]
                    if b >= 1:
                        conv_tanh_of(b - 1)
                    act.wait_ge(used, g + 1)
                    if b == 0:
                        act.wait_ge(vec_ready, 1)
                        act.wait_ge(consts, N_CONSTS)
                        act.wait_ge(norm[0]["xn_T"], 2 * ROWS)
                    else:
                        act.wait_ge(conv_tap, CONV_K * b)
                    act.activation(z_pad[:, CONV_K - 1:], psum[qk_bank(b)][:, :], ACT.Identity,
                                   bias=vec[:, V_QK + b:V_QK + b + 1]).then_inc(z_padded, 1)
                if g == G_MV:
                    conv_tanh_of(7)
                if g == G_GATE + 1:
                    act.wait_ge(gate_abs, 1)
                    act.activation(softp, abs_neg, ACT.Exp).then_inc(gate_exp, 1)
                    act.wait_ge(gate_exp, 1)
                    act.activation(softp, softp, ACT.Ln, bias=1.0).then_inc(gate_ln, 1)
                if g == G_GATE + 5:
                    act.wait_ge(consts, N_CONSTS)
                    for n, (a, b) in enumerate(ROW_CHUNKS):
                        act.wait_ge(frame_T, n + 1)
                        act.activation(rows_both[0:LANES, a * P:b * P], psum[5 + n][0:LANES, 0:(b - a) * P],
                                       ACT.Copy).then_inc(rows_hi_ready, 1)
                if G_FQK + KB <= g < G_MO:
                    b = g - G_FQK - KB
                    act.wait_ge(used, g + 1)
                    act.activation(k_f[:, b, :], psum[fqk_bank(KB + b)][:, :], ACT.Identity,
                                   bias=vec[:, V_FQK + KB + b:V_FQK + KB + b + 1]).then_inc(fk_ready, 1)

            act.wait_ge(m_step, 2)
            act.activation(m_floor[:, :, :], m_floor[:, :, :], ACT.Exp, scale=-1.0).then_inc(floor_ready, 1)

            def take_ymT_hi(h):
                act.wait_ge(y_m32, h + 1)
                act.activation(ymT_hi[:, h, :], work[4 + h % 2][:, :], ACT.Copy).then_inc(ymT_hi_ready, 1)

            for h in range(H_M):
                act.wait_ge(m_spread, h + 1)
                act.wait_ge(m_masked, h + 1)
                if h >= 2:
                    act.wait_ge(num_m, 2 * (h - 1))
                for j in range(ROWS):
                    for q in range(j, ROWS):
                        o = decay_at(j) + (q - j) * P
                        m = stab_masked[h % 2] if q == j else psum[2]
                        act.activation(decay[h % 2][:, o:o + P], m[:, q * P:(q + 1) * P],
                                       ACT.Exp, scale=-1.0,
                                       bias=frame[:, ROWS * q + j, h:h + 1]).then_inc(decay_exp, 1)
                if h >= 3:
                    take_ymT_hi(h - 3)
                split_hi(G_MO + h + AHEAD)
                act.wait_ge(used, G_MO + h + 1)
                if h >= 1:
                    act.wait_ge(o_ready, h)
                act.activation(mo_half_tanh[:, :], psum[3][:, :], ACT.Tanh, scale=0.5,
                               bias=vec_half[:, V_MO + h:V_MO + h + 1]).then_inc(mo_tanh, 1)
            take_ymT_hi(1)

            def take_yfT_hi(hp):
                act.wait_ge(fox_pv, 8 * (hp + 1))
                act.activation(yfT_hi[:, hp, :], psum[hp % 2][:, :], ACT.Copy).then_inc(yfT_hi_ready, 1)

            def fox_softmax(u):
                _, q, _ = fox_unit(u)
                n = (q + 1) * P
                act.wait_ge(fox_max, u + 1)
                if u >= 3:
                    act.wait_ge(fox_T, u - 2)
                act.activation(probs[u % 3][:, 0:n], psum[4 + u % 3][:, 0:n], ACT.Exp,
                               bias=neg_max[:, u % 4:u % 4 + 1],
                               accum_out=row_sum[:, u % 4:u % 4 + 1]).then_inc(fox_exp, 1)

            def fox_take_odd(u):
                _, q, _ = fox_unit(u)
                n = (q + 1) * P
                act.wait_ge(fox_T, u + 1)
                if u >= 2:
                    act.wait_ge(fox_pv, u - 1)
                act.activation(work[1][:, 0:n], psum[3][:, 0:n], ACT.Copy).then_inc(fox_PT[1], 1)

            act.wait_ge(decay_exp, 10 * H_M)
            act.wait_ge(o_ready, H_M)
            for u in range(32 + 2):
                if u < 32:
                    fox_softmax(u)
                if u == 2:
                    take_ymT_hi(2)
                    act.wait_ge(y_m, H_M)
                if u == 4:
                    take_ymT_hi(3)
                if u >= 2 and u % 2:
                    fox_take_odd(u - 2)
                if u in (16, 20):
                    split_hi(G_BR + 2 + (u - 16) // 4)
                if u >= 8 and u % 8 == 4:
                    take_yfT_hi(u // 8 - 1)
            take_yfT_hi(KB - 1)

            for c in range(4):
                for n in range(6):
                    g = G_BR + 6 * c + n
                    if g >= G_BR + 2:
                        split_hi(g + AHEAD)
                    act.wait_ge(used, g + 1)
                    if n < 4:
                        if c >= 1:
                            act.wait_ge(mix_step, 3 * 2 * c - (1 if n % 2 else 4))
                        else:
                            act.wait_ge(ymT_lo_ready, H_M)
                        col = (V_GM, V_GF)[n // 2] + 2 * c + n % 2
                        act.activation(work[2 + n][:, :], psum[GATE_BANKS[n]][:, :], ACT.Tanh, scale=0.5,
                                       bias=vec_half[:, col:col + 1]).then_inc(gate_tanh, 1)
                    else:
                        b = 2 * c + n - 4
                        act.wait_ge(mix_step, 3 * b + 3)
                        act.activation(mixT_hi[:, b, :], mix_sum[b % 2][:, :], ACT.Copy, scale=0.5).then_inc(mix_hi_ready, 1)

            for n in range(6):
                split_hi(G_OUT + AHEAD + n)
            for r in range(ROWS):
                act.wait_ge(x1_ready, r + 1)
                square(1, x1, r, (0,))
            for r in range(ROWS):
                if r == ROWS - 1:
                    for n in range(2):
                        split_hi(G_FFN + n)
                act.wait_ge(x1_ready, ROWS + r + 1)
                square(1, x1, r, (1,))
                if r >= 1:
                    take_hT_hi(1, r - 1)
            split_hi(G_FFN + 2)
            take_hT_hi(1, ROWS - 1)

            for p in range(F_BLOCKS // 2):
                for n in range(4):
                    g = G_FFN + 4 * p + n
                    if g + AHEAD >= G_FFN + N_FIRST:
                        split_hi(g + AHEAD)
                    act.wait_ge(used, g + 1)
                    if n < 2:
                        f = 2 * p + n
                        if p >= 1:
                            act.wait_ge(ffn_step, 2 * (f - 2) + 1)
                        else:
                            act.wait_ge(mix_lo_ready, 8)
                        act.activation(work[n][:, :], psum[4 * (p % 2) + n][:, :], ACT.Tanh, scale=0.5).then_inc(ffn_tanh, 1)
                    else:
                        f = 2 * p + n - 2
                        act.wait_ge(ffn_step, 2 * f + 2)
                        act.activation(aT_hi[:, f, :], work[2 + n - 2][:, :], ACT.Copy).then_inc(aT_hi_ready, 1)

            for n in range(2 * D_GRAN - RING):
                split_hi(G_DOWN + n + AHEAD)
                if n == D_GRAN + 1:
                    for r in range(ROWS):
                        act.wait_ge(x2_ready, r + 1)
                        square(2, x1, r, (0,))
            for n in range(AHEAD):
                split_hi(N_GRAN - AHEAD + n)
            for r in range(ROWS):
                act.wait_ge(x2_ready, ROWS + r + 1)
                square(2, x1, r, (1,))

        @block.vector
        def _(dve):
            def mean_of_squares(i, r, n_squares):
                dve.wait_ge(norm[i]["squared"], n_squares)
                dve.tensor_tensor(mean_sq[:, r:r + 1], square_sum[:, r, 0:1], square_sum[:, r, 1:2],
                                  ALU.add).then_inc(norm[i]["summed"], 1)
                dve.wait_ge(norm[i]["summed"], 2 * r + 1)
                dve.tensor_scalar(mean_sq[:, r:r + 1], mean_sq[:, r:r + 1], 1.0 / D, EPS, ALU.mult,
                                  ALU.add).then_inc(norm[i]["summed"], 1)

            def normalise(i, src, r, gain, dst):
                dve.wait_ge(norm[i]["rstd_ready"], r + 1)
                dve.scalar_tensor_tensor(out=dst, in0=src[:, r, :], scalar=rstd[:, r:r + 1], in1=gain[:, :],
                                         op0=ALU.mult, op1=ALU.mult).then_inc(norm[i]["xn_ready"], 1)

            def take_hT_lo(i, r):
                for half in range(2):
                    dve.wait_ge(norm[i]["hT_hi_ready"], 2 * r + half + 1)
                    bank = norm_bank(i, r, half)
                    hT = (slice(None), slice(4 * half, 4 * half + 4), slice(r * P, (r + 1) * P))
                    dve.tensor_tensor(hT_lo[hT], psum[bank][:, :].rearrange("p (k c) -> p k c", k=4),
                                      hT_hi[hT].bitcast(F32), ALU.subtract).then_inc(norm[i]["hT_lo_ready"], 1)

            def split_lo(g):
                if g >= N_GRAN:
                    return
                dve.wait_ge(hi_split, g + 1)
                dve.tensor_tensor(ring(w_lo, g), staged(g), ring(w_hi, g).bitcast(F32),
                                  ALU.subtract).then_inc(lo_split, 1)

            def norm_rows(r):
                mean_of_squares(0, r, 2 * r + 2)
                if r >= 2:
                    dve.wait_ge(norm[0]["xn_T"], 2 * (r - 1))
                normalise(0, x_nat, r, gain_a, xn[r % 2][:, :])

            dve.wait_ge(gain1_in, 16)
            norm_rows(0)
            norm_rows(1)
            take_hT_lo(0, 0)
            take_hT_lo(0, 1)
            split_lo(0)
            norm_rows(2)
            split_lo(1)
            norm_rows(3)
            take_hT_lo(0, 2)
            split_lo(2)
            take_hT_lo(0, 3)
            dve.wait_ge(vec_T, 1)
            dve.tensor_copy(vec[:, :], psum[0][:, 0:N_VEC]).then_inc(vec_ready, 1)
            dve.tensor_scalar(vec_half[:, :], psum[0][:, 0:N_VEC], 0.5, None, ALU.mult).then_inc(vec_ready, 1)
            dve.wait_ge(vec_ready, 2)

            def qk_of(b):
                dve.wait_ge(conv_tanh, b + 1)
                dst = (q_m if b < KB else k_m)[:, b % KB, :]
                dve.scalar_tensor_tensor(out=dst, in0=work[2 + b % 2][:, :], scalar=1.0, in1=work[b % 2][:, :],
                                         op0=ALU.add, op1=ALU.mult).then_inc(qk_ready, 1)

            for g in range(G_MO):
                if g + AHEAD >= N_FIRST:
                    split_lo(g + AHEAD)
                if g == G_GATE:
                    dve.wait_ge(used, g + 1)
                    dve.wait_ge(gbias_in, 32)
                    dve.tensor_scalar(gate_rows[0:LANES + H_M, :], psum[1][0:LANES + H_M, :], gate_bias[:, 0:1], None,
                                      ALU.add).then_inc(gate_rows_ready, 1)
                if g in qk_block:
                    b = qk_block[g]
                    if b >= 1:
                        qk_of(b - 1)
                    dve.wait_ge(z_padded, b + 1)
                    if b >= 2:
                        dve.wait_ge(qk_ready, b - 1)
                    u = work[b % 2]
                    dve.tensor_scalar(u[:, :], z_pad[:, 0:SEQ], vec[:, V_CONVW + b:V_CONVW + b + 1],
                                      vec[:, V_CONVB + b:V_CONVB + b + 1], ALU.mult, ALU.add).then_inc(conv_tap, 1)
                    for j in range(1, CONV_K):
                        dve.wait_ge(conv_tap, CONV_K * b + j)
                        c = V_CONVW + 8 * j + b
                        dve.scalar_tensor_tensor(out=u[:, :], in0=z_pad[:, j:j + SEQ], scalar=vec[:, c:c + 1],
                                                 in1=u[:, :], op0=ALU.mult, op1=ALU.add).then_inc(conv_tap, 1)
                if g == G_MV:
                    qk_of(7)
                if g == G_GATE + 1:
                    dve.wait_ge(gates_T, 1)
                    dve.tensor_copy(gates[:, :, :], psum[4][:, 0:64].rearrange("p (j l) -> p j l", l=16)).then_inc(gates_ready, 1)
                    dve.wait_ge(gates_ready, 1)
                    lanes = gates[:, :, H_M:]
                    dve.tensor_scalar(abs_neg, lanes, -1.0, None, ALU.mult).then_inc(gates_ready, 1)
                    dve.wait_ge(gates_ready, 2)
                    dve.tensor_tensor(abs_neg, abs_neg, lanes, ALU.min).then_inc(gate_abs, 1)
                if g == G_GATE + 2:
                    dve.wait_ge(gate_ln, 1)
                    dve.scalar_tensor_tensor(out=log_f[:, :, :], in0=gates[:, :, H_M:], scalar=0.0, in1=softp,
                                             op0=ALU.min, op1=ALU.subtract).then_inc(log_f_ready, 1)
                if g == G_GATE + 3:
                    dve.wait_ge(cum_done, 1)
                    cums = psum[4][:, 64:64 + ROWS * LANES].rearrange("p (j l) -> p j l", l=LANES)
                    tots = psum[4][:, 128:128 + ROWS * LANES].rearrange("p (j l) -> p j l", l=LANES)
                    n = 0

                    def step(ins):
                        nonlocal n
                        ins.then_inc(frame_step, 1)
                        n += 1
                        dve.wait_ge(frame_step, n)

                    step(dve.tensor_copy(cum[:, :, :], cums))
                    step(dve.tensor_scalar(frame[:, 0::ROWS + 1, :], cum[:, :, :], -1.0, None, ALU.mult))
                    step(dve.tensor_tensor(frame[:, 0::ROWS + 1, 0:H_M], gates[:, :, 0:H_M],
                                           frame[:, 0::ROWS + 1, 0:H_M], ALU.add))
                    step(dve.memset(before[:, 0, :], 0.0))
                    for q in range(1, ROWS):
                        tot = tots[:, q - 1, :]
                        step(dve.tensor_tensor(frame[:, ROWS * q:ROWS * q + q, :],
                                               frame[:, ROWS * (q - 1):ROWS * (q - 1) + q, :],
                                               tots[:, q - 1:q, :].to_broadcast([P, q, LANES]), ALU.add))
                        step(dve.tensor_tensor(before[:, q, :], before[:, q - 1, :], tot[:, 0:H_M], ALU.add))
                    assert n == FRAME_STEPS
                if g == G_GATE + 5:
                    for n, (a, b) in enumerate(ROW_CHUNKS):
                        dve.wait_ge(rows_hi_ready, n + 1)
                        dve.tensor_tensor(rows_both[LO:LO + LANES, a * P:b * P], psum[5 + n][0:LANES, 0:(b - a) * P],
                                          rows_both[0:LANES, a * P:b * P].bitcast(F32), ALU.subtract).then_inc(rows_lo_ready, 1)
                if g in (G_FV - 1, G_FQK - 1):
                    n = (G_FV - 1, G_FQK - 1).index(g)
                    dve.wait_ge(used, g + 1)
                    dve.wait_ge(vbias_in, 32)
                    dve.wait_ge(norm[0]["xn_ready"], ROWS)
                    for r in range(ROWS):
                        if n == 0:
                            dve.tensor_tensor(v_m[:, r, :, 0:DH_M], psum[4 + r][:, :].rearrange("p (h d) -> p h d", h=H_M),
                                              v_bias[:, 0, :].rearrange("p (h d) -> p h d", h=H_M), ALU.add).then_inc(v_ready, 1)
                        else:
                            dve.tensor_tensor(v_f[:, r, :], psum[r][:, :], v_bias[:, 1, :], ALU.add).then_inc(v_ready, 1)
                if G_FQK <= g < G_FQK + KB:
                    b = g - G_FQK
                    dve.wait_ge(used, g + 1)
                    dve.tensor_scalar(q_f[:, b, :], psum[fqk_bank(b)][:, :], vec[:, V_FQK + b:V_FQK + b + 1],
                                      DH_F ** -0.5, ALU.add, ALU.mult).then_inc(fq_ready, 1)
                if G_FQK <= g < G_MO:
                    for u in (2 * (g - G_FQK), 2 * (g - G_FQK) + 1):
                        q, h = u // H_M, u % H_M
                        dve.wait_ge(g_spread, u + 1)
                        dve.reduce_max(m_stab[:, q, h:h + 1], psum[u % 2][:, 0:(q + 1) * P], AX.X).then_inc(g_max, 1)

            dve.wait_ge(g_max, 16)
            dve.tensor_tensor(m_stab[:, :, :], m_stab[:, :, :], before[:, :, :], ALU.max).then_inc(m_step, 1)
            dve.wait_ge(m_step, 1)
            dve.tensor_tensor(m_floor[:, :, :], m_stab[:, :, :], cum[:, :, 0:H_M], ALU.add).then_inc(m_step, 1)

            def take_ymT(h):
                dve.wait_ge(y_mT, h + 1)
                if h >= 2:
                    dve.wait_ge(ymT_lo_ready, h - 1)
                dve.tensor_tensor(work[4 + h % 2][:, :], psum[7][:, :], o_gate[:, h, :], ALU.mult).then_inc(y_m32, 1)
                dve.wait_ge(ymT_hi_ready, h + 1)
                dve.tensor_tensor(ymT_lo[:, h, :], work[4 + h % 2][:, :], ymT_hi[:, h, :].bitcast(F32),
                                  ALU.subtract).then_inc(ymT_lo_ready, 1)

            QK_SCALE = 0.25 * DH_M ** -0.5
            def mask_stabiliser(h):
                dve.wait_ge(m_spread, h + 1)
                if h >= 2:
                    dve.wait_ge(decay_exp, 10 * (h - 1))
                dve.tensor_tensor(stab_masked[h % 2][:, :].rearrange("p (q t) -> p q t", q=ROWS),
                                  psum[2][:, :].rearrange("p (q t) -> p q t", q=ROWS),
                                  mask_T[:, :].rearrange("p (a t) -> p a t", a=1).to_broadcast([P, ROWS, P]),
                                  ALU.add).then_inc(m_masked, 1)

            def head_mean_square(h):
                dve.wait_ge(h_squared, h + 1)
                if h >= 1:
                    dve.wait_ge(h_rstd, h)
                dve.reduce_sum(head_ms[:, :], work[2][:, :].rearrange("p (q d) -> p q d", q=ROWS), AX.X).then_inc(h_mean, 1)
                dve.wait_ge(h_mean, 2 * h + 1)
                dve.tensor_scalar(head_ms[:, :], head_ms[:, :], 1.0 / DH_M, EPS, ALU.mult, ALU.add).then_inc(h_mean, 1)

            def weigh_scores(h):
                for j in range(ROWS):
                    o, n = decay_at(j), SEQ - j * P
                    c = (0, 0, 0, 256)[j]
                    dve.wait_ge(s_m, 4 * h + (1, 2, 4, 4)[j])
                    dve.wait_ge(decay_exp, 10 * h + sum(ROWS - m for m in range(j + 1)))
                    dve.scalar_tensor_tensor(out=decay[h % 2][:, o:o + n], in0=psum[4 + min(j, 2)][:, c:c + n],
                                             scalar=QK_SCALE, in1=decay[h % 2][:, o:o + n], op0=ALU.mult,
                                             op1=ALU.mult).then_inc(weighted, 1)

            def pair_tile(n):
                return psum[n][:, 0:2 * (DH_M + 1)].rearrange("p (q d) -> p q d", q=2)

            def head_output(h):
                if h == 0:
                    dve.wait_ge(floor_ready, 1)
                else:
                    dve.wait_ge(h_m, 2 * h)
                for n in range(2):
                    dve.wait_ge(num_m, 2 * h + n + 1)
                    dve.scalar_tensor_tensor(out=den[:, 2 * n:2 * n + 2], in0=pair_tile(n)[:, :, DH_M], scalar=-1.0,
                                             in1=m_floor[:, 2 * n:2 * n + 2, h], op0=ALU.mult,
                                             op1=ALU.max).then_inc(den_step, 1)
                for n in range(2):
                    dve.wait_ge(den_step, 5 * h + n + 1)
                    dve.tensor_tensor(den[:, 2 * n:2 * n + 2], pair_tile(n)[:, :, DH_M], den[:, 2 * n:2 * n + 2],
                                      ALU.max).then_inc(den_step, 1)
                dve.wait_ge(den_step, 5 * h + 4)
                dve.reciprocal(den[:, :], den[:, :]).then_inc(den_step, 1)
                dve.wait_ge(den_step, 5 * h + 5)
                if h >= 2:
                    dve.wait_ge(y_m, h - 1)
                for n in range(2):
                    dve.tensor_tensor(work[h % 2][:, 256 * n:256 * n + 256].rearrange("p (q d) -> p q d", q=2),
                                      pair_tile(n)[:, :, 0:DH_M],
                                      den[:, 2 * n:2 * n + 2].rearrange("p (q a) -> p q a", a=1).to_broadcast([P, 2, DH_M]),
                                      ALU.mult).then_inc(h_m, 1)

            def head_normalise(h):
                dve.wait_ge(h_rstd, h + 1)
                if h >= 1:
                    dve.wait_ge(y_mT, h)
                dve.tensor_tensor(work[3][:, :].rearrange("p (q d) -> p q d", q=ROWS),
                                  work[h % 2][:, :].rearrange("p (q d) -> p q d", q=ROWS),
                                  head_rs[:, :].rearrange("p (q a) -> p q a", a=1).to_broadcast([P, ROWS, DH_M]),
                                  ALU.mult).then_inc(y_m, 1)

            QK_SCALE = 0.25 * DH_M ** -0.5
            for h in range(H_M):
                mask_stabiliser(h)
                if h >= 2:
                    head_mean_square(h - 2)
                weigh_scores(h)
                if h >= 2:
                    head_normalise(h - 2)
                if h >= 1:
                    head_output(h - 1)
                if h >= 3:
                    take_ymT(h - 3)
                split_lo(G_MO + h + AHEAD)
                dve.wait_ge(mo_tanh, h + 1)
                dve.tensor_scalar(o_gate[:, h, :], mo_half_tanh[:, :], 1.0,
                                  vec_half[:, V_NORM + h:V_NORM + h + 1], ALU.add, ALU.mult).then_inc(o_ready, 1)
            dve.wait_ge(o_ready, H_M)
            head_mean_square(2)
            head_output(3)
            head_normalise(2)
            take_ymT(1)

            def take_yfT_lo(hp):
                dve.wait_ge(yfT_hi_ready, hp + 1)
                dve.tensor_tensor(yfT_lo[:, hp, :], psum[hp % 2][:, :], yfT_hi[:, hp, :].bitcast(F32),
                                  ALU.subtract).then_inc(yfT_lo_ready, 1)

            def fox_row_max(u):
                _, q, _ = fox_unit(u)
                dve.wait_ge(logits, u + 1)
                if u >= 4:
                    dve.wait_ge(fox_exp, u - 3)
                dve.tensor_reduce(neg_max[:, u % 4:u % 4 + 1], psum[4 + u % 3][:, 0:(q + 1) * P], AX.X, ALU.max,
                                  negate=True).then_inc(fox_max, 1)

            def fox_divide(u):
                _, q, _ = fox_unit(u)
                n = (q + 1) * P
                dve.wait_ge(fox_exp, u + 1)
                if u >= 1:
                    dve.wait_ge(fox_norm, 2 * u)
                dve.reciprocal(row_inv[:, 0:1], row_sum[:, u % 4:u % 4 + 1]).then_inc(fox_norm, 1)
                dve.wait_ge(fox_norm, 2 * u + 1)
                dve.tensor_scalar(probs[u % 3][:, 0:n], probs[u % 3][:, 0:n], row_inv[:, 0:1], None,
                                  ALU.mult).then_inc(fox_norm, 1)

            def fox_take_even(u):
                _, q, _ = fox_unit(u)
                n = (q + 1) * P
                dve.wait_ge(fox_T, u + 1)
                if u >= 2:
                    dve.wait_ge(fox_pv, u - 1)
                dve.tensor_copy(work[0][:, 0:n], psum[2][:, 0:n]).then_inc(fox_PT[0], 1)

            for u in range(32 + 2):
                if u < 32:
                    fox_row_max(u)
                if 1 <= u < 33:
                    fox_divide(u - 1)
                if u == 0:
                    head_mean_square(3)
                if u == 1:
                    head_normalise(3)
                if u == 2:
                    take_ymT(2)
                if u == 4:
                    take_ymT(3)
                if u >= 2 and u % 2 == 0:
                    fox_take_even(u - 2)
                if u in (16, 20):
                    split_lo(G_BR + 2 + (u - 16) // 4)
                if u >= 8 and u % 8 == 4:
                    take_yfT_lo(u // 8 - 1)
            take_yfT_lo(KB - 1)

            for c in range(4):
                for n in range(6):
                    if c or n >= 2:
                        split_lo(G_BR + 6 * c + n + AHEAD)
                    if n >= 4:
                        j, b = n - 4, 2 * c + n - 4
                        dve.wait_ge(used, G_BR + 6 * c + n + 1)
                        dve.wait_ge(gate_tanh, 4 * c + 4)
                        if b >= 2:
                            dve.wait_ge(mix_lo_ready, b - 1)
                        if b >= 1:
                            dve.wait_ge(mix_step, 3 * b)
                        if b == 0:
                            dve.wait_ge(fox_pv, 32)
                        s = mix_sum[b % 2]
                        dve.scalar_tensor_tensor(out=s[:, :], in0=work[2 + j][:, :], scalar=1.0, in1=psum[2 * j][:, :],
                                                 op0=ALU.add, op1=ALU.mult).then_inc(mix_step, 1)
                        dve.scalar_tensor_tensor(out=work[0][:, :], in0=work[4 + j][:, :], scalar=1.0, in1=psum[2 * j + 1][:, :],
                                                 op0=ALU.add, op1=ALU.mult).then_inc(mix_step, 1)
                        dve.wait_ge(mix_step, 3 * b + 2)
                        dve.tensor_tensor(s[:, :], s[:, :], work[0][:, :], ALU.add).then_inc(mix_step, 1)
                        dve.wait_ge(mix_hi_ready, b + 1)
                        dve.scalar_tensor_tensor(out=mixT_lo[:, b, :], in0=s[:, :], scalar=0.5,
                                                 in1=mixT_hi[:, b, :].bitcast(F32), op0=ALU.mult,
                                                 op1=ALU.subtract).then_inc(mix_lo_ready, 1)

            for n in range(6):
                if n == 4:
                    dve.wait_ge(used, G_OUT + 4)
                    dve.wait_ge(xagain_in, 16)
                split_lo(G_OUT + AHEAD + n)
            for r in range(ROWS):
                dve.tensor_tensor(x1[:, r, 0:HALF], x1[:, r, 0:HALF], psum[4 + r][:, :], ALU.add).then_inc(x1_ready, 1)
            dve.wait_ge(gain2_in, 16)
            for r in range(ROWS):
                if r == ROWS - 1:
                    for n in range(2):
                        split_lo(G_FFN + n)
                    dve.wait_ge(used, G_OUT + 8)
                else:
                    dve.wait_ge(row_out, r + 1)
                dve.tensor_tensor(x1[:, r, HALF:D], x1[:, r, HALF:D], psum[r][:, :], ALU.add).then_inc(x1_ready, 1)
                mean_of_squares(1, r, ROWS + r + 1)
                if r == ROWS - 1:
                    take_hT_lo(1, r - 1)
                if r >= 2:
                    dve.wait_ge(norm[1]["xn_T"], 2 * (r - 1))
                normalise(1, x1, r, gain_b, xn2[r % 2][:, :])
                if 1 <= r < ROWS - 1:
                    take_hT_lo(1, r - 1)
            split_lo(G_FFN + 2)
            take_hT_lo(1, ROWS - 1)

            for p in range(F_BLOCKS // 2):
                for n in range(4):
                    g = G_FFN + 4 * p + n
                    if g + AHEAD >= G_FFN + N_FIRST:
                        split_lo(g + AHEAD)
                    if n >= 2:
                        j, f = n - 2, 2 * p + n - 2
                        y = work[2 + j]
                        dve.wait_ge(used, g + 1)
                        dve.wait_ge(ffn_tanh, f + 1)
                        if f >= 2:
                            dve.wait_ge(aT_lo_ready, f - 1)
                        dve.scalar_tensor_tensor(out=y[:, :], in0=work[j][:, :], scalar=1.0,
                                                 in1=psum[4 * (p % 2) + j][:, :], op0=ALU.add,
                                                 op1=ALU.mult).then_inc(ffn_step, 1)
                        dve.wait_ge(ffn_step, 2 * f + 1)
                        dve.scalar_tensor_tensor(out=y[:, :], in0=y[:, :], scalar=0.5,
                                                 in1=psum[4 * (p % 2) + n][:, :], op0=ALU.mult,
                                                 op1=ALU.mult).then_inc(ffn_step, 1)
                        dve.wait_ge(aT_hi_ready, f + 1)
                        dve.tensor_tensor(aT_lo[:, f, :], y[:, :], aT_hi[:, f, :].bitcast(F32),
                                          ALU.subtract).then_inc(aT_lo_ready, 1)

            for n in range(2 * D_GRAN - RING):
                split_lo(G_DOWN + n + AHEAD)
                if n == D_GRAN - 1:
                    dve.wait_ge(used, G_DOWN + D_GRAN)
                    dve.wait_ge(norm[1]["xn_ready"], ROWS)
                    for r in range(ROWS):
                        dve.tensor_tensor(x1[:, r, 0:HALF], x1[:, r, 0:HALF], psum[4 + r][:, :], ALU.add).then_inc(x2_ready, 1)
            for n in range(AHEAD):
                split_lo(N_GRAN - AHEAD + n)
            dve.wait_ge(gain3_in, 16)
            for r in range(ROWS):
                if r < ROWS - 1:
                    dve.wait_ge(row_down, r + 1)
                else:
                    dve.wait_ge(used, N_GRAN)
                dve.tensor_tensor(x1[:, r, HALF:D], x1[:, r, HALF:D], psum[r][:, :], ALU.add).then_inc(x2_ready, 1)
                mean_of_squares(2, r, ROWS + r + 1)
                normalise(2, x1, r, gain_a, x1[:, r, :])

        @block.tensor
        def _(pe):
            freed = {}

            def take(bank, by):
                if bank in freed:
                    pe.wait_ge(*freed[bank])
                freed[bank] = by

            def three(o, a_hi, a_lo, b_hi, b_lo, first, last):
                pe.matmul(o, a_hi, b_hi, start=first, stop=False)
                pe.matmul(o, a_hi, b_lo, start=False, stop=False)
                return pe.matmul(o, a_lo, b_hi, start=False, stop=last)

            def transpose_rows(i, tiles):
                def one(r):
                    pe.wait_ge(norm[i]["xn_ready"], r + 1)
                    for half in range(2):
                        bank = norm_bank(i, r, half)
                        take(bank, (norm[i]["hT_lo_ready"], 2 * r + half + 1))
                        for k in range(4):
                            c = (4 * half + k) * P
                            last = pe.transpose(psum[bank][:, k * P:(k + 1) * P], tiles[r % 2][:, c:c + P], ident[:, :])
                        last.then_inc(norm[i]["xn_T"], 1)
                return one

            def columns(g, bank, by, src_hi, src_lo, k0=0, n=KD, last_of_granule=True, times=slice(0, SEQ)):
                if times.start == 0:
                    take(bank, by)
                wh, wl = ring(w_hi, g), ring(w_lo, g)
                for k in range(n):
                    last = three(psum[bank][:, times], wh[:, k0 + k, :], wl[:, k0 + k, :], src_hi[:, k, times],
                                 src_lo[:, k, times], k == 0, k == n - 1)
                if last_of_granule:
                    last.then_inc(used, 1)

            def z_columns(g, bank, by):
                pe.wait_ge(lo_split, g + 1)
                columns(g, bank, by, hT_hi, hT_lo)

            def z_first_rows(i, g, bank, by):
                pe.wait_ge(lo_split, g + 1)
                pe.wait_ge(norm[i]["hT_lo_ready"], 4)
                columns(g, bank, by, hT_hi, hT_lo, last_of_granule=False, times=slice(0, SEQ // 2))

            def z_last_rows(i, g, bank):
                pe.wait_ge(norm[i]["hT_lo_ready"], 2 * ROWS)
                columns(g, bank, None, hT_hi, hT_lo, times=slice(SEQ // 2, SEQ))

            def row_product(g, bank, r, src_hi, src_lo, k0, first, last):
                wh, wl = ring(w_hi, g), ring(w_lo, g)
                rows = slice(r * P, (r + 1) * P)
                for k in range(2):
                    ins = three(psum[bank][:, :], src_hi[:, k0 + k, rows], src_lo[:, k0 + k, rows], wh[:, k, :], wl[:, k, :],
                                first and k == 0, last and k == 1)
                return ins

            pe.wait_ge(consts, N_CONSTS)
            one = transpose_rows(0, xn)
            one(0)
            one(1)
            first = [(0, qk_bank(0), (z_padded, 1)), (1, qk_bank(1), (z_padded, 2)), (G_GATE, 1, (gate_rows_ready, 1))]
            for n, (g, bank, by) in enumerate(first):
                z_first_rows(0, g, bank, by)
                if n < 2:
                    one(2 + n)
            for g, bank, _ in first:
                z_last_rows(0, g, bank)
            pe.wait_ge(vec_in, 16 * 7)
            take(0, (vec_ready, 2))
            pe.transpose(psum[0][:, 0:N_VEC], vec_raw[:, :], ident[0:N_VEC, 0:N_VEC]).then_inc(vec_T, 1)

            for g, b in qk_block.items():
                if g < G_GATE:
                    continue
                z_columns(g, qk_bank(b), (z_padded, b + 1))
                b -= 2
                if b == 0:
                    pe.wait_ge(gate_rows_ready, 1)
                    take(4, (frame_step, FRAME_STEPS))
                    for j in range(ROWS):
                        last = pe.transpose(psum[4][:, 16 * j:16 * j + 16], gate_rows[0:16, j * P:(j + 1) * P], ident[0:16, 0:16])
                    last.then_inc(gates_T, 1)
                if b == 2:
                    pe.wait_ge(log_f_ready, 1)
                    lf = log_f[:, :, :].rearrange("p j l -> p (j l)")
                    pe.matmul(psum[4][:, 64:64 + ROWS * LANES], upper[:, :], lf, start=True, stop=True)
                    pe.matmul(psum[4][:, 128:128 + ROWS * LANES], ones[:, :], lf, start=True, stop=True).then_inc(cum_done, 1)
                if b == 4:
                    pe.wait_ge(frame_step, FRAME_STEPS)
                    for n, (a, z) in enumerate(ROW_CHUNKS):
                        take(5 + n, (rows_lo_ready, n + 1))
                        for m in range(a, z):
                            q = next(i for i in range(ROWS) if pair(i, i) >= m)
                            last = pe.transpose(psum[5 + n][0:LANES, (m - a) * P:(m - a + 1) * P],
                                                frame[:, ROWS * q + m - pair(q, 0), :], ident[:, :])
                        last.then_inc(frame_T, 1)

            for n, (g0, bank0) in enumerate(((G_MV, 4), (G_FV, 0))):
                for r in range(ROWS):
                    take(bank0 + r, (v_ready, ROWS * n + r + 1))
                for d in range(4):
                    pe.wait_ge(lo_split, g0 + d + 1)
                    for r in range(ROWS):
                        last = row_product(g0 + d, bank0 + r, r, hT_hi, hT_lo, 2 * d, d == 0, d == 3)
                    last.then_inc(used, 1)

            def spread_row(bank, lane, q, first, last):
                n = (q + 1) * P
                cols = slice(pair(q, 0) * P, pair(q, 0) * P + n)
                both = pick[:, lane:lane + 1].to_broadcast([P, P])
                pe.matmul(psum[bank][:, 0:n], both, rows_both[:, cols], start=first, stop=False)
                return pe.matmul(psum[bank][:, q * P:n], ident_b[:, :], mask_b[:, :], start=False, stop=last)

            for b in range(8):
                z_columns(G_FQK + b, fqk_bank(b), (fq_ready, b + 1) if b < KB else (fk_ready, b - KB + 1))
                if b == 0:
                    pe.wait_ge(rows_lo_ready, 3)
                for u in (2 * b, 2 * b + 1):
                    q, h = u // H_M, u % H_M
                    take(u % 2, (g_max, u + 1))
                    spread_row(u % 2, h, q, True, True).then_inc(g_spread, 1)

            def mlstm_scores(h):
                if h == 0:
                    pe.wait_ge(m_step, 2)
                    pe.wait_ge(qk_ready, 8)
                take(2, (decay_exp, 10 * (h + 1)))
                for q in range(ROWS):
                    last = pe.matmul(psum[2][:, q * P:(q + 1) * P],
                                     m_stab[:, q, h:h + 1].to_broadcast([P, P]), ident[:, :], start=True, stop=True)
                last.then_inc(m_spread, 1)
                for j in range(ROWS):
                    o = (0, 0, 0, 256)[j]
                    if j < 3:
                        take(4 + j, (weighted, 4 * h + (j + 1 if j < 2 else 4)))
                    pe.matmul(psum[4 + min(j, 2)][:, o:o + SEQ - j * P], k_m[:, h, j * P:(j + 1) * P],
                              q_m[:, h, j * P:SEQ], start=True, stop=True).then_inc(s_m, 1)

            def mlstm_values(h):
                if h == 0:
                    pe.wait_ge(v_ready, ROWS)
                    pe.wait_ge(v_ones, 1)
                for q in range(ROWS):
                    if q % 2 == 0:
                        take(q // 2, (h_m, 2 * h + q // 2 + 1))
                    pe.wait_ge(weighted, 4 * h + q + 1)
                    for j in range(q + 1):
                        o = decay_at(j) + (q - j) * P
                        last = pe.matmul(psum[q // 2][:, (q % 2) * (DH_M + 1):(q % 2 + 1) * (DH_M + 1)],
                                         decay[h % 2][:, o:o + P], v_m[:, j, h, :], start=(j == 0), stop=(j == q))
                    if q % 2:
                        last.then_inc(num_m, 1)

            def mlstm_transpose(h):
                pe.wait_ge(y_m, h + 1)
                take(7, (y_m32, h + 1))
                for q in range(ROWS):
                    last = pe.transpose(psum[7][:, q * P:(q + 1) * P], work[3][:, q * P:(q + 1) * P], ident[:, :])
                last.then_inc(y_mT, 1)

            def fox_logits(u):
                hp, q, h2 = fox_unit(u)
                if u == 0:
                    pe.wait_ge(fq_ready, KB)
                    pe.wait_ge(fk_ready, KB)
                bank, n = 4 + u % 3, (q + 1) * P
                head = slice(h2 * DH_F, (h2 + 1) * DH_F)
                take(bank, (fox_exp, u + 1))
                pe.matmul(psum[bank][:, 0:n], q_f[head, hp, q * P:(q + 1) * P], k_f[head, hp, 0:n], start=True, stop=False)
                spread_row(bank, H_M + 2 * hp + h2, q, False, True).then_inc(logits, 1)

            def fox_transpose(u):
                _, q, _ = fox_unit(u)
                pe.wait_ge(fox_norm, 2 * u + 2)
                take(2 + u % 2, (fox_PT[u % 2], u // 2 + 1))
                for j in range(q + 1):
                    last = pe.transpose(psum[2 + u % 2][:, j * P:(j + 1) * P], probs[u % 3][:, j * P:(j + 1) * P], ident[:, :])
                last.then_inc(fox_T, 1)

            def fox_values(u):
                hp, q, h2 = fox_unit(u)
                if u == 0:
                    pe.wait_ge(v_ready, 2 * ROWS)
                pe.wait_ge(fox_PT[u % 2], u // 2 + 1)
                if u % 8 == 0:
                    take(hp % 2, (yfT_lo_ready, hp + 1))
                c = (2 * hp + h2) * DH_F
                for j in range(q + 1):
                    last = pe.matmul(psum[hp % 2][h2 * DH_F:(h2 + 1) * DH_F, q * P:(q + 1) * P],
                                     v_f[:, j, c:c + DH_F], work[u % 2][:, j * P:(j + 1) * P],
                                     start=(j == 0), stop=(j == q))
                last.then_inc(fox_pv, 1)

            def mo_columns(b):
                z_columns(G_MO + b, 3, (mo_tanh, b + 1))

            for h in range(H_M):
                mlstm_scores(h)
                if h >= 1:
                    mlstm_values(h - 1)
                if h >= 2:
                    mlstm_transpose(h - 2)
                mo_columns(h)
            mlstm_values(3)
            fox_logits(0)
            mlstm_transpose(2)
            fox_logits(1)
            for u in range(2, 35):
                if u < 32:
                    fox_logits(u)
                if u == 2:
                    mlstm_transpose(3)
                if u < 34:
                    fox_transpose(u - 2)
                if u == 32:
                    z_columns(G_BR, GATE_BANKS[0], (gate_tanh, 1))
                if u == 33:
                    z_columns(G_BR + 1, GATE_BANKS[1], (gate_tanh, 2))
                if u >= 3:
                    fox_values(u - 3)

            for c in range(4):
                for n in range(4):
                    if c or n >= 2:
                        z_columns(G_BR + 6 * c + n, GATE_BANKS[n], (gate_tanh, 4 * c + n + 1))
                if c == 0:
                    pe.wait_ge(ymT_lo_ready, H_M)
                    pe.wait_ge(yfT_lo_ready, KB)
                for j in range(2):
                    g, b = G_BR + 6 * c + 4 + j, 2 * c + j
                    pe.wait_ge(lo_split, g + 1)
                    columns(g, 2 * j, (mix_step, 3 * b + 1), ymT_hi, ymT_lo, 0, KB, False)
                    columns(g, 2 * j + 1, (mix_step, 3 * b + 2), yfT_hi, yfT_lo, KB, KB)

            for r in range(ROWS):
                take(4 + r, (x1_ready, r + 1))
            for d in range(4):
                pe.wait_ge(lo_split, G_OUT + d + 1)
                pe.wait_ge(mix_lo_ready, 2 * d + 2)
                for r in range(ROWS):
                    last = row_product(G_OUT + d, 4 + r, r, mixT_hi, mixT_lo, 2 * d, d == 0, d == 3)
                last.then_inc(used, 1)
            one = transpose_rows(1, xn2)
            for r in range(ROWS):
                take(r, (x1_ready, ROWS + r + 1))
                for d in range(4):
                    if r == 0:
                        pe.wait_ge(lo_split, G_OUT + 4 + d + 1)
                    last = row_product(G_OUT + 4 + d, r, r, mixT_hi, mixT_lo, 2 * d, d == 0, d == 3)
                    if r == ROWS - 1:
                        last.then_inc(used, 1)
                if r < ROWS - 1:
                    last.then_inc(row_out, 1)
                if r >= 1:
                    one(r - 1)

            def ffn_bank(n):
                p, i = n // 4, n % 4
                return 4 * (p % 2) + i, (ffn_step, 2 * (2 * p + i % 2) + 1 + i // 2)

            for n in range(N_FIRST):
                z_first_rows(1, G_FFN + n, *ffn_bank(n))
                if n == 1:
                    one(ROWS - 1)
            for n in range(N_FIRST):
                z_last_rows(1, G_FFN + n, ffn_bank(n)[0])
            for n in range(N_FIRST, G_DOWN - G_FFN):
                z_columns(G_FFN + n, *ffn_bank(n))

            for half in range(2):
                bank0 = 4 - 4 * half
                for r in range(ROWS):
                    take(bank0 + r, (x2_ready, ROWS * half + r + 1))
                n_shared = D_GRAN - half * RING
                for d in range(n_shared):
                    g = G_DOWN + half * D_GRAN + d
                    pe.wait_ge(lo_split, g + 1)
                    pe.wait_ge(aT_lo_ready, 2 * d + 2)
                    for r in range(ROWS):
                        last = row_product(g, bank0 + r, r, aT_hi, aT_lo, 2 * d, d == 0, d == D_GRAN - 1)
                    last.then_inc(used, 1)
            for r in range(ROWS):
                for d in range(D_GRAN - RING, D_GRAN):
                    g = G_DOWN + D_GRAN + d
                    if r == 0:
                        pe.wait_ge(lo_split, g + 1)
                    last = row_product(g, r, r, aT_hi, aT_lo, 2 * d, False, d == D_GRAN - 1)
                    if r == ROWS - 1:
                        last.then_inc(used, 1)
                if r < ROWS - 1:
                    last.then_inc(row_down, 1)


LO = 32
N_CONSTS = 17
FRAME_STEPS = 10
ROW_CHUNKS = ((0, 4), (4, 8), (8, 10))
N_FIRST = 3
GATE_BANKS = (6, 4, 5, 7)


def norm_bank(i, r, half):
    return 2 * r + half if i == 0 else 4 + (2 * r + half) % 4


def qk_bank(b):
    return (2 + b) % 4


def fqk_bank(b):
    return 4 + b % 4


def fox_unit(u):
    return u // 8, (0, 3, 1, 2)[u % 8 // 2], u % 2


_INS = ["x", "norm1_g", "w_in", "b_in", "conv_w", "conv_b", "mlstm_norm_g", "w_br_mlstm", "w_br_fox",
        "w_out", "norm2_g", "w_gate", "w_up", "w_down", "norm_f_g"]


def kernel(**inputs):
    import concourse.bacc as bacc
    from concourse.bass_utils import run_bass_kernel_spmd

    nc = bacc.Bacc("TRN2", target_bir_lowering=False, num_devices=1)
    arrays, args = {}, []
    for name in _INS:
        a = np.ascontiguousarray(inputs[name])
        arrays[f"in_{name}"] = a
        args.append(nc.dram_tensor(f"in_{name}", a.shape, mybir.dt.from_np(a.dtype), kind="ExternalInput").ap())
    out = nc.dram_tensor("out_block", (1, SEQ, D), F32, kind="ExternalOutput").ap()
    block_kernel(nc, *args, out)
    r = run_bass_kernel_spmd(nc, [arrays], core_ids=[0])
    return r.results[0]["out_block"]
```

```python
import numpy as np
import concourse.bass as bass
from concourse import mybir
from contextlib import ExitStack

F32 = mybir.dt.float32
F32R = mybir.dt.float32r
BF16 = mybir.dt.bfloat16
ACT = mybir.ActivationFunctionType
ALU = mybir.AluOpType
AX = mybir.AxisListType

P = 128
D = 1024
SEQ = 512
ROWS = SEQ // P
KD = D // P
HALF = D // 2
H_M, H_F = 4, 8
W_M = W_F = D // 2
DH_M, DH_F = W_M // H_M, W_F // H_F
KB = W_M // P
CONV_K = 4
D_FF = 2816
F_BLOCKS = D_FF // P
EPS = 1e-6
LANES = H_M + H_F
NEG = -1.0e30

C_QK = 0
C_MV = 2 * W_M
C_MO = 3 * W_M
C_MI = 4 * W_M
C_FQK = C_MI + 2 * H_M
C_FV = C_FQK + 2 * W_F
C_FF = C_FV + W_F
C_GM = C_FF + H_F
C_GF = C_GM + D

V_QK, V_MO, V_FQK, V_GM, V_GF = 0, 8, 12, 20, 28
V_CONVW, V_CONVB, V_NORM, N_VEC = 36, 68, 76, 80

RING = 4
STAGES = 2
AHEAD = 2
GRAN = 1024


def block_kernel(nc, x, norm1_g, w_in, b_in, conv_w, conv_b, mlstm_norm_g, w_br_mlstm,
                 w_br_fox, w_out, norm2_g, w_gate, w_up, w_down, norm_f_g, out):
    w_in, b_in = w_in[0], b_in[0]
    conv_w, conv_b, mlstm_norm_g = conv_w[0], conv_b[0], mlstm_norm_g[0]
    w_bm, w_bf, w_o = w_br_mlstm[0], w_br_fox[0], w_out[0]
    w_g, w_u, w_d = w_gate[0], w_up[0], w_down[0]
    norm1_g, norm2_g = norm1_g[0], norm2_g[0]
    x_rows = x[0].rearrange("(r p) d -> r p d", p=P)
    out_rows = out[0].rearrange("(r p) d -> r p d", p=P)

    slots, granules = [], []

    def slot(views, loads):
        for view in views:
            granules.append((len(slots), view))
        slots.append((len(granules), loads))

    def whole(n):
        return lambda st: st.rearrange("p (k c) -> p k c", k=n)

    def column_slot(w, col):
        src = w[:, col:col + 2 * P].rearrange("(k p) c -> p k c", p=P)
        views = [lambda st, j=j: whole(KD)(st)[:, :, j * P:(j + 1) * P] for j in range(2)]
        if not slots:
            slot(views, [(views[j], src[:, :, j * P:(j + 1) * P]) for j in range(2)])
        else:
            slot(views, [(whole(KD), src)])

    def row_slot(w, block, col):
        src = w[block * P:(block + 4) * P, col:col + HALF].rearrange("(k p) c -> p k c", p=P)
        slot([lambda st, j=j: whole(4)(st)[:, 2 * j:2 * j + 2, :] for j in range(2)],
             [(whole(4), src)])

    gate_view = lambda st: st[:, 0:GRAN].rearrange("p (k c) -> p k c", k=KD)
    gate_loads = [
        (lambda st: gate_view(st)[:, :, 0:2 * H_M],
         w_in[:, C_MI:C_MI + 2 * H_M].rearrange("(k p) c -> p k c", p=P)),
        (lambda st: gate_view(st)[:, :, 2 * H_M:P],
         w_in[:, C_FF:C_FF + P - 2 * H_M].rearrange("(k p) c -> p k c", p=P))]
    column_slot(w_in, C_QK)
    G_GATE = len(granules)
    slot([gate_view], gate_loads)
    for i in range(1, 4):
        column_slot(w_in, C_QK + 2 * P * i)
    qk_block = {(b if b < G_GATE else b + 1): b for b in range(2 * KB)}
    G_MV = len(granules)
    for i in range(2):
        row_slot(w_in, 4 * i, C_MV)
    G_FV = len(granules)
    for i in range(2):
        row_slot(w_in, 4 * i, C_FV)
    G_FQK = len(granules)
    for i in range(4):
        column_slot(w_in, C_FQK + 2 * P * i)
    G_MO = len(granules)
    for i in range(2):
        column_slot(w_in, C_MO + 2 * P * i)
    G_BR = len(granules)
    for i in range(4):
        column_slot(w_in, C_GM + 2 * P * i)
        column_slot(w_in, C_GF + 2 * P * i)
        slot([lambda st, j=j: whole(KD)(st)[:, :, j * P:(j + 1) * P] for j in range(2)],
             [(lambda st, n=n: whole(KD)(st)[:, n * KB:(n + 1) * KB, :],
               w[:, 2 * P * i:2 * P * (i + 1)].rearrange("(k p) c -> p k c", p=P))
              for n, w in enumerate((w_bm, w_bf))])
    G_OUT = len(granules)
    S_OUT = len(slots)
    for half in range(2):
        for i in range(2):
            row_slot(w_o, 4 * i, half * HALF)
    G_FFN = len(granules)
    for i in range(F_BLOCKS // 2):
        column_slot(w_g, 2 * P * i)
        column_slot(w_u, 2 * P * i)
    G_DOWN = len(granules)
    D_GRAN = F_BLOCKS // 2
    down = [(half, 2 * d) for half in range(2) for d in range(D_GRAN)]
    for i in range(0, 2 * D_GRAN, 2):
        slot([lambda st, j=j: whole(4)(st)[:, 2 * j:2 * j + 2, :] for j in range(2)],
             [(lambda st, j=j: whole(4)(st)[:, 2 * j:2 * j + 2, :],
               w_d[f * P:(f + 2) * P, half * HALF:(half + 1) * HALF]
               .rearrange("(k p) c -> p k c", p=P))
              for j, (half, f) in enumerate(down[i:i + 2])])
    N_GRAN = len(granules)

    ctx = ExitStack()
    with ctx:
        base = (nc.sbuf_base + 31) // 32 * 32

        def at(name, shape, dtype, offset):
            return nc.alloc_sbuf_tensor_at(name, shape, dtype, offset=base + offset)

        K = 1024
        A = 0
        x_nat = at("x_nat", [P, ROWS, D], F32, A)
        v_m = at("v_m", [P, ROWS, H_M, DH_M + 1], F32, A)
        v_f = at("v_f", [P, ROWS, W_F], F32, A + 8256)
        x1 = at("x1", [P, ROWS, D], F32, A)
        B = A + 16896
        hT_hi = at("hT_hi", [P, KD, SEQ], F32R, B)
        hT_lo = at("hT_lo", [P, KD, SEQ], F32R, B + 16 * K)
        C = B + 32 * K
        stage = [at(f"stage{i}", [P, 2 * GRAN], F32, C + 8 * K * i) for i in range(STAGES)]
        C += 8 * K * STAGES
        w_hi = [at(f"w_hi{i}", [P, GRAN], F32R, C + 8 * K * i) for i in range(RING)]
        w_lo = [at(f"w_lo{i}", [P, GRAN], F32R, C + 8 * K * i + 4 * K) for i in range(RING)]
        G = C + 8 * K * RING
        gain_a = at("gain_a", [P, D], F32, G)
        gain_b = at("gain_b", [P, D], F32, G + 4 * K)
        v_bias = at("v_bias", [P, 2, W_M], F32, G + 4 * K)
        W = G + 8 * K
        work = [at(f"work{i}", [P, SEQ], F32, W + 2 * K * i) for i in range(6)]
        square_out = at("square_out", [P, SEQ], F32, W + 8 * K)
        R = W + 12 * K
        q_m = at("q_m", [P, H_M, SEQ], F32, R)
        k_m = at("k_m", [P, H_M, SEQ], F32, R + 8 * K)
        q_f = at("q_f", [P, KB, SEQ], F32, R + 16 * K)
        k_f = at("k_f", [P, KB, SEQ], F32, R + 24 * K)
        o_gate = at("o_gate", [P, KB, SEQ], F32, R + 32 * K)
        ymT_hi = at("ymT_hi", [P, KB, SEQ], F32R, R + 40 * K)
        ymT_lo = at("ymT_lo", [P, KB, SEQ], F32R, R + 48 * K)
        yfT_hi = at("yfT_hi", [P, KB, SEQ], F32R, R + 56 * K)
        yfT_lo = at("yfT_lo", [P, KB, SEQ], F32R, R + 64 * K)
        xn = [at(f"xn{i}", [P, D], F32, R + 56 * K + 4 * K * i) for i in range(2)]
        z_pad = at("z_pad", [P, CONV_K - 1 + SEQ], F32, R + 64 * K)
        N_E = sum(SEQ - P * j for j in range(ROWS))
        decay = [at(f"decay{i}", [P, N_E], F32, R + 56 * K + 5 * K * i) for i in range(2)]
        rows_both = at("rows_both", [P, 10 * P], F32R, R + 72 * K)
        probs = [at(f"probs{i}", [P, SEQ], F32, R + 82 * K + 2 * K * i) for i in range(3)]
        mo_half_tanh = at("mo_half_tanh", [P, SEQ], F32, R + 70 * K)
        stab_masked = [at(f"stab_masked{i}", [P, SEQ], F32, R + 82 * K + 2 * K * i) for i in range(2)]
        vec_raw = at("vec_raw", [N_VEC, P], F32, R + 82 * K)
        upper = at("upper", [P, P], F32, R + 86 * K)
        ones = at("ones", [P, P], F32, R + 86 * K + 512)
        mixT_hi = at("mixT_hi", [P, KD, SEQ], F32R, R)
        mixT_lo = at("mixT_lo", [P, KD, SEQ], F32R, R + 16 * K)
        mix_sum = [at(f"mix_sum{i}", [P, SEQ], F32, R + 72 * K + 2 * K * i) for i in range(2)]
        xn2 = [at(f"xn2{i}", [P, D], F32, R + 40 * K + 4 * K * i) for i in range(2)]
        aT_hi = at("aT_hi", [P, F_BLOCKS, SEQ], F32R, R)
        aT_lo = at("aT_lo", [P, F_BLOCKS, SEQ], F32R, R + 44 * K)
        S = R + 88 * K
        small_at = [S]

        def small(name, shape, dtype=F32):
            n = int(np.prod(shape[1:])) * (2 if dtype == BF16 else 4)
            t = at(name, shape, dtype, small_at[0])
            small_at[0] += (n + 31) // 32 * 32
            assert base + small_at[0] <= nc.sbuf_usable_end, small_at[0]
            return t

        ident = small("ident", [P, P])
        ident_b = small("ident_b", [P, P], BF16)
        mask_b = small("mask_b", [P, P], BF16)
        mask_T = small("mask_T", [P, P], BF16)
        pick = small("pick", [P, LANES], F32R)
        vec = small("vec", [P, N_VEC])
        vec_half = small("vec_half", [P, N_VEC])
        gate_bias = small("gate_bias", [LANES + H_M, 1])
        square_sum = small("square_sum", [P, ROWS, 2])
        mean_sq = small("mean_sq", [P, ROWS])
        rstd = small("rstd", [P, ROWS])
        minus_half = small("minus_half", [P, ROWS])
        frame = small("frame", [P, ROWS * ROWS, LANES])
        before = small("before", [P, ROWS, H_M])
        m_stab = small("m_stab", [P, ROWS, H_M])
        m_floor = small("m_floor", [P, ROWS, H_M])
        den = small("den", [P, ROWS])
        head_ms = small("head_ms", [P, ROWS])
        head_rs = small("head_rs", [P, ROWS])
        neg_max = small("neg_max", [P, 4])
        row_sum = small("row_sum", [P, 4])
        row_inv = small("row_inv", [P, 4])
        gate_rows = work[5]
        abs_neg = work[4][:, 0:ROWS * LANES].rearrange("p (j l) -> p j l", l=LANES)
        gates = work[4][:, 128:192].rearrange("p (j l) -> p j l", l=LANES + H_M)
        log_f = work[4][:, 192:192 + ROWS * LANES].rearrange("p (j l) -> p j l", l=LANES)
        cum = work[4][:, 256:256 + ROWS * LANES].rearrange("p (j l) -> p j l", l=LANES)
        softp = work[4][:, 64:64 + ROWS * LANES].rearrange("p (j l) -> p j l", l=LANES)
        psum = [ctx.enter_context(nc.psum_tensor(f"bank{i}", [P, 512], F32)) for i in range(8)]

        def sem(name):
            return ctx.enter_context(nc.semaphore(name))

        x_in = [sem(f"x_in{r}") for r in range(ROWS)]
        gain1_in, vec_in, gbias_in, vbias_in = (sem(n) for n in ("gain1_in", "vec_in", "gbias_in", "vbias_in"))
        first_in = sem("first_in")
        gained, last_half = sem("gained"), sem("last_half")
        gain2_in, gain3_in, xagain_in = sem("gain2_in"), sem("gain3_in"), sem("xagain_in")
        stage_in = [sem(f"stage_in{i}") for i in range(STAGES)]
        hi_split, lo_split, used = sem("hi_split"), sem("lo_split"), sem("granule_used")
        consts = sem("consts")
        vec_T, vec_ready = sem("vec_T"), sem("vec_ready")
        norm = [{n: sem(f"{n}_{i}") for n in ("squared", "summed", "rstd_ready", "xn_ready", "xn_T",
                                              "hT_hi_ready", "hT_lo_ready")} for i in range(3)]
        z_padded, conv_tap, conv_tanh, qk_ready = (sem(n) for n in ("z_padded", "conv_tap", "conv_tanh", "qk_ready"))
        v_ready, v_ones = sem("v_ready"), sem("v_ones")
        fq_ready, fk_ready, mo_tanh, o_ready = (sem(n) for n in ("fq_ready", "fk_ready", "mo_tanh", "o_ready"))
        gate_rows_ready, gates_T, gates_ready = sem("gate_rows_ready"), sem("gates_T"), sem("gates_ready")
        gate_abs, gate_exp, gate_ln, log_f_ready = (sem(n) for n in ("gate_abs", "gate_exp", "gate_ln", "log_f_ready"))
        cum_done, frame_step, frame_T = sem("cum_done"), sem("frame_step"), sem("frame_T")
        rows_hi_ready, rows_lo_ready = sem("rows_hi_ready"), sem("rows_lo_ready")
        g_spread, g_max, m_step, floor_ready = (sem(n) for n in ("g_spread", "g_max", "m_step", "floor_ready"))
        m_spread, s_m, decay_exp, m_masked, weighted = (sem(n) for n in ("m_spread", "s_m", "decay_exp", "m_masked", "weighted"))
        num_m, den_step, h_m, h_squared, h_mean, h_rstd, y_m = (sem(n) for n in ("num_m", "den_step", "h_m", "h_squared", "h_mean", "h_rstd", "y_m"))
        y_mT, y_m32, ymT_hi_ready, ymT_lo_ready = (sem(n) for n in ("y_mT", "y_m32", "ymT_hi_ready", "ymT_lo_ready"))
        logits, fox_max, fox_exp, fox_norm, fox_T, fox_pv = (sem(n) for n in ("logits", "fox_max", "fox_exp", "fox_norm", "fox_T", "fox_pv"))
        fox_PT = [sem("fox_PT_even"), sem("fox_PT_odd")]
        yfT_hi_ready, yfT_lo_ready = sem("yfT_hi_ready"), sem("yfT_lo_ready")
        gate_tanh, mix_step, mix_hi_ready, mix_lo_ready = (sem(n) for n in ("gate_tanh", "mix_step", "mix_hi_ready", "mix_lo_ready"))
        row_out, x1_ready = sem("row_out"), sem("x1_ready")
        ffn_tanh, ffn_step, aT_hi_ready, aT_lo_ready = (sem(n) for n in ("ffn_tanh", "ffn_step", "aT_hi_ready", "aT_lo_ready"))
        row_down, x2_ready, stored = sem("row_down"), sem("x2_ready"), sem("stored")
        block = ctx.enter_context(nc.Block())

        def pair(i, j):
            return i * (i + 1) // 2 + j

        def decay_at(j):
            return sum(SEQ - P * n for n in range(j))

        def wait_stage(eng, g):
            if g == 0:
                eng.wait_ge(first_in, 16)
                return
            s = granules[g][0]
            n = sum(len(slots[i][1]) for i in range(s % STAGES, s + 1, STAGES))
            eng.wait_ge(stage_in[s % STAGES], 16 * (n - 1 if s % STAGES == 0 else n))

        def staged(g):
            s, view = granules[g]
            return view(stage[s % STAGES][:, :])

        def ring(tiles, g):
            n = granules_shape(g)
            return tiles[g % RING][:, :].rearrange("p (k c) -> p k c", k=n)

        def granules_shape(g):
            rows = (G_MV <= g < G_FQK) or (G_OUT <= g < G_FFN) or g >= G_DOWN
            return 2 if rows else KD

        @block.sync
        def _(sp):
            def load_slot(s):
                for n, (view, src) in enumerate(slots[s][1]):
                    landed = first_in if s == 0 and n == 0 else stage_in[s % STAGES]
                    sp.dma_start(view(stage[s % STAGES][:, :]), src).then_inc(landed, 16)

            def load_rows(r):
                sp.dma_start(x_nat[:, r, :], x_rows[r]).then_inc(x_in[r], 16)

            load_rows(0)
            load_rows(1)
            sp.dma_start(gain_a[:, :], norm1_g.rearrange("(a n) -> a n", a=1).to_broadcast([P, D])).then_inc(gain1_in, 16)
            load_slot(0)
            load_rows(2)
            load_rows(3)
            load_slot(1)
            vec_loads = ((V_QK, b_in[C_QK:C_QK + 2 * W_M]), (V_MO, b_in[C_MO:C_MO + W_M]),
                         (V_FQK, b_in[C_FQK:C_FQK + 2 * W_F]), (V_GM, b_in[C_GM:C_GM + 2 * D]),
                         (V_CONVW, conv_w.rearrange("j c -> (j c)")), (V_CONVB, conv_b), (V_NORM, mlstm_norm_g))
            for row, src in vec_loads:
                n = src.shape[0] // P
                sp.dma_start(vec_raw[row:row + n, :], src.rearrange("(a n) -> a n", n=P)).then_inc(vec_in, 16)
            sp.dma_start(gate_bias[0:2 * H_M, :], b_in[C_MI:C_MI + 2 * H_M].rearrange("(n a) -> n a", a=1)).then_inc(gbias_in, 16)
            sp.dma_start(gate_bias[2 * H_M:2 * H_M + H_F, :], b_in[C_FF:C_FF + H_F].rearrange("(n a) -> n a", a=1)).then_inc(gbias_in, 16)
            for n, c in enumerate((C_MV, C_FV)):
                sp.dma_start(v_bias[:, n, :], b_in[c:c + W_M].rearrange("(a n) -> a n", a=1).to_broadcast([P, W_M])).then_inc(vbias_in, 16)
            for s in range(STAGES, len(slots)):
                if s == 12:
                    sp.wait_ge(v_ready, 2 * ROWS)
                    sp.dma_start(gain_b[:, :], norm2_g.rearrange("(a n) -> a n", a=1).to_broadcast([P, D])).then_inc(gain2_in, 16)
                    sp.wait_ge(norm[0]["xn_ready"], ROWS)
                    sp.dma_start(gain_a[:, :], norm_f_g.rearrange("(a n) -> a n", a=1).to_broadcast([P, D])).then_inc(gain3_in, 16)
                if s == S_OUT - 4:
                    sp.wait_ge(fox_pv, 32)
                    sp.wait_ge(num_m, 2 * H_M)
                    sp.dma_start(x1[:, :, :], x[0].rearrange("(r p) d -> p r d", p=P)).then_inc(xagain_in, 16)
                sp.wait_ge(lo_split, slots[s - STAGES][0])
                load_slot(s)
            for r in range(ROWS - 1):
                sp.wait_ge(norm[2]["xn_ready"], r + 1)
                sp.dma_start(out_rows[r], x1[:, r, :]).then_inc(stored, 16)
            for n, (ready, count) in enumerate(((norm[2]["xn_ready"], ROWS), (last_half, 1))):
                sp.wait_ge(ready, count)
                cols = slice(n * HALF, (n + 1) * HALF)
                sp.dma_start(out_rows[ROWS - 1][:, cols], x1[:, ROWS - 1, cols]).then_inc(stored, 16)
            sp.wait_ge(stored, 16 * (ROWS + 1))

        @block.gpsimd
        def _(pool):
            steps = [0]

            def const(ins):
                ins.then_inc(consts, 1)
                steps[0] += 1

            const(pool.memset(ones[:, :], 1.0))
            const(pool.memset(ident[:, :], 0.0))
            const(pool.memset(ident_b[:, :], 0.0))
            const(pool.memset(mask_b[:, :], 0.0))
            const(pool.memset(mask_T[:, :], 0.0))
            const(pool.memset(pick[:, :].bitcast(F32), 0.0))
            const(pool.memset(rows_both[:, :].bitcast(F32), 0.0))
            const(pool.memset(upper[:, :], 1.0))
            const(pool.memset(minus_half[:, :], -0.5))
            const(pool.memset(z_pad[:, 0:CONV_K - 1], 0.0))
            pool.wait_ge(consts, steps[0])
            for t in (ident, ident_b):
                const(pool.affine_select(out=t[:, :], in_=t[:, :], compare_op=ALU.not_equal, fill=1.0, base=0,
                                         pattern=[[-1, P]], channel_multiplier=1))
            for at_row in (0, LO):
                const(pool.affine_select(out=pick[:, :], in_=pick[:, :].bitcast(F32), compare_op=ALU.not_equal,
                                         fill=1.0, base=-at_row, pattern=[[-1, LANES]], channel_multiplier=1))
                pool.wait_ge(consts, steps[0])
            const(pool.affine_select(out=mask_b[:, :], in_=mask_b[:, :], compare_op=ALU.is_ge, fill=NEG,
                                     base=0, pattern=[[-1, P]], channel_multiplier=1))
            const(pool.affine_select(out=mask_T[:, :], in_=mask_T[:, :], compare_op=ALU.is_ge, fill=-NEG,
                                     base=0, pattern=[[1, P]], channel_multiplier=-1))
            const(pool.affine_select(out=upper[:, :], in_=upper[:, :], compare_op=ALU.is_ge, fill=0.0,
                                     base=0, pattern=[[1, P]], channel_multiplier=-1))
            assert steps[0] == N_CONSTS

            def rows_rstd(i):
                for r in range(ROWS):
                    if i == 0 and r == 2:
                        pool.wait_ge(hi_split, 1)
                        pool.tensor_tensor(ring(w_lo, 0), staged(0), ring(w_hi, 0).bitcast(F32),
                                           ALU.subtract).then_inc(lo_split, 1)
                    pool.wait_ge(norm[i]["summed"], 2 * (r + 1))
                    pool.tensor_tensor(rstd[:, r:r + 1], mean_sq[:, r:r + 1], minus_half[:, 0:1],
                                       ALU.pow).then_inc(norm[i]["rstd_ready"], 1)

            rows_rstd(0)
            pool.wait_ge(norm[0]["xn_ready"], ROWS)
            pool.memset(v_m[:, :, :, DH_M:DH_M + 1], 1.0).then_inc(v_ones, 1)
            for i in range(H_M + 1):
                if i >= 1:
                    h = i - 1
                    pool.wait_ge(h_mean, 2 * h + 2)
                    if h >= 1:
                        pool.wait_ge(y_m, h)
                    pool.tensor_tensor(head_rs[:, :], head_ms[:, :], minus_half[:, :],
                                       ALU.pow).then_inc(h_rstd, 1)
                if i < H_M:
                    h = i
                    pool.wait_ge(h_m, 2 * h + 2)
                    if h >= 1:
                        pool.wait_ge(h_mean, 2 * h)
                    pool.tensor_tensor(work[2][:, :], work[h % 2][:, :], work[h % 2][:, :],
                                       ALU.mult).then_inc(h_squared, 1)
            rows_rstd(1)
            rows_rstd(2)

        @block.scalar
        def _(act):
            def square(i, src, r, halves):
                for half in halves:
                    n = count_squares[i]
                    if n:
                        act.wait_ge(norm[i]["squared"], n)
                    act.activation(square_out[:, :], src[:, r, half * HALF:(half + 1) * HALF], ACT.Square,
                                   accum_out=square_sum[:, r, half:half + 1]).then_inc(norm[i]["squared"], 1)
                    count_squares[i] += 1

            count_squares = [0, 0, 0]

            def take_hT_hi(i, r):
                for half in range(2):
                    act.wait_ge(norm[i]["xn_T"], 2 * r + half + 1)
                    bank = norm_bank(i, r, half)
                    act.activation(hT_hi[:, 4 * half:4 * half + 4, r * P:(r + 1) * P],
                                   psum[bank][:, :].rearrange("p (k c) -> p k c", k=4),
                                   ACT.Copy).then_inc(norm[i]["hT_hi_ready"], 1)

            def split_hi(g):
                if g >= N_GRAN:
                    return
                wait_stage(act, g)
                if g >= RING:
                    act.wait_ge(used, g - RING + 1)
                act.activation(ring(w_hi, g), staged(g), ACT.Copy).then_inc(hi_split, 1)

            for r in range(2):
                act.wait_ge(x_in[r], 16)
                square(0, x_nat, r, (0, 1))
            split_hi(0)
            take_hT_hi(0, 0)
            take_hT_hi(0, 1)
            for r in range(2, ROWS):
                act.wait_ge(x_in[r], 16)
                square(0, x_nat, r, (0, 1))
                split_hi(r - 1)
            take_hT_hi(0, 2)
            take_hT_hi(0, 3)
            split_hi(3)

            def conv_tanh_of(b):
                act.wait_ge(conv_tap, CONV_K * (b + 1))
                if b >= 2:
                    act.wait_ge(qk_ready, b - 1)
                act.activation(work[2 + b % 2][:, :], work[b % 2][:, :], ACT.Tanh, scale=0.5).then_inc(conv_tanh, 1)

            for g in range(G_MO):
                if g + AHEAD > N_FIRST:
                    split_hi(g + AHEAD)
                if g in qk_block:
                    b = qk_block[g]
                    if b >= 1:
                        conv_tanh_of(b - 1)
                    act.wait_ge(used, g + 1)
                    if b == 0:
                        act.wait_ge(vec_ready, 1)
                        act.wait_ge(consts, N_CONSTS)
                        act.wait_ge(norm[0]["xn_T"], 2 * ROWS)
                    else:
                        act.wait_ge(conv_tap, CONV_K * b)
                    act.activation(z_pad[:, CONV_K - 1:], psum[qk_bank(b)][:, :], ACT.Identity,
                                   bias=vec[:, V_QK + b:V_QK + b + 1]).then_inc(z_padded, 1)
                if g == G_MV:
                    conv_tanh_of(7)
                if g == G_GATE + 2:
                    act.wait_ge(gate_abs, 1)
                    act.activation(softp, abs_neg, ACT.Exp).then_inc(gate_exp, 1)
                    act.wait_ge(gate_exp, 1)
                    act.activation(softp, softp, ACT.Ln, bias=1.0).then_inc(gate_ln, 1)
                if g == G_MV + 2:
                    act.wait_ge(consts, N_CONSTS)
                    for n, (a, b) in enumerate(ROW_CHUNKS):
                        act.wait_ge(frame_T, n + 1)
                        act.activation(rows_both[0:LANES, a * P:b * P], psum[5 + n][0:LANES, 0:(b - a) * P],
                                       ACT.Copy).then_inc(rows_hi_ready, 1)
                if G_FQK + KB <= g < G_MO:
                    b = g - G_FQK - KB
                    act.wait_ge(used, g + 1)
                    act.activation(k_f[:, b, :], psum[fqk_bank(KB + b)][:, :], ACT.Identity,
                                   bias=vec[:, V_FQK + KB + b:V_FQK + KB + b + 1]).then_inc(fk_ready, 1)

            act.wait_ge(m_step, 2)
            act.activation(m_floor[:, :, :], m_floor[:, :, :], ACT.Exp, scale=-1.0).then_inc(floor_ready, 1)

            def take_ymT_hi(h):
                act.wait_ge(y_m32, h + 1)
                act.activation(ymT_hi[:, h, :], work[4 + h % 2][:, :], ACT.Copy).then_inc(ymT_hi_ready, 1)

            def mo_tanh_of(h):
                act.wait_ge(used, G_MO + h + 1)
                if h >= 1:
                    act.wait_ge(o_ready, h)
                act.activation(mo_half_tanh[:, :], psum[3][:, :], ACT.Tanh, scale=0.5,
                               bias=vec_half[:, V_MO + h:V_MO + h + 1]).then_inc(mo_tanh, 1)

            for h in range(H_M):
                act.wait_ge(m_spread, h + 1)
                act.wait_ge(m_masked, h + 1)
                if h >= 2:
                    act.wait_ge(num_m, 2 * (h - 1))
                for j in range(ROWS):
                    for q in range(j, ROWS):
                        o = decay_at(j) + (q - j) * P
                        m = stab_masked[h % 2] if q == j else psum[2]
                        act.activation(decay[h % 2][:, o:o + P], m[:, q * P:(q + 1) * P],
                                       ACT.Exp, scale=-1.0,
                                       bias=frame[:, ROWS * q + j, h:h + 1]).then_inc(decay_exp, 1)
                if h >= 2:
                    take_ymT_hi(h - 2)
                split_hi(G_MO + h + AHEAD)
                if h < H_M - 1:
                    mo_tanh_of(h)

            def take_yfT_hi(hp):
                act.wait_ge(fox_pv, 8 * (hp + 1))
                act.activation(yfT_hi[:, hp, :], psum[hp % 2][:, :], ACT.Copy).then_inc(yfT_hi_ready, 1)

            def fox_softmax(u):
                _, q, _ = fox_unit(u)
                n = (q + 1) * P
                act.wait_ge(fox_max, u + 1)
                if u >= 3:
                    act.wait_ge(fox_T, u - 2)
                act.activation(probs[u % 3][:, 0:n], psum[4 + u % 3][:, 0:n], ACT.Exp,
                               bias=neg_max[:, u % 4:u % 4 + 1],
                               accum_out=row_sum[:, u % 4:u % 4 + 1]).then_inc(fox_exp, 1)

            def fox_take_odd(u):
                _, q, _ = fox_unit(u)
                n = (q + 1) * P
                act.wait_ge(fox_T, u + 1)
                if u >= 2:
                    act.wait_ge(fox_pv, u - 1)
                act.activation(work[1][:, 0:n], psum[3][:, 0:n], ACT.Copy).then_inc(fox_PT[1], 1)

            def gate_tanh_of(c, n, bank):
                col = (V_GM, V_GF)[n // 2] + 2 * c + n % 2
                act.activation(work[2 + n][:, :], psum[bank][:, :], ACT.Tanh, scale=0.5,
                               bias=vec_half[:, col:col + 1]).then_inc(gate_tanh, 1)

            def first_gate_tanh(n):
                act.wait_ge(used, G_BR + n + 1)
                if n == 0:
                    act.wait_ge(ymT_lo_ready, H_M)
                gate_tanh_of(0, n, 7)

            act.wait_ge(decay_exp, 10 * H_M)
            for u in range(32 + 2):
                n = (u - FILL_FROM) // KD - 1
                gate_done = u > FILL_FROM and (u - FILL_FROM) % KD == 0
                if gate_done:
                    first_gate_tanh(n)
                if u < 32:
                    fox_softmax(u)
                if u == 1:
                    mo_tanh_of(3)
                if u == 3:
                    act.wait_ge(y_m, H_M)
                if u >= 2 and u % 2:
                    fox_take_odd(u - 2)
                if u in (3, 5):
                    take_ymT_hi(u // 2 + 1)
                if n in (0, 1) and (u - FILL_FROM) % KD == 2:
                    split_hi(G_BR + 4 + n)
                if u in (6, 8):
                    split_hi(G_BR + 2 + (u - 6) // 2)
                if u >= 8 and u % 8 == 4:
                    take_yfT_hi(u // 8 - 1)
            take_yfT_hi(KB - 1)
            first_gate_tanh(3)

            for c in range(4):
                for n in range(6):
                    if c == 0 and n < 4:
                        continue
                    g = G_BR + 6 * c + n
                    split_hi(g + AHEAD)
                    act.wait_ge(used, g + 1)
                    if n < 4:
                        act.wait_ge(mix_step, 3 * 2 * c - (1 if n % 2 else 4))
                        gate_tanh_of(c, n, GATE_BANKS[n])
                    else:
                        b = 2 * c + n - 4
                        act.wait_ge(mix_step, 3 * b + 3)
                        act.activation(mixT_hi[:, b, :], mix_sum[b % 2][:, :], ACT.Copy, scale=0.5).then_inc(mix_hi_ready, 1)

            for n in range(6):
                split_hi(G_OUT + AHEAD + n)
            for r in range(ROWS):
                act.wait_ge(x1_ready, r + 1)
                square(1, x1, r, (0,))
            for r in range(ROWS):
                if r == ROWS - 1:
                    for n in range(2):
                        split_hi(G_FFN + n)
                act.wait_ge(x1_ready, ROWS + r + 1)
                square(1, x1, r, (1,))
                if r >= 1:
                    take_hT_hi(1, r - 1)
            split_hi(G_FFN + 2)
            take_hT_hi(1, ROWS - 1)

            for p in range(F_BLOCKS // 2):
                for n in range(4):
                    g = G_FFN + 4 * p + n
                    if g + AHEAD >= G_FFN + N_FIRST:
                        split_hi(g + AHEAD)
                    act.wait_ge(used, g + 1)
                    if n < 2:
                        f = 2 * p + n
                        if p >= 1:
                            act.wait_ge(ffn_step, 2 * (f - 2) + 1)
                        else:
                            act.wait_ge(mix_lo_ready, 8)
                        act.activation(work[n][:, :], psum[4 * (p % 2) + n][:, :], ACT.Tanh, scale=0.5).then_inc(ffn_tanh, 1)
                    else:
                        f = 2 * p + n - 2
                        act.wait_ge(ffn_step, 2 * f + 2)
                        act.activation(aT_hi[:, f, :], work[2 + n - 2][:, :], ACT.Copy).then_inc(aT_hi_ready, 1)

            for n in range(2 * D_GRAN - RING):
                split_hi(G_DOWN + n + AHEAD)
                if n == D_GRAN + 1:
                    for r in range(ROWS):
                        act.wait_ge(x2_ready, r + 1)
                        square(2, x1, r, (0,))
            for n in range(AHEAD):
                split_hi(N_GRAN - AHEAD + n)
            for r in range(ROWS):
                act.wait_ge(x2_ready, ROWS + r + 1)
                square(2, x1, r, (1,))
            act.wait_ge(gained, 2)
            act.wait_ge(norm[2]["rstd_ready"], ROWS)
            act.activation(x1[:, ROWS - 1, HALF:D], work[1][:, :], ACT.Copy,
                           scale=rstd[:, ROWS - 1:ROWS]).then_inc(last_half, 1)

        @block.vector
        def _(dve):
            def mean_of_squares(i, r, n_squares):
                dve.wait_ge(norm[i]["squared"], n_squares)
                dve.tensor_tensor(mean_sq[:, r:r + 1], square_sum[:, r, 0:1], square_sum[:, r, 1:2],
                                  ALU.add).then_inc(norm[i]["summed"], 1)
                dve.wait_ge(norm[i]["summed"], 2 * r + 1)
                dve.tensor_scalar(mean_sq[:, r:r + 1], mean_sq[:, r:r + 1], 1.0 / D, EPS, ALU.mult,
                                  ALU.add).then_inc(norm[i]["summed"], 1)

            def normalise(i, src, r, gain, dst):
                dve.wait_ge(norm[i]["rstd_ready"], r + 1)
                dve.scalar_tensor_tensor(out=dst, in0=src[:, r, :], scalar=rstd[:, r:r + 1], in1=gain[:, :],
                                         op0=ALU.mult, op1=ALU.mult).then_inc(norm[i]["xn_ready"], 1)

            def take_hT_lo(i, r):
                for half in range(2):
                    dve.wait_ge(norm[i]["hT_hi_ready"], 2 * r + half + 1)
                    bank = norm_bank(i, r, half)
                    hT = (slice(None), slice(4 * half, 4 * half + 4), slice(r * P, (r + 1) * P))
                    dve.tensor_tensor(hT_lo[hT], psum[bank][:, :].rearrange("p (k c) -> p k c", k=4),
                                      hT_hi[hT].bitcast(F32), ALU.subtract).then_inc(norm[i]["hT_lo_ready"], 1)

            def split_lo(g):
                if g >= N_GRAN:
                    return
                dve.wait_ge(hi_split, g + 1)
                if g == 1:
                    dve.wait_ge(lo_split, 1)
                if g == G_GATE:
                    n = LANES + H_M
                    dve.tensor_tensor(ring(w_hi, g)[:, :, LO:LO + n], staged(g)[:, :, 0:n],
                                      ring(w_hi, g)[:, :, 0:n].bitcast(F32), ALU.subtract).then_inc(lo_split, 1)
                    return
                dve.tensor_tensor(ring(w_lo, g), staged(g), ring(w_hi, g).bitcast(F32),
                                  ALU.subtract).then_inc(lo_split, 1)

            def norm_rows(r):
                if r >= 2:
                    mean_of_squares(0, r, 2 * r + 2)
                    dve.wait_ge(norm[0]["xn_T"], 2 * (r - 1))
                normalise(0, x_nat, r, gain_a, xn[r % 2][:, :])

            for r in range(2):
                mean_of_squares(0, r, 2 * r + 2)
            dve.wait_ge(gain1_in, 16)
            norm_rows(0)
            norm_rows(1)
            take_hT_lo(0, 0)
            take_hT_lo(0, 1)
            norm_rows(2)
            split_lo(1)
            norm_rows(3)
            take_hT_lo(0, 2)
            split_lo(2)
            take_hT_lo(0, 3)
            split_lo(3)
            dve.wait_ge(vec_T, 1)
            dve.tensor_copy(vec[:, :], psum[0][:, 0:N_VEC]).then_inc(vec_ready, 1)
            dve.tensor_scalar(vec_half[:, :], psum[0][:, 0:N_VEC], 0.5, None, ALU.mult).then_inc(vec_ready, 1)
            dve.wait_ge(vec_ready, 2)

            def qk_of(b):
                dve.wait_ge(conv_tanh, b + 1)
                dst = (q_m if b < KB else k_m)[:, b % KB, :]
                dve.scalar_tensor_tensor(out=dst, in0=work[2 + b % 2][:, :], scalar=1.0, in1=work[b % 2][:, :],
                                         op0=ALU.add, op1=ALU.mult).then_inc(qk_ready, 1)

            for g in range(G_MO):
                if g + AHEAD > N_FIRST:
                    split_lo(g + AHEAD)
                if g == G_GATE:
                    dve.wait_ge(used, g + 1)
                    dve.wait_ge(gbias_in, 32)
                    n = LANES + H_M
                    dve.tensor_copy(gate_rows[0:n, :], psum[1][LO:LO + n, :]).then_inc(gate_rows_ready, 1)
                    dve.wait_ge(gate_rows_ready, 1)
                    dve.scalar_tensor_tensor(out=gate_rows[0:n, :], in0=psum[1][0:n, :], scalar=gate_bias[:, 0:1],
                                             in1=gate_rows[0:n, :], op0=ALU.add, op1=ALU.add).then_inc(gate_rows_ready, 1)
                if g in qk_block:
                    b = qk_block[g]
                    if b >= 1:
                        qk_of(b - 1)
                    dve.wait_ge(z_padded, b + 1)
                    if b >= 2:
                        dve.wait_ge(qk_ready, b - 1)
                    u = work[b % 2]
                    dve.tensor_scalar(u[:, :], z_pad[:, 0:SEQ], vec[:, V_CONVW + b:V_CONVW + b + 1],
                                      vec[:, V_CONVB + b:V_CONVB + b + 1], ALU.mult, ALU.add).then_inc(conv_tap, 1)
                    for j in range(1, CONV_K):
                        dve.wait_ge(conv_tap, CONV_K * b + j)
                        c = V_CONVW + 8 * j + b
                        dve.scalar_tensor_tensor(out=u[:, :], in0=z_pad[:, j:j + SEQ], scalar=vec[:, c:c + 1],
                                                 in1=u[:, :], op0=ALU.mult, op1=ALU.add).then_inc(conv_tap, 1)
                if g == G_MV:
                    qk_of(7)
                if g == G_GATE + 2:
                    dve.wait_ge(gates_T, 1)
                    dve.tensor_copy(gates[:, :, :], psum[1][:, 0:64].rearrange("p (j l) -> p j l", l=16)).then_inc(gates_ready, 1)
                    dve.wait_ge(gates_ready, 1)
                    lanes = gates[:, :, H_M:]
                    dve.tensor_scalar(abs_neg, lanes, -1.0, None, ALU.mult).then_inc(gates_ready, 1)
                    dve.wait_ge(gates_ready, 2)
                    dve.tensor_tensor(abs_neg, abs_neg, lanes, ALU.min).then_inc(gate_abs, 1)
                if g == G_GATE + 3:
                    dve.wait_ge(gate_ln, 1)
                    dve.scalar_tensor_tensor(out=log_f[:, :, :], in0=gates[:, :, H_M:], scalar=0.0, in1=softp,
                                             op0=ALU.min, op1=ALU.subtract).then_inc(log_f_ready, 1)
                if g == G_MV:
                    dve.wait_ge(cum_done, 1)
                    cums = psum[1][:, 64:64 + ROWS * LANES].rearrange("p (j l) -> p j l", l=LANES)
                    tots = psum[1][:, 128:128 + ROWS * LANES].rearrange("p (j l) -> p j l", l=LANES)
                    n = 0

                    def step(ins):
                        nonlocal n
                        ins.then_inc(frame_step, 1)
                        n += 1
                        dve.wait_ge(frame_step, n)

                    step(dve.tensor_copy(cum[:, :, :], cums))
                    step(dve.tensor_scalar(frame[:, 0::ROWS + 1, :], cum[:, :, :], -1.0, None, ALU.mult))
                    step(dve.tensor_tensor(frame[:, 0::ROWS + 1, 0:H_M], gates[:, :, 0:H_M],
                                           frame[:, 0::ROWS + 1, 0:H_M], ALU.add))
                    step(dve.memset(before[:, 0, :], 0.0))
                    for q in range(1, ROWS):
                        tot = tots[:, q - 1, :]
                        step(dve.tensor_tensor(frame[:, ROWS * q:ROWS * q + q, :],
                                               frame[:, ROWS * (q - 1):ROWS * (q - 1) + q, :],
                                               tots[:, q - 1:q, :].to_broadcast([P, q, LANES]), ALU.add))
                        step(dve.tensor_tensor(before[:, q, :], before[:, q - 1, :], tot[:, 0:H_M], ALU.add))
                    assert n == FRAME_STEPS
                if g == G_MV + 2:
                    for n, (a, b) in enumerate(ROW_CHUNKS):
                        dve.wait_ge(rows_hi_ready, n + 1)
                        dve.tensor_tensor(rows_both[LO:LO + LANES, a * P:b * P], psum[5 + n][0:LANES, 0:(b - a) * P],
                                          rows_both[0:LANES, a * P:b * P].bitcast(F32), ALU.subtract).then_inc(rows_lo_ready, 1)
                if g in (G_FV - 1, G_FQK - 1):
                    n = (G_FV - 1, G_FQK - 1).index(g)
                    dve.wait_ge(used, g + 1)
                    dve.wait_ge(vbias_in, 32)
                    dve.wait_ge(norm[0]["xn_ready"], ROWS)
                    for r in range(ROWS):
                        if n == 0:
                            dve.tensor_tensor(v_m[:, r, :, 0:DH_M], psum[V_BANKS[0][r]][:, :].rearrange("p (h d) -> p h d", h=H_M),
                                              v_bias[:, 0, :].rearrange("p (h d) -> p h d", h=H_M), ALU.add).then_inc(v_ready, 1)
                        else:
                            dve.tensor_tensor(v_f[:, r, :], psum[V_BANKS[1][r]][:, :], v_bias[:, 1, :], ALU.add).then_inc(v_ready, 1)
                if G_FQK <= g < G_FQK + KB:
                    b = g - G_FQK
                    dve.wait_ge(used, g + 1)
                    dve.tensor_scalar(q_f[:, b, :], psum[fqk_bank(b)][:, :], vec[:, V_FQK + b:V_FQK + b + 1],
                                      DH_F ** -0.5, ALU.add, ALU.mult).then_inc(fq_ready, 1)
                if G_FQK <= g < G_MO:
                    for u in spread_units(g - G_FQK):
                        q, h = u // H_M, u % H_M
                        dve.wait_ge(g_spread, u + 1)
                        dve.reduce_max(m_stab[:, q, h:h + 1], psum[spread_bank(u)][:, 0:(q + 1) * P], AX.X).then_inc(g_max, 1)

            dve.wait_ge(g_max, 16)
            dve.tensor_tensor(m_stab[:, :, :], m_stab[:, :, :], before[:, :, :], ALU.max).then_inc(m_step, 1)
            dve.wait_ge(m_step, 1)
            dve.tensor_tensor(m_floor[:, :, :], m_stab[:, :, :], cum[:, :, 0:H_M], ALU.add).then_inc(m_step, 1)

            def take_ymT(h):
                dve.wait_ge(y_mT, h + 1)
                dve.wait_ge(o_ready, h + 1)
                if h >= 2:
                    dve.wait_ge(ymT_lo_ready, h - 1)
                dve.tensor_tensor(work[4 + h % 2][:, :], psum[head_T_bank(h)][:, :], o_gate[:, h, :], ALU.mult).then_inc(y_m32, 1)
                dve.wait_ge(ymT_hi_ready, h + 1)
                dve.tensor_tensor(ymT_lo[:, h, :], work[4 + h % 2][:, :], ymT_hi[:, h, :].bitcast(F32),
                                  ALU.subtract).then_inc(ymT_lo_ready, 1)

            QK_SCALE = 0.25 * DH_M ** -0.5
            def mask_stabiliser(h):
                dve.wait_ge(m_spread, h + 1)
                if h >= 2:
                    dve.wait_ge(decay_exp, 10 * (h - 1))
                dve.tensor_tensor(stab_masked[h % 2][:, :].rearrange("p (q t) -> p q t", q=ROWS),
                                  psum[2][:, :].rearrange("p (q t) -> p q t", q=ROWS),
                                  mask_T[:, :].rearrange("p (a t) -> p a t", a=1).to_broadcast([P, ROWS, P]),
                                  ALU.add).then_inc(m_masked, 1)

            def head_mean_square(h):
                dve.wait_ge(h_squared, h + 1)
                if h >= 1:
                    dve.wait_ge(h_rstd, h)
                dve.reduce_sum(head_ms[:, :], work[2][:, :].rearrange("p (q d) -> p q d", q=ROWS), AX.X).then_inc(h_mean, 1)
                dve.wait_ge(h_mean, 2 * h + 1)
                dve.tensor_scalar(head_ms[:, :], head_ms[:, :], 1.0 / DH_M, EPS, ALU.mult, ALU.add).then_inc(h_mean, 1)

            def weigh_scores(h):
                for j in range(ROWS):
                    o, n = decay_at(j), SEQ - j * P
                    c = (0, 0, 0, 256)[j]
                    dve.wait_ge(s_m, 4 * h + (1, 2, 4, 4)[j])
                    dve.wait_ge(decay_exp, 10 * h + sum(ROWS - m for m in range(j + 1)))
                    dve.scalar_tensor_tensor(out=decay[h % 2][:, o:o + n], in0=psum[4 + min(j, 2)][:, c:c + n],
                                             scalar=QK_SCALE, in1=decay[h % 2][:, o:o + n], op0=ALU.mult,
                                             op1=ALU.mult).then_inc(weighted, 1)

            def pair_tile(n):
                return psum[n][:, 0:2 * (DH_M + 1)].rearrange("p (q d) -> p q d", q=2)

            def head_output(h):
                if h == 0:
                    dve.wait_ge(floor_ready, 1)
                else:
                    dve.wait_ge(h_m, 2 * h)
                for n in range(2):
                    dve.wait_ge(num_m, 2 * h + n + 1)
                    dve.scalar_tensor_tensor(out=den[:, 2 * n:2 * n + 2], in0=pair_tile(n)[:, :, DH_M], scalar=-1.0,
                                             in1=m_floor[:, 2 * n:2 * n + 2, h], op0=ALU.mult,
                                             op1=ALU.max).then_inc(den_step, 1)
                for n in range(2):
                    dve.wait_ge(den_step, 5 * h + n + 1)
                    dve.tensor_tensor(den[:, 2 * n:2 * n + 2], pair_tile(n)[:, :, DH_M], den[:, 2 * n:2 * n + 2],
                                      ALU.max).then_inc(den_step, 1)
                dve.wait_ge(den_step, 5 * h + 4)
                dve.reciprocal(den[:, :], den[:, :]).then_inc(den_step, 1)
                dve.wait_ge(den_step, 5 * h + 5)
                if h >= 2:
                    dve.wait_ge(y_m, h - 1)
                for n in range(2):
                    dve.tensor_tensor(work[h % 2][:, 256 * n:256 * n + 256].rearrange("p (q d) -> p q d", q=2),
                                      pair_tile(n)[:, :, 0:DH_M],
                                      den[:, 2 * n:2 * n + 2].rearrange("p (q a) -> p q a", a=1).to_broadcast([P, 2, DH_M]),
                                      ALU.mult).then_inc(h_m, 1)

            def head_normalise(h):
                dve.wait_ge(h_rstd, h + 1)
                if h >= 1:
                    dve.wait_ge(y_mT, h)
                dve.tensor_tensor(work[3][:, :].rearrange("p (q d) -> p q d", q=ROWS),
                                  work[h % 2][:, :].rearrange("p (q d) -> p q d", q=ROWS),
                                  head_rs[:, :].rearrange("p (q a) -> p q a", a=1).to_broadcast([P, ROWS, DH_M]),
                                  ALU.mult).then_inc(y_m, 1)

            def open_gate(h):
                dve.wait_ge(mo_tanh, h + 1)
                dve.tensor_scalar(o_gate[:, h, :], mo_half_tanh[:, :], 1.0,
                                  vec_half[:, V_NORM + h:V_NORM + h + 1], ALU.add, ALU.mult).then_inc(o_ready, 1)

            for h in range(H_M):
                mask_stabiliser(h)
                weigh_scores(h)
                if h >= 1:
                    head_output(h - 1)
                if h >= 2:
                    take_ymT(h - 2)
                if h >= 1:
                    head_mean_square(h - 1)
                split_lo(G_MO + h + AHEAD)
                if h >= 1:
                    head_normalise(h - 1)
                if h < H_M - 1:
                    open_gate(h)
            head_output(3)

            def take_yfT_lo(hp):
                dve.wait_ge(yfT_hi_ready, hp + 1)
                dve.tensor_tensor(yfT_lo[:, hp, :], psum[hp % 2][:, :], yfT_hi[:, hp, :].bitcast(F32),
                                  ALU.subtract).then_inc(yfT_lo_ready, 1)

            def fox_row_max(u):
                _, q, _ = fox_unit(u)
                dve.wait_ge(logits, u + 1)
                if u >= 4:
                    dve.wait_ge(fox_exp, u - 3)
                dve.tensor_reduce(neg_max[:, u % 4:u % 4 + 1], psum[4 + u % 3][:, 0:(q + 1) * P], AX.X, ALU.max,
                                  negate=True).then_inc(fox_max, 1)

            def fox_divide(u):
                _, q, _ = fox_unit(u)
                n = (q + 1) * P
                dve.wait_ge(fox_exp, u + 1)
                if u >= 1:
                    dve.wait_ge(fox_norm, 2 * u)
                dve.reciprocal(row_inv[:, 0:1], row_sum[:, u % 4:u % 4 + 1]).then_inc(fox_norm, 1)
                dve.wait_ge(fox_norm, 2 * u + 1)
                dve.tensor_scalar(probs[u % 3][:, 0:n], probs[u % 3][:, 0:n], row_inv[:, 0:1], None,
                                  ALU.mult).then_inc(fox_norm, 1)

            def fox_take_even(u):
                _, q, _ = fox_unit(u)
                n = (q + 1) * P
                dve.wait_ge(fox_T, u + 1)
                if u >= 2:
                    dve.wait_ge(fox_pv, u - 1)
                dve.tensor_copy(work[0][:, 0:n], psum[2][:, 0:n]).then_inc(fox_PT[0], 1)

            for u in range(32 + 2):
                if u < 32:
                    fox_row_max(u)
                if 1 <= u < 33:
                    fox_divide(u - 1)
                if u == 1:
                    head_mean_square(3)
                if u >= 2 and u % 2 == 0:
                    fox_take_even(u - 2)
                if u == 2:
                    head_normalise(3)
                if u == 3:
                    take_ymT(2)
                if u == 4:
                    open_gate(3)
                if u == 5:
                    take_ymT(3)
                if u in (7, 9):
                    split_lo(G_BR + 2 + (u - 7) // 2)
                if u > FILL_FROM + KD and (u - FILL_FROM) % KD == 3 and u < FILL_FROM + 3 * KD:
                    split_lo(G_BR + 4 + (u - FILL_FROM) // KD - 1)
                if u >= 8 and u % 8 == 4:
                    take_yfT_lo(u // 8 - 1)
            take_yfT_lo(KB - 1)

            for c in range(4):
                for n in range(6):
                    if c or n >= 4:
                        split_lo(G_BR + 6 * c + n + AHEAD)
                    if n >= 4:
                        j, b = n - 4, 2 * c + n - 4
                        dve.wait_ge(used, G_BR + 6 * c + n + 1)
                        dve.wait_ge(gate_tanh, 4 * c + 4)
                        if b >= 2:
                            dve.wait_ge(mix_lo_ready, b - 1)
                        if b >= 1:
                            dve.wait_ge(mix_step, 3 * b)
                        if b == 0:
                            dve.wait_ge(fox_pv, 32)
                        s = mix_sum[b % 2]
                        dve.scalar_tensor_tensor(out=s[:, :], in0=work[2 + j][:, :], scalar=1.0, in1=psum[2 * j][:, :],
                                                 op0=ALU.add, op1=ALU.mult).then_inc(mix_step, 1)
                        dve.scalar_tensor_tensor(out=work[0][:, :], in0=work[4 + j][:, :], scalar=1.0, in1=psum[2 * j + 1][:, :],
                                                 op0=ALU.add, op1=ALU.mult).then_inc(mix_step, 1)
                        dve.wait_ge(mix_step, 3 * b + 2)
                        dve.tensor_tensor(s[:, :], s[:, :], work[0][:, :], ALU.add).then_inc(mix_step, 1)
                        dve.wait_ge(mix_hi_ready, b + 1)
                        dve.scalar_tensor_tensor(out=mixT_lo[:, b, :], in0=s[:, :], scalar=0.5,
                                                 in1=mixT_hi[:, b, :].bitcast(F32), op0=ALU.mult,
                                                 op1=ALU.subtract).then_inc(mix_lo_ready, 1)

            for n in range(6):
                if n == 4:
                    dve.wait_ge(used, G_OUT + 4)
                    dve.wait_ge(xagain_in, 16)
                split_lo(G_OUT + AHEAD + n)
            for r in range(ROWS):
                dve.tensor_tensor(x1[:, r, 0:HALF], x1[:, r, 0:HALF], psum[4 + r][:, :], ALU.add).then_inc(x1_ready, 1)
            dve.wait_ge(gain2_in, 16)
            for r in range(ROWS):
                if r == ROWS - 1:
                    for n in range(2):
                        split_lo(G_FFN + n)
                    dve.wait_ge(used, G_OUT + 8)
                else:
                    dve.wait_ge(row_out, r + 1)
                dve.tensor_tensor(x1[:, r, HALF:D], x1[:, r, HALF:D], psum[r][:, :], ALU.add).then_inc(x1_ready, 1)
                mean_of_squares(1, r, ROWS + r + 1)
                if r == ROWS - 1:
                    take_hT_lo(1, r - 1)
                if r >= 2:
                    dve.wait_ge(norm[1]["xn_T"], 2 * (r - 1))
                normalise(1, x1, r, gain_b, xn2[r % 2][:, :])
                if 1 <= r < ROWS - 1:
                    take_hT_lo(1, r - 1)
            split_lo(G_FFN + 2)
            take_hT_lo(1, ROWS - 1)

            for p in range(F_BLOCKS // 2):
                for n in range(4):
                    g = G_FFN + 4 * p + n
                    if g + AHEAD >= G_FFN + N_FIRST:
                        split_lo(g + AHEAD)
                    if n >= 2:
                        j, f = n - 2, 2 * p + n - 2
                        y = work[2 + j]
                        dve.wait_ge(used, g + 1)
                        dve.wait_ge(ffn_tanh, f + 1)
                        if f >= 2:
                            dve.wait_ge(aT_lo_ready, f - 1)
                        dve.scalar_tensor_tensor(out=y[:, :], in0=work[j][:, :], scalar=1.0,
                                                 in1=psum[4 * (p % 2) + j][:, :], op0=ALU.add,
                                                 op1=ALU.mult).then_inc(ffn_step, 1)
                        dve.wait_ge(ffn_step, 2 * f + 1)
                        dve.scalar_tensor_tensor(out=y[:, :], in0=y[:, :], scalar=0.5,
                                                 in1=psum[4 * (p % 2) + n][:, :], op0=ALU.mult,
                                                 op1=ALU.mult).then_inc(ffn_step, 1)
                        dve.wait_ge(aT_hi_ready, f + 1)
                        dve.tensor_tensor(aT_lo[:, f, :], y[:, :], aT_hi[:, f, :].bitcast(F32),
                                          ALU.subtract).then_inc(aT_lo_ready, 1)

            for n in range(2 * D_GRAN - RING):
                split_lo(G_DOWN + n + AHEAD)
                if n == D_GRAN - 1:
                    dve.wait_ge(used, G_DOWN + D_GRAN)
                    dve.wait_ge(norm[1]["xn_ready"], ROWS)
                    for r in range(ROWS):
                        dve.tensor_tensor(x1[:, r, 0:HALF], x1[:, r, 0:HALF], psum[4 + r][:, :], ALU.add).then_inc(x2_ready, 1)
            for n in range(AHEAD):
                split_lo(N_GRAN - AHEAD + n)
            dve.wait_ge(gain3_in, 16)
            for r in range(ROWS - 1):
                dve.wait_ge(row_down, r + 1)
                dve.tensor_tensor(x1[:, r, HALF:D], x1[:, r, HALF:D], psum[r][:, :], ALU.add).then_inc(x2_ready, 1)
                mean_of_squares(2, r, ROWS + r + 1)
                normalise(2, x1, r, gain_a, x1[:, r, :])
            r = ROWS - 1
            dve.tensor_tensor(work[0][:, :], x1[:, r, 0:HALF], gain_a[:, 0:HALF], ALU.mult).then_inc(gained, 1)
            dve.wait_ge(used, N_GRAN)
            dve.tensor_tensor(x1[:, r, HALF:D], x1[:, r, HALF:D], psum[r][:, :], ALU.add).then_inc(x2_ready, 1)
            dve.wait_ge(x2_ready, 2 * ROWS)
            dve.tensor_tensor(work[1][:, :], x1[:, r, HALF:D], gain_a[:, HALF:D], ALU.mult).then_inc(gained, 1)
            mean_of_squares(2, r, ROWS + r + 1)
            dve.wait_ge(norm[2]["rstd_ready"], r + 1)
            dve.wait_ge(gained, 1)
            dve.tensor_scalar(x1[:, r, 0:HALF], work[0][:, :], rstd[:, r:r + 1], None, ALU.mult).then_inc(norm[2]["xn_ready"], 1)

        @block.tensor
        def _(pe):
            freed = {}

            def take(bank, by):
                if bank in freed:
                    pe.wait_ge(*freed[bank])
                freed[bank] = by

            def three(o, a_hi, a_lo, b_hi, b_lo, first, last):
                pe.matmul(o, a_hi, b_hi, start=first, stop=False)
                pe.matmul(o, a_hi, b_lo, start=False, stop=False)
                return pe.matmul(o, a_lo, b_hi, start=False, stop=last)

            def transpose_rows(i, tiles):
                def one(r):
                    pe.wait_ge(norm[i]["xn_ready"], r + 1)
                    for half in range(2):
                        bank = norm_bank(i, r, half)
                        take(bank, (norm[i]["hT_lo_ready"], 2 * r + half + 1))
                        for k in range(4):
                            c = (4 * half + k) * P
                            last = pe.transpose(psum[bank][:, k * P:(k + 1) * P], tiles[r % 2][:, c:c + P], ident[:, :])
                        last.then_inc(norm[i]["xn_T"], 1)
                return one

            def columns(g, bank, by, src_hi, src_lo, k0=0, n=KD, last_of_granule=True, times=slice(0, SEQ)):
                if times.start == 0:
                    take(bank, by)
                wh, wl = ring(w_hi, g), ring(w_lo, g)
                if g == G_GATE:
                    for k in range(n):
                        pe.matmul(psum[bank][:, times], wh[:, k, :], src_hi[:, k, times], start=k == 0, stop=False)
                        last = pe.matmul(psum[bank][:, times], wh[:, k, :], src_lo[:, k, times], start=False,
                                         stop=k == n - 1)
                    if last_of_granule:
                        last.then_inc(used, 1)
                    return
                for k in range(n):
                    last = three(psum[bank][:, times], wh[:, k0 + k, :], wl[:, k0 + k, :], src_hi[:, k, times],
                                 src_lo[:, k, times], k == 0, k == n - 1)
                if last_of_granule:
                    last.then_inc(used, 1)

            def z_columns(g, bank, by):
                pe.wait_ge(lo_split, g + 1)
                columns(g, bank, by, hT_hi, hT_lo)

            def z_first_rows(i, g, bank, by):
                pe.wait_ge(lo_split, g + 1)
                pe.wait_ge(norm[i]["hT_lo_ready"], 4)
                columns(g, bank, by, hT_hi, hT_lo, last_of_granule=False, times=slice(0, SEQ // 2))

            def z_last_rows(i, g, bank):
                pe.wait_ge(norm[i]["hT_lo_ready"], 2 * ROWS)
                columns(g, bank, None, hT_hi, hT_lo, times=slice(SEQ // 2, SEQ))

            def row_product(g, bank, r, src_hi, src_lo, k0, first, last):
                wh, wl = ring(w_hi, g), ring(w_lo, g)
                rows = slice(r * P, (r + 1) * P)
                for k in range(2):
                    ins = three(psum[bank][:, :], src_hi[:, k0 + k, rows], src_lo[:, k0 + k, rows], wh[:, k, :], wl[:, k, :],
                                first and k == 0, last and k == 1)
                return ins

            pe.wait_ge(consts, 1)
            for _ in range(WARM_UP):
                pe.matmul(psum[7][:, 0:P], ones[:, :], ones[:, :], start=True, stop=True)
            pe.wait_ge(consts, N_CONSTS)
            one = transpose_rows(0, xn)
            one(0)
            one(1)
            first = [(0, qk_bank(0), (z_padded, 1)), (1, qk_bank(1), (z_padded, 2)), (G_GATE, 1, (gate_rows_ready, 2))]
            for n, (g, bank, by) in enumerate(first):
                z_first_rows(0, g, bank, by)
                if n < 2:
                    one(2 + n)
            pe.wait_ge(vec_in, 16 * 7)
            take(0, (vec_ready, 2))
            pe.transpose(psum[0][:, 0:N_VEC], vec_raw[:, :], ident[0:N_VEC, 0:N_VEC]).then_inc(vec_T, 1)
            for g, bank, _ in first:
                z_last_rows(0, g, bank)

            for g, b in qk_block.items():
                if g < G_GATE:
                    continue
                z_columns(g, qk_bank(b), (z_padded, b + 1))
                b -= 2
                if b == 1:
                    pe.wait_ge(gate_rows_ready, 2)
                    take(1, (frame_step, FRAME_STEPS))
                    for j in range(ROWS):
                        last = pe.transpose(psum[1][:, 16 * j:16 * j + 16], gate_rows[0:16, j * P:(j + 1) * P], ident[0:16, 0:16])
                    last.then_inc(gates_T, 1)
                if b == 4:
                    pe.wait_ge(log_f_ready, 1)
                    lf = log_f[:, :, :].rearrange("p j l -> p (j l)")
                    pe.matmul(psum[1][:, 64:64 + ROWS * LANES], upper[:, :], lf, start=True, stop=True)
                    pe.matmul(psum[1][:, 128:128 + ROWS * LANES], ones[:, :], lf, start=True, stop=True).then_inc(cum_done, 1)

            def keys_as_rows():
                pe.wait_ge(frame_step, FRAME_STEPS)
                for n, (a, z) in enumerate(ROW_CHUNKS):
                    take(5 + n, (rows_lo_ready, n + 1))
                    for m in range(a, z):
                        q = next(i for i in range(ROWS) if pair(i, i) >= m)
                        last = pe.transpose(psum[5 + n][0:LANES, (m - a) * P:(m - a + 1) * P],
                                            frame[:, ROWS * q + m - pair(q, 0), :], ident[:, :])
                    last.then_inc(frame_T, 1)

            for n, g0 in enumerate((G_MV, G_FV)):
                for d in range(4):
                    pe.wait_ge(lo_split, g0 + d + 1)
                    for r in range(ROWS):
                        if d == 0:
                            take(V_BANKS[n][r], (v_ready, ROWS * n + r + 1))
                        last = row_product(g0 + d, V_BANKS[n][r], r, hT_hi, hT_lo, 2 * d, d == 0, d == 3)
                    last.then_inc(used, 1)
                    if n == 0 and d == 1:
                        keys_as_rows()

            def spread_row(bank, lane, q, first, last):
                n = (q + 1) * P
                cols = slice(pair(q, 0) * P, pair(q, 0) * P + n)
                both = pick[:, lane:lane + 1].to_broadcast([P, P])
                pe.matmul(psum[bank][:, 0:n], both, rows_both[:, cols], start=first, stop=False)
                return pe.matmul(psum[bank][:, q * P:n], ident_b[:, :], mask_b[:, :], start=False, stop=last)

            for b in range(8):
                z_columns(G_FQK + b, fqk_bank(b), (fq_ready, b + 1) if b < KB else (fk_ready, b - KB + 1))
                if b == 0:
                    pe.wait_ge(rows_lo_ready, 3)
                for u in spread_units(b):
                    q, h = u // H_M, u % H_M
                    take(spread_bank(u), (g_max, u + 1))
                    spread_row(spread_bank(u), h, q, True, True).then_inc(g_spread, 1)

            def mlstm_scores(h):
                if h == 0:
                    pe.wait_ge(m_step, 2)
                    pe.wait_ge(qk_ready, 8)
                take(2, (decay_exp, 10 * (h + 1)))
                for q in range(ROWS):
                    last = pe.matmul(psum[2][:, q * P:(q + 1) * P],
                                     m_stab[:, q, h:h + 1].to_broadcast([P, P]), ident[:, :], start=True, stop=True)
                last.then_inc(m_spread, 1)
                for j in range(ROWS):
                    o = (0, 0, 0, 256)[j]
                    if j < 3:
                        take(4 + j, (weighted, 4 * h + (j + 1 if j < 2 else 4)))
                    pe.matmul(psum[4 + min(j, 2)][:, o:o + SEQ - j * P], k_m[:, h, j * P:(j + 1) * P],
                              q_m[:, h, j * P:SEQ], start=True, stop=True).then_inc(s_m, 1)

            def mlstm_values(h):
                if h == 0:
                    pe.wait_ge(v_ready, ROWS)
                    pe.wait_ge(v_ones, 1)
                for q in range(ROWS):
                    if q % 2 == 0:
                        take(q // 2, (h_m, 2 * h + q // 2 + 1))
                    pe.wait_ge(weighted, 4 * h + q + 1)
                    for j in range(q + 1):
                        o = decay_at(j) + (q - j) * P
                        last = pe.matmul(psum[q // 2][:, (q % 2) * (DH_M + 1):(q % 2 + 1) * (DH_M + 1)],
                                         decay[h % 2][:, o:o + P], v_m[:, j, h, :], start=(j == 0), stop=(j == q))
                    if q % 2:
                        last.then_inc(num_m, 1)

            def mlstm_transpose(h):
                pe.wait_ge(y_m, h + 1)
                take(head_T_bank(h), (y_m32, h + 1))
                for q in range(ROWS):
                    last = pe.transpose(psum[head_T_bank(h)][:, q * P:(q + 1) * P], work[3][:, q * P:(q + 1) * P], ident[:, :])
                last.then_inc(y_mT, 1)

            def fox_logits(u):
                hp, q, h2 = fox_unit(u)
                if u == 0:
                    pe.wait_ge(fq_ready, KB)
                    pe.wait_ge(fk_ready, KB)
                bank, n = 4 + u % 3, (q + 1) * P
                head = slice(h2 * DH_F, (h2 + 1) * DH_F)
                take(bank, (fox_exp, u + 1))
                pe.matmul(psum[bank][:, 0:n], q_f[head, hp, q * P:(q + 1) * P], k_f[head, hp, 0:n], start=True, stop=False)
                spread_row(bank, H_M + 2 * hp + h2, q, False, True).then_inc(logits, 1)

            def fox_transpose(u):
                _, q, _ = fox_unit(u)
                pe.wait_ge(fox_norm, 2 * u + 2)
                take(2 + u % 2, (fox_PT[u % 2], u // 2 + 1))
                for j in range(q + 1):
                    last = pe.transpose(psum[2 + u % 2][:, j * P:(j + 1) * P], probs[u % 3][:, j * P:(j + 1) * P], ident[:, :])
                last.then_inc(fox_T, 1)

            def fox_values(u):
                hp, q, h2 = fox_unit(u)
                if u == 0:
                    pe.wait_ge(v_ready, 2 * ROWS)
                pe.wait_ge(fox_PT[u % 2], u // 2 + 1)
                if u % 8 == 0:
                    take(hp % 2, (yfT_lo_ready, hp + 1))
                c = (2 * hp + h2) * DH_F
                for j in range(q + 1):
                    last = pe.matmul(psum[hp % 2][h2 * DH_F:(h2 + 1) * DH_F, q * P:(q + 1) * P],
                                     v_f[:, j, c:c + DH_F], work[u % 2][:, j * P:(j + 1) * P],
                                     start=(j == 0), stop=(j == q))
                last.then_inc(fox_pv, 1)

            def mo_columns(b, k0, k1):
                g = G_MO + b
                if k0 == 0:
                    pe.wait_ge(lo_split, g + 1)
                    take(3, (mo_tanh, b + 1))
                for k in range(k0, k1):
                    last = three(psum[3][:, :], ring(w_hi, g)[:, k, :], ring(w_lo, g)[:, k, :], hT_hi[:, k, :],
                                 hT_lo[:, k, :], k == 0, k == KD - 1)
                if k1 == KD:
                    last.then_inc(used, 1)

            def gate_piece(i):
                n, k = i // KD, i % KD
                g = G_BR + n
                if k == 0:
                    pe.wait_ge(lo_split, g + 1)
                    take(7, (gate_tanh, n + 1))
                last = three(psum[7][:, :], ring(w_hi, g)[:, k, :], ring(w_lo, g)[:, k, :], hT_hi[:, k, :], hT_lo[:, k, :],
                             k == 0, k == KD - 1)
                if k == KD - 1:
                    last.then_inc(used, 1)

            for h in range(H_M):
                mlstm_scores(h)
                if h >= 2:
                    mlstm_transpose(h - 2)
                if h >= 1:
                    mlstm_values(h - 1)
                mo_columns(h, 0, KD if h < H_M - 1 else 4)
            mlstm_values(3)
            fox_logits(0)
            mo_columns(3, 4, 6)
            fox_logits(1)
            mo_columns(3, 6, KD)
            mlstm_transpose(2)

            for u in range(2, 35):
                if u < 32:
                    fox_logits(u)
                if u == 4:
                    mlstm_transpose(3)
                if u < 34:
                    fox_transpose(u - 2)
                first_piece = (u - FILL_FROM) % KD == 0
                if u >= FILL_FROM and not first_piece:
                    gate_piece(u - FILL_FROM)
                if u >= 3:
                    fox_values(u - 3)
                if u >= FILL_FROM and first_piece:
                    gate_piece(u - FILL_FROM)

            for i in range(35 - FILL_FROM, 4 * KD):
                gate_piece(i)

            for c in range(4):
                for n in range(4):
                    if c:
                        z_columns(G_BR + 6 * c + n, GATE_BANKS[n], (gate_tanh, 4 * c + n + 1))
                if c == 0:
                    pe.wait_ge(ymT_lo_ready, H_M)
                for j in range(2):
                    g, b = G_BR + 6 * c + 4 + j, 2 * c + j
                    pe.wait_ge(lo_split, g + 1)
                    columns(g, 2 * j, (mix_step, 3 * b + 1), ymT_hi, ymT_lo, 0, KB, False)
                    if b == 0:
                        pe.wait_ge(yfT_lo_ready, KB)
                    columns(g, 2 * j + 1, (mix_step, 3 * b + 2), yfT_hi, yfT_lo, KB, KB)

            for r in range(ROWS):
                take(4 + r, (x1_ready, r + 1))
            for d in range(4):
                pe.wait_ge(lo_split, G_OUT + d + 1)
                pe.wait_ge(mix_lo_ready, 2 * d + 2)
                for r in range(ROWS):
                    last = row_product(G_OUT + d, 4 + r, r, mixT_hi, mixT_lo, 2 * d, d == 0, d == 3)
                last.then_inc(used, 1)
            one = transpose_rows(1, xn2)
            for r in range(ROWS):
                take(r, (x1_ready, ROWS + r + 1))
                for d in range(4):
                    if r == 0:
                        pe.wait_ge(lo_split, G_OUT + 4 + d + 1)
                    last = row_product(G_OUT + 4 + d, r, r, mixT_hi, mixT_lo, 2 * d, d == 0, d == 3)
                    if r == ROWS - 1:
                        last.then_inc(used, 1)
                if r < ROWS - 1:
                    last.then_inc(row_out, 1)
                if r >= 1:
                    one(r - 1)

            def ffn_bank(n):
                p, i = n // 4, n % 4
                return 4 * (p % 2) + i, (ffn_step, 2 * (2 * p + i % 2) + 1 + i // 2)

            for n in range(N_FIRST):
                z_first_rows(1, G_FFN + n, *ffn_bank(n))
                if n == 1:
                    one(ROWS - 1)
            for n in range(N_FIRST):
                z_last_rows(1, G_FFN + n, ffn_bank(n)[0])
            for n in range(N_FIRST, G_DOWN - G_FFN):
                z_columns(G_FFN + n, *ffn_bank(n))

            for half in range(2):
                bank0 = 4 - 4 * half
                for r in range(ROWS):
                    take(bank0 + r, (x2_ready, ROWS * half + r + 1))
                n_shared = D_GRAN - half * RING
                for d in range(n_shared):
                    g = G_DOWN + half * D_GRAN + d
                    pe.wait_ge(lo_split, g + 1)
                    pe.wait_ge(aT_lo_ready, 2 * d + 2)
                    for r in range(ROWS):
                        last = row_product(g, bank0 + r, r, aT_hi, aT_lo, 2 * d, d == 0, d == D_GRAN - 1)
                    last.then_inc(used, 1)
            for r in range(ROWS):
                for d in range(D_GRAN - RING, D_GRAN):
                    g = G_DOWN + D_GRAN + d
                    if r == 0:
                        pe.wait_ge(lo_split, g + 1)
                    last = row_product(g, r, r, aT_hi, aT_lo, 2 * d, False, d == D_GRAN - 1)
                    if r == ROWS - 1:
                        last.then_inc(used, 1)
                if r < ROWS - 1:
                    last.then_inc(row_down, 1)


LO = 32
N_CONSTS = 17
FRAME_STEPS = 10
WARM_UP = 16
ROW_CHUNKS = ((0, 4), (4, 8), (8, 10))
N_FIRST = 3
FILL_FROM = 4
GATE_BANKS = (6, 4, 5, 7)
V_BANKS = ((2, 3, 0, 4), (5, 6, 7, 1))


def norm_bank(i, r, half):
    return 2 * r + half if i == 0 else 4 + (2 * r + half) % 4


def qk_bank(b):
    return (2, 3, 0, 4)[b % 4]


def fqk_bank(b):
    return b % 4


def spread_bank(u):
    return 4 + u % 4


def head_T_bank(h):
    return 7 if h < 3 else 1


def spread_units(b):
    return range(3 * b, min(3 * b + 3, ROWS * H_M))


def fox_unit(u):
    q, head = ((0, 0), (1, 0), (2, 0), (3, 0), (3, 1), (2, 1), (1, 1), (0, 1))[u % 8]
    return u // 8, q, head


_INS = ["x", "norm1_g", "w_in", "b_in", "conv_w", "conv_b", "mlstm_norm_g", "w_br_mlstm", "w_br_fox",
        "w_out", "norm2_g", "w_gate", "w_up", "w_down", "norm_f_g"]


def kernel(**inputs):
    import concourse.bacc as bacc
    from concourse.bass_utils import run_bass_kernel_spmd

    nc = bacc.Bacc("TRN2", target_bir_lowering=False, num_devices=1)
    arrays, args = {}, []
    for name in _INS:
        a = np.ascontiguousarray(inputs[name])
        arrays[f"in_{name}"] = a
        args.append(nc.dram_tensor(f"in_{name}", a.shape, mybir.dt.from_np(a.dtype), kind="ExternalInput").ap())
    out = nc.dram_tensor("out_block", (1, SEQ, D), F32, kind="ExternalOutput").ap()
    block_kernel(nc, *args, out)
    r = run_bass_kernel_spmd(nc, [arrays], core_ids=[0])
    return r.results[0]["out_block"]
```
